# Optimizing a Trainium2 kernel written in Bass

```python
import math
import jax, jax.numpy as jnp
from jax import lax
import numpy as np

D_MODEL = 2048
BATCH = 1
SEQ = 256
DEPTH = 1

CONV_WIDTH = D_MODEL // 2
CONV_KERNEL = 31
SSM_WIDTH = D_MODEL // 2
SSM_GROUP = 16
SSM_GROUPS = SSM_WIDTH // SSM_GROUP
SSM_STATE = 64
N_BRANCHES = 2
IN_WIDTH = 2 * CONV_WIDTH + SSM_WIDTH + N_BRANCHES * D_MODEL
PEER_HEADS = 8
PEER_KEYS = 128
PEER_EXPERTS = PEER_KEYS * PEER_KEYS
PEER_QDIM = 256
PEER_HALF = PEER_QDIM // 2
PEER_TOPK = 16
PEER_TOKEN_BLOCK = 128
RMS_EPS = 1e-6
LN_EPS = 1e-5
DT_MIN = 1e-3
DT_MAX = 1e-1


def rmsnorm(x, g):
    xf = x.astype(jnp.float32)
    y = xf * lax.rsqrt(jnp.mean(xf * xf, axis=-1, keepdims=True) + RMS_EPS)
    return (y * g.astype(jnp.float32)).astype(x.dtype)

def layernorm(x, g, b):
    xf = x.astype(jnp.float32)
    mu = jnp.mean(xf, axis=-1, keepdims=True)
    var = jnp.mean(jnp.square(xf - mu), axis=-1, keepdims=True)
    y = (xf - mu) * lax.rsqrt(var + LN_EPS)
    return (y * g.astype(jnp.float32) + b.astype(jnp.float32)).astype(x.dtype)

def conformer_conv(a, w_dw, b_dw, ln_g, ln_b, w_pw):
    glu = a[..., :CONV_WIDTH] * jax.nn.sigmoid(a[..., CONV_WIDTH:])
    padded = jnp.pad(glu, ((0, 0), (CONV_KERNEL - 1, 0), (0, 0)))
    y = lax.conv_general_dilated(
        padded, w_dw.astype(glu.dtype)[:, None, :], window_strides=(1,), padding='VALID',
        dimension_numbers=('NWC', 'WIO', 'NWC'), feature_group_count=CONV_WIDTH)
    y = y + b_dw.astype(glu.dtype)
    y = jax.nn.silu(layernorm(y, ln_g, ln_b))
    return y @ w_pw

def s5_ssm(u, a_re, a_im, log_dt, b_re, b_im, c_re, c_im, d_skip, w_val, w_gate):
    bsz, seq, _ = u.shape
    uf = u.astype(jnp.float32)
    ug = uf.reshape(bsz, seq, SSM_GROUPS, SSM_GROUP)
    lam = lax.complex(a_re.astype(jnp.float32), a_im.astype(jnp.float32))
    dt = jnp.exp(log_dt.astype(jnp.float32))[:, None]
    lam_bar = jnp.exp(lam * dt)
    b_mat = lax.complex(b_re.astype(jnp.float32), b_im.astype(jnp.float32))
    b_bar = ((lam_bar - 1.0) / lam)[..., None] * b_mat
    bu = jnp.einsum('gph,bsgh->bsgp', b_bar, ug.astype(jnp.complex64))
    a_seq = jnp.broadcast_to(lam_bar[None, None], (1, seq, SSM_GROUPS, SSM_STATE))

    def combine(left, right):
        a_l, b_l = left
        a_r, b_r = right
        return a_r * a_l, a_r * b_l + b_r

    _, states = lax.associative_scan(combine, (a_seq, bu), axis=1)
    y = (jnp.einsum('ghp,bsgp->bsgh', c_re.astype(jnp.float32), jnp.real(states))
         - jnp.einsum('ghp,bsgp->bsgh', c_im.astype(jnp.float32), jnp.imag(states)))
    y = y.reshape(bsz, seq, SSM_WIDTH) + d_skip.astype(jnp.float32) * uf
    z = jax.nn.gelu(y).astype(u.dtype)
    return (z @ w_val) * jax.nn.sigmoid(z @ w_gate)

def peer(h, w_q, sub_keys, u_tab, v_tab):
    bsz, seq, d = h.shape
    tokens = h.reshape(bsz * seq // PEER_TOKEN_BLOCK, PEER_TOKEN_BLOCK, d)

    def block(xb):
        q = (xb @ w_q).reshape(PEER_TOKEN_BLOCK, PEER_HEADS, 2, PEER_HALF)
        s = jnp.einsum('thcd,hcnd->thcn', q, sub_keys).astype(jnp.float32)
        s_top, i_top = lax.top_k(s, PEER_TOPK)
        cand = s_top[:, :, 0, :, None] + s_top[:, :, 1, None, :]
        cand_idx = i_top[:, :, 0, :, None] * PEER_KEYS + i_top[:, :, 1, None, :]
        cand = cand.reshape(PEER_TOKEN_BLOCK, PEER_HEADS, PEER_TOPK * PEER_TOPK)
        cand_idx = cand_idx.reshape(PEER_TOKEN_BLOCK, PEER_HEADS, PEER_TOPK * PEER_TOPK)
        best, pos = lax.top_k(cand, PEER_TOPK)
        expert = jnp.take_along_axis(cand_idx, pos, axis=-1)
        gates = jax.nn.softmax(best, axis=-1).astype(xb.dtype)
        u_sel = u_tab[expert]
        v_sel = v_tab[expert]
        act = jax.nn.gelu(jnp.einsum('td,thkd->thk', xb, u_sel))
        return jnp.einsum('thk,thkd->td', gates * act, v_sel)

    out = lax.map(block, tokens)
    return out.reshape(bsz, seq, d)

def first_inputs(seed: int = 0) -> dict:
    key = jax.random.key(seed)
    ks = jax.random.split(key, 32)
    f32 = jnp.float32
    L, D = DEPTH, D_MODEL

    def nrm(k, shape, scale):
        return jax.random.normal(k, shape, f32) * scale

    n_idx = jnp.arange(SSM_STATE, dtype=f32)
    return {
        "x": nrm(ks[0], (BATCH, SEQ, D), 1.0),
        "norm_mix": 1.0 + nrm(ks[1], (L, D), 0.02),
        "w_in": nrm(ks[2], (L, D, IN_WIDTH), D ** -0.5),
        "b_gate": nrm(ks[3], (L, N_BRANCHES * D), 0.01),
        "conv_w_dw": nrm(ks[4], (L, CONV_KERNEL, CONV_WIDTH), CONV_KERNEL ** -0.5),
        "conv_b_dw": nrm(ks[5], (L, CONV_WIDTH), 0.01),
        "conv_ln_g": 1.0 + nrm(ks[6], (L, CONV_WIDTH), 0.02),
        "conv_ln_b": nrm(ks[7], (L, CONV_WIDTH), 0.01),
        "conv_w_out": nrm(ks[8], (L, CONV_WIDTH, D), CONV_WIDTH ** -0.5),
        "ssm_a_re": -0.5 + nrm(ks[9], (L, SSM_GROUPS, SSM_STATE), 0.01),
        "ssm_a_im": math.pi * n_idx + nrm(ks[10], (L, SSM_GROUPS, SSM_STATE), 0.01),
        "ssm_log_dt": jax.random.uniform(ks[11], (L, SSM_GROUPS), f32, math.log(DT_MIN), math.log(DT_MAX)),
        "ssm_b_re": nrm(ks[12], (L, SSM_GROUPS, SSM_STATE, SSM_GROUP), (2.0 * SSM_GROUP) ** -0.5),
        "ssm_b_im": nrm(ks[13], (L, SSM_GROUPS, SSM_STATE, SSM_GROUP), (2.0 * SSM_GROUP) ** -0.5),
        "ssm_c_re": nrm(ks[14], (L, SSM_GROUPS, SSM_GROUP, SSM_STATE), (2.0 * SSM_STATE) ** -0.5),
        "ssm_c_im": nrm(ks[15], (L, SSM_GROUPS, SSM_GROUP, SSM_STATE), (2.0 * SSM_STATE) ** -0.5),
        "ssm_d": nrm(ks[16], (L, SSM_WIDTH), 1.0),
        "ssm_w_val": nrm(ks[17], (L, SSM_WIDTH, D), SSM_WIDTH ** -0.5),
        "ssm_w_gate": nrm(ks[18], (L, SSM_WIDTH, D), SSM_WIDTH ** -0.5),
        "w_out": nrm(ks[19], (L, D, D), D ** -0.5),
        "norm_ffn": 1.0 + nrm(ks[20], (L, D), 0.02),
        "peer_w_q": nrm(ks[21], (L, D, PEER_HEADS * PEER_QDIM), D ** -0.5),
        "peer_sub_keys": nrm(ks[22], (L, PEER_HEADS, 2, PEER_KEYS, PEER_HALF), PEER_HALF ** -0.5),
        "peer_u": nrm(ks[23], (L, PEER_EXPERTS, D), D ** -0.5),
        "peer_v": nrm(ks[24], (L, PEER_EXPERTS, D), PEER_HEADS ** -0.5),
        "norm_final": 1.0 + nrm(ks[25], (D,), 0.02),
    }

def first_block(x, norm_mix, w_in, b_gate, conv_w_dw, conv_b_dw, conv_ln_g, conv_ln_b, conv_w_out,
              ssm_a_re, ssm_a_im, ssm_log_dt, ssm_b_re, ssm_b_im, ssm_c_re, ssm_c_im, ssm_d,
              ssm_w_val, ssm_w_gate, w_out, norm_ffn, peer_w_q, peer_sub_keys, peer_u, peer_v,
              norm_final):
    bsz, seq, _ = x.shape
    for l in range(DEPTH):
        h = rmsnorm(x, norm_mix[l])
        proj = h @ w_in[l]
        conv_in = proj[..., :2 * CONV_WIDTH]
        ssm_in = proj[..., 2 * CONV_WIDTH:2 * CONV_WIDTH + SSM_WIDTH]
        gate_in = proj[..., 2 * CONV_WIDTH + SSM_WIDTH:]
        branch_conv = conformer_conv(conv_in, conv_w_dw[l], conv_b_dw[l], conv_ln_g[l], conv_ln_b[l], conv_w_out[l])
        branch_ssm = s5_ssm(ssm_in, ssm_a_re[l], ssm_a_im[l], ssm_log_dt[l], ssm_b_re[l], ssm_b_im[l],
                            ssm_c_re[l], ssm_c_im[l], ssm_d[l], ssm_w_val[l], ssm_w_gate[l])
        gates = jax.nn.sigmoid(gate_in + b_gate[l]).reshape(bsz, seq, N_BRANCHES, D_MODEL)
        merged = gates[:, :, 0, :] * branch_conv + gates[:, :, 1, :] * branch_ssm
        x = x + merged @ w_out[l]
        h = rmsnorm(x, norm_ffn[l])
        x = x + peer(h, peer_w_q[l], peer_sub_keys[l], peer_u[l], peer_v[l])
    return rmsnorm(x, norm_final)


DEPTH_2 = 2

CHUNK = 64
N_MIXERS = 2
EPS = 1e-6

A_HEADS = 16
A_HEAD_DIM = 128
A_INNER = A_HEADS * A_HEAD_DIM
CONV_K = 4

B_HEADS = 16
B_HEAD_DIM = 128
B_INNER = B_HEADS * B_HEAD_DIM
LEFT_CHUNKS = 8
BAND = (LEFT_CHUNKS + 1) * CHUNK
REL_CLIP = 256


def rms_norm(x, w):
    xf = x.astype(jnp.float32)
    y = xf * lax.rsqrt(jnp.mean(xf * xf, axis=-1, keepdims=True) + EPS)
    return (y * w.astype(jnp.float32)).astype(x.dtype)

def l2_norm(x):
    xf = x.astype(jnp.float32)
    return xf * lax.rsqrt(jnp.sum(xf * xf, axis=-1, keepdims=True) + EPS)

def causal_depthwise_conv(x, w):
    c = x.shape[-1]
    return lax.conv_general_dilated(
        x, w[:, None, :].astype(x.dtype), window_strides=(1,),
        padding=[(CONV_K - 1, 0)], dimension_numbers=("NWC", "WIO", "NWC"),
        feature_group_count=c)

def gated_deltanet(h, w_in, conv_w, a_log, dt_bias, out_norm_w, w_out):
    bsz, t, _ = h.shape
    nc = t // CHUNK
    proj = h @ w_in.astype(h.dtype)
    qkv = proj[..., :3 * A_INNER]
    z = proj[..., 3 * A_INNER:4 * A_INNER]
    a_in = proj[..., 4 * A_INNER:4 * A_INNER + A_HEADS]
    b_in = proj[..., 4 * A_INNER + A_HEADS:]
    qkv = jax.nn.silu(causal_depthwise_conv(qkv, conv_w))
    q = qkv[..., :A_INNER].reshape(bsz, t, A_HEADS, A_HEAD_DIM)
    k = qkv[..., A_INNER:2 * A_INNER].reshape(bsz, t, A_HEADS, A_HEAD_DIM)
    v = qkv[..., 2 * A_INNER:].reshape(bsz, t, A_HEADS, A_HEAD_DIM).astype(jnp.float32)
    q = l2_norm(q) * (A_HEAD_DIM ** -0.5)
    k = l2_norm(k)
    beta = jax.nn.sigmoid(b_in.astype(jnp.float32))
    g = -jnp.exp(a_log.astype(jnp.float32)) * jax.nn.softplus(
        a_in.astype(jnp.float32) + dt_bias.astype(jnp.float32))

    def to_chunks(u):
        u = u.reshape((bsz, nc, CHUNK) + u.shape[2:])
        return jnp.moveaxis(u, 3, 1)

    q, k, v = to_chunks(q), to_chunks(k), to_chunks(v)
    beta, g = to_chunks(beta), to_chunks(g)
    gc = jnp.cumsum(g, axis=-1)
    tri_incl = jnp.tril(jnp.ones((CHUNK, CHUNK), dtype=bool))
    tri_strict = jnp.tril(jnp.ones((CHUNK, CHUNK), dtype=bool), k=-1)
    diff = gc[..., :, None] - gc[..., None, :]
    decay = jnp.exp(jnp.where(tri_incl, diff, -jnp.inf))

    k_beta = k * beta[..., None]
    v_beta = v * beta[..., None]
    lower = jnp.where(tri_strict, jnp.einsum('bhncd,bhnsd->bhncs', k_beta, k) * decay, 0.0)
    eye = jnp.eye(CHUNK, dtype=jnp.float32)
    rhs = jnp.concatenate([v_beta, k_beta * jnp.exp(gc)[..., None]], axis=-1)
    sol = lax.linalg.triangular_solve(eye + lower, rhs, left_side=True, lower=True,
                                      unit_diagonal=True)
    u = sol[..., :A_HEAD_DIM]
    w = sol[..., A_HEAD_DIM:]
    qk = jnp.einsum('bhncd,bhnsd->bhncs', q, k) * decay
    q_dec = q * jnp.exp(gc)[..., None]
    k_dec = k * jnp.exp(gc[..., -1:] - gc)[..., None]
    g_last = jnp.exp(gc[..., -1])

    def step(state, inp):
        qk_n, q_dec_n, k_dec_n, u_n, w_n, gl_n = inp
        v_new = u_n - jnp.einsum('bhcd,bhdv->bhcv', w_n, state)
        o_n = (jnp.einsum('bhcd,bhdv->bhcv', q_dec_n, state)
               + jnp.einsum('bhcs,bhsv->bhcv', qk_n, v_new))
        state = state * gl_n[..., None, None] + jnp.einsum('bhcd,bhcv->bhdv', k_dec_n, v_new)
        return state, o_n

    xs = tuple(jnp.moveaxis(a, 2, 0) for a in (qk, q_dec, k_dec, u, w, g_last))
    s0 = jnp.zeros((bsz, A_HEADS, A_HEAD_DIM, A_HEAD_DIM), jnp.float32)
    _, o = lax.scan(step, s0, xs)
    o = jnp.transpose(o, (1, 0, 3, 2, 4)).reshape(bsz, t, A_HEADS, A_HEAD_DIM)
    zg = jax.nn.silu(z.astype(jnp.float32)).reshape(bsz, t, A_HEADS, A_HEAD_DIM)
    o = rms_norm(o, out_norm_w) * zg
    return o.reshape(bsz, t, A_INNER).astype(h.dtype) @ w_out.astype(h.dtype)

def chunk_band_attention(h, w_in, q_norm_w, k_norm_w, rel_bias, w_out):
    bsz, t, _ = h.shape
    nc = t // CHUNK
    pad = LEFT_CHUNKS * CHUNK
    proj = h @ w_in.astype(h.dtype)
    q = rms_norm(proj[..., :B_INNER].reshape(bsz, t, B_HEADS, B_HEAD_DIM), q_norm_w)
    k = rms_norm(proj[..., B_INNER:2 * B_INNER].reshape(bsz, t, B_HEADS, B_HEAD_DIM), k_norm_w)
    v = proj[..., 2 * B_INNER:3 * B_INNER].reshape(bsz, t, B_HEADS, B_HEAD_DIM)
    z = proj[..., 3 * B_INNER:]
    k_pad = jnp.pad(k, ((0, 0), (pad, 0), (0, 0), (0, 0)))
    v_pad = jnp.pad(v, ((0, 0), (pad, 0), (0, 0), (0, 0)))
    q_chunks = jnp.moveaxis(q.reshape(bsz, nc, CHUNK, B_HEADS, B_HEAD_DIM), 1, 0)

    r = jnp.arange(CHUNK)
    m = jnp.arange(BAND)
    rel = (pad + r[:, None]) - m[None, :]
    idx = jnp.clip(rel, -REL_CLIP, REL_CLIP) + REL_CLIP
    bias = rel_bias.astype(jnp.float32)[:, idx]
    scale = B_HEAD_DIM ** -0.5

    def one_chunk(args):
        n, q_n = args
        start = n * CHUNK
        k_n = lax.dynamic_slice_in_dim(k_pad, start, BAND, axis=1)
        v_n = lax.dynamic_slice_in_dim(v_pad, start, BAND, axis=1)
        s = jnp.einsum('bchd,bmhd->bhcm', q_n, k_n).astype(jnp.float32) * scale + bias
        valid = (start - pad + m) >= 0
        s = jnp.where(valid[None, None, None, :], s, -jnp.inf)
        p = jax.nn.softmax(s, axis=-1).astype(v_n.dtype)
        return jnp.einsum('bhcm,bmhd->bchd', p, v_n)

    o = lax.map(one_chunk, (jnp.arange(nc, dtype=jnp.int32), q_chunks))
    o = jnp.moveaxis(o, 0, 1).reshape(bsz, t, B_INNER)
    o = (o.astype(jnp.float32) * jax.nn.silu(z.astype(jnp.float32))).astype(h.dtype)
    return o @ w_out.astype(h.dtype)

def second_inputs(seed: int = 0) -> dict:
    key = jax.random.key(seed)
    ks = jax.random.split(key, 16)
    n_a = (DEPTH_2 + 1) // N_MIXERS
    n_b = DEPTH_2 // N_MIXERS
    f32 = jnp.float32
    x = jax.random.normal(ks[0], (BATCH, SEQ, D_MODEL), f32)
    norm_w = 1.0 + 0.02 * jax.random.normal(ks[1], (DEPTH_2, D_MODEL), f32)
    a_w_in = jax.random.normal(ks[2], (n_a, D_MODEL, 4 * A_INNER + 2 * A_HEADS), f32) * D_MODEL ** -0.5
    a_conv_w = jax.random.normal(ks[3], (n_a, CONV_K, 3 * A_INNER), f32) * CONV_K ** -0.5
    a_a_log = jnp.log(jax.random.uniform(ks[4], (n_a, A_HEADS), f32, 1.0, 16.0))
    dt = jnp.exp(jax.random.uniform(ks[5], (n_a, A_HEADS), f32, math.log(1e-3), math.log(1e-1)))
    a_dt_bias = dt + jnp.log(-jnp.expm1(-dt))
    a_out_norm_w = 1.0 + 0.02 * jax.random.normal(ks[6], (n_a, A_HEAD_DIM), f32)
    a_w_out = jax.random.normal(ks[7], (n_a, A_INNER, D_MODEL), f32) * A_INNER ** -0.5
    b_w_in = jax.random.normal(ks[8], (n_b, D_MODEL, 4 * B_INNER), f32) * D_MODEL ** -0.5
    b_q_norm_w = 1.0 + 0.02 * jax.random.normal(ks[9], (n_b, B_HEAD_DIM), f32)
    b_k_norm_w = 1.0 + 0.02 * jax.random.normal(ks[10], (n_b, B_HEAD_DIM), f32)
    b_rel_bias = 0.5 * jax.random.normal(ks[11], (n_b, B_HEADS, 2 * REL_CLIP + 1), f32)
    b_w_out = jax.random.normal(ks[12], (n_b, B_INNER, D_MODEL), f32) * B_INNER ** -0.5
    return {"x": x, "norm_w": norm_w, "a_w_in": a_w_in, "a_conv_w": a_conv_w,
            "a_a_log": a_a_log, "a_dt_bias": a_dt_bias, "a_out_norm_w": a_out_norm_w,
            "a_w_out": a_w_out, "b_w_in": b_w_in, "b_q_norm_w": b_q_norm_w,
            "b_k_norm_w": b_k_norm_w, "b_rel_bias": b_rel_bias, "b_w_out": b_w_out}

def second_block(x, norm_w, a_w_in, a_conv_w, a_a_log, a_dt_bias, a_out_norm_w, a_w_out,
              b_w_in, b_q_norm_w, b_k_norm_w, b_rel_bias, b_w_out):
    h = x
    for i in range(DEPTH_2):
        j = i // N_MIXERS
        hn = rms_norm(h, norm_w[i])
        if i % N_MIXERS == 0:
            y = gated_deltanet(hn, a_w_in[j], a_conv_w[j], a_a_log[j], a_dt_bias[j],
                               a_out_norm_w[j], a_w_out[j])
        else:
            y = chunk_band_attention(hn, b_w_in[j], b_q_norm_w[j], b_k_norm_w[j],
                                     b_rel_bias[j], b_w_out[j])
        h = h + y
    return h


def setup_inputs(seed=0):
    out = dict(first_inputs(seed))
    for name, value in second_inputs(seed + 1).items():
        if name != "x":
            out[name + "_2"] = value
    return out


def reference(
    x, norm_mix, w_in, b_gate, conv_w_dw, conv_b_dw, conv_ln_g, conv_ln_b, conv_w_out, ssm_a_re,
    ssm_a_im, ssm_log_dt, ssm_b_re, ssm_b_im, ssm_c_re, ssm_c_im, ssm_d, ssm_w_val, ssm_w_gate,
    w_out, norm_ffn, peer_w_q, peer_sub_keys, peer_u, peer_v, norm_final, norm_w_2, a_w_in_2,
    a_conv_w_2, a_a_log_2, a_dt_bias_2, a_out_norm_w_2, a_w_out_2, b_w_in_2, b_q_norm_w_2,
    b_k_norm_w_2, b_rel_bias_2, b_w_out_2,
):
    x = first_block(
        x, norm_mix, w_in, b_gate, conv_w_dw, conv_b_dw, conv_ln_g, conv_ln_b, conv_w_out,
        ssm_a_re, ssm_a_im, ssm_log_dt, ssm_b_re, ssm_b_im, ssm_c_re, ssm_c_im, ssm_d,
        ssm_w_val, ssm_w_gate, w_out, norm_ffn, peer_w_q, peer_sub_keys, peer_u, peer_v,
        norm_final,
    )
    return second_block(
        x, norm_w_2, a_w_in_2, a_conv_w_2, a_a_log_2, a_dt_bias_2, a_out_norm_w_2, a_w_out_2,
        b_w_in_2, b_q_norm_w_2, b_k_norm_w_2, b_rel_bias_2, b_w_out_2,
    )


_drawn_inputs = setup_inputs


def setup_inputs(seed=0):
    import zlib

    import numpy as np

    out = dict(_drawn_inputs(seed))
    spreads = {}
    factors = {'b_gate': 6.134,
     'conv_ln_b': 4.147,
     'ssm_a_re': 8.0,
     'ssm_b_re': 2.775,
     'ssm_b_im': 2.827,
     'ssm_c_re': 2.778,
     'ssm_c_im': 2.892,
     'norm_w_2': 3.129,
     'a_out_norm_w_2': 5.368,
     'b_q_norm_w_2': 8.0,
     'b_k_norm_w_2': 8.0}
    for name, (base, spread) in spreads.items():
        noise = np.random.default_rng([zlib.crc32(name.encode()), seed]).standard_normal(out[name].shape)
        drawn = base * np.exp(spread * noise) if base else spread * noise
        out[name] = __import__('jax').numpy.asarray(drawn.astype(out[name].dtype))
    for name, factor in factors.items():
        out[name] = (out[name] * factor).astype(out[name].dtype)
    return out
```

```python
from contextlib import ExitStack

import concourse.bass as bass
import concourse.mybir as mybir
import numpy as np
from concourse.alu_op_type import AluOpType as ALU

F32 = mybir.dt.float32
U32 = mybir.dt.uint32
ACT = mybir.ActivationFunctionType
AX_X = mybir.AxisListType.X

P = 128
KB = 256
NEG = -3.0e38
RMS_EPS, LN_EPS = 1e-6, 1e-5
CHUNK = 64
PI_SAFE = 3.1415925
ROUND = 12582912.0
TWO_PI = (6.28125, 0.0019350051879882812, 3.019916050561733e-07)


class Engine:

    def __init__(self, handle, semaphore):
        self.e, self.sem, self.n, self.seen = handle, semaphore, 0, {}

    def wait(self, *tokens):
        for sem, value in tokens:
            if self.seen.get(sem.name, 0) < value:
                self.e.wait_ge(sem, value)
                self.seen[sem.name] = value

    def mark(self, instruction):
        instruction.then_inc(self.sem, 1)
        self.n += 1
        return (self.sem, self.n)


class Vec(Engine):

    def tt(self, out, a, b, op, after=()):
        self.wait(*after)
        return self.mark(self.e.tensor_tensor(out, a, b, op))

    def ts(self, out, a, s1, op0, s2=None, op1=None, after=()):
        self.wait(*after)
        if op1 is None:
            return self.mark(self.e.tensor_scalar(out, a, s1, None, op0))
        return self.mark(self.e.tensor_scalar(out, a, s1, s2, op0, op1))

    def stt(self, out, a, s, b, op0, op1, after=()):
        self.wait(*after)
        return self.mark(self.e.scalar_tensor_tensor(out=out, in0=a, scalar=s, in1=b, op0=op0, op1=op1))

    def copy(self, out, a, after=()):
        self.wait(*after)
        return self.mark(self.e.tensor_copy(out, a))

    def memset(self, out, value, after=()):
        self.wait(*after)
        return self.mark(self.e.memset(out, value))

    def recip(self, out, a, after=()):
        self.wait(*after)
        return self.mark(self.e.reciprocal(out, a))


class Scalar(Engine):

    def act(self, out, a, func, after=(), **kw):
        self.wait(*after)
        return self.mark(self.e.activation(out, a, func, **kw))


class Tensor(Engine):

    def mm(self, out, lhsT, rhs, start=True, stop=True, after=()):
        self.wait(*after)
        return self.e.matmul(out, lhsT, rhs, start=start, stop=stop, skip_group_check=True)


class Loads:

    def __init__(self, semaphore):
        self.sem, self.n = semaphore, 0

    def start(self, queue, out, in_):
        queue.dma_start(out, in_).then_inc(self.sem, 16)
        self.n += 16
        return (self.sem, self.n)


def wide(ap, shape):
    return ap.broadcast_to(shape)


def param_columns():
    at, cols = 0, {}
    for name, n in (("norm_mix", 16), ("b_gate", 32), ("dw_w", 31 * 8), ("dw_b", 8), ("ln_g", 8), ("ln_b", 8),
                    ("a_re", 32), ("a_im", 32), ("log_dt", 32), ("ssm_d", 8), ("norm_ffn", 16),
                    ("norm_final", 16), ("norm2a", 16), ("norm2b", 16), ("qkv_w", 4 * 48), ("onorm", 1),
                    ("qnorm", 1), ("knorm", 1), ("a_log", 16), ("dt_bias", 16), ("eps_rms", 1), ("eps_ln", 1)):
        cols[name] = (at, n)
        at += n
    return cols, at


PCOL, NPARAM = param_columns()
CCOL = {"ident": (0, P), "ones": (P, P), "upto": (2 * P, P), "flip": (3 * P, P), "level": (4 * P, 7 * P),
        "band": (11 * P, 3 * P), "iota": (14 * P, 16)}
NCONST = 14 * P + 16


def build(nc, x, consts, params, w_in, conv_out, bT, cT, w_val, w_gate, w_out, w_q, keysT, u_tab, v_tab,
          a_in, a_out, b_in, rel_rev, b_out, out):
    D, T, NCH = 2048, 256, 16
    TAPS = 31
    NH = 16
    ctx = ExitStack()

    def sem(name):
        return ctx.enter_context(nc.semaphore(name))

    sb = ctx.enter_context(nc.sbuf_tensor("sb", [P, 206 * KB], F32))
    ps = ctx.enter_context(nc.psum_tensor("ps", [P, 8, 512], F32))

    pe = Tensor(nc.tensor, sem("pe_done"))
    dve = Vec(nc.vector, sem("dve_done"))
    pool = Vec(nc.gpsimd, sem("pool_done"))
    act = Scalar(nc.scalar, sem("act_done"))
    sp = Engine(nc.sync, None)
    small = Loads(sem("small_loads"))
    stores = Loads(sem("stores"))

    def at(kb, *shape):
        n = int(np.prod(shape))
        v = sb[:, int(kb * KB):int(kb * KB) + n]
        if len(shape) == 1:
            return v
        names = "abcd"[:len(shape)]
        sizes = {k: s for k, s in zip(names[1:], shape[1:])}
        return v.rearrange(f"p ({' '.join(names)}) -> p {' '.join(names)}", **sizes)

    def fence():
        return [(e.sem, e.n) for e in (pe, dve, pool, act) if e.n]

    cst = at(196, NCONST)
    par = at(196 + NCONST / KB, NPARAM)
    assert 196 * KB + NCONST + NPARAM <= 206 * KB

    def C(name, k=0, n=P):
        a = CCOL[name][0] + k * P
        return cst[:, a:a + n]

    def Pm(name, k=0, n=1):
        a = PCOL[name][0] + k
        return par[:, a:a + n]

    ident, ones, upto = C("ident"), C("ones"), C("upto")

    NSLOT = 4
    slot_sem = [sem(f"weights{s}") for s in range(NSLOT)]
    stream = []

    def plan(w, k0, n_cols, width):
        for c in range(n_cols // width):
            stream.append(w[:, k0 + c * width:k0 + (c + 1) * width])

    plan(w_in, 2048, 1024, 256)
    for q in range(4):
        plan(w_in, 256 * q, 256, 256)
        plan(w_in, 1024 + 256 * q, 256, 256)
    plan(w_in, 3072, 4096, 256)
    for q in range(4):
        for w in (conv_out, w_val, w_gate):
            plan(w, 512 * q, 512, 512)
    plan(w_out, 0, D, 256)
    plan(w_q, 0, D, 256)
    n_before_peer = len(stream)
    plan(a_in, 8192, 32, 32)
    plan(a_in, 6144, D, 256)
    for h in range(NH // 2):
        for part in range(3):
            plan(a_in, part * D + 256 * h, 256, 256)
    plan(a_out, 0, D, 256)
    plan(b_in, 2 * D, D, 256)
    plan(b_in, 3 * D, D, 256)
    for h in range(NH // 2):
        for part in range(2):
            plan(b_in, part * D + 256 * h, 256, 256)
    plan(b_out, 0, D, 256)

    slot_uses = [0] * NSLOT
    started = [0]
    used = [0]

    def slot_view(n):
        w = stream[n]
        kn = w.shape[0] // P
        return at(16 * (n % NSLOT), kn, w.shape[1])

    def start_load():
        n = started[0]
        w = stream[n]
        nc.sync.dma_start(slot_view(n), w.rearrange("(k p) n -> p k n", p=P)).then_inc(slot_sem[n % NSLOT], 16)
        slot_uses[n % NSLOT] += 1
        started[0] += 1

    def take_block():
        n = used[0]
        used[0] += 1
        return slot_view(n), (slot_sem[n % NSLOT], 16 * (n // NSLOT + 1))

    def release_block(last_use):
        hold = n_before_peer if not peer_done[0] else len(stream)
        if started[0] < hold:
            sp.wait(last_use)
            start_load()

    peer_done = [False]
    bank_free = {b: [] for b in range(8)}

    def use_bank(b):
        pe.wait(*bank_free[b])
        bank_free[b] = []

    lin_bank = [0]

    def linear(n_blocks, src, src_ready, evacuate, step=None, banks=(0, 1, 2), every=4):
        kn = src.shape[1]
        pe.wait(*src_ready)
        count = 0
        for blk in range(n_blocks):
            w, loaded = take_block()
            pe.wait(loaded)
            for pair in range(w.shape[2] // 256):
                b = banks[lin_bank[0] % len(banks)]
                lin_bank[0] += 1
                use_bank(b)
                acc = ps[:, b, :].rearrange("p (h t) -> p h t", h=2)
                for half in range(2):
                    col = (2 * pair + half) * P
                    for k in range(kn):
                        last = pe.mm(acc[:, half, :], w[:, k, col:col + P], src[:, k, :],
                                     start=(k == 0), stop=(k == kn - 1))
                        count += 1
                        if k == kn - 1 and half == 1:
                            done = pe.mark(last)
                        if step is not None and count % every == 0:
                            step()
                bank_free[b] = evacuate(blk * (w.shape[2] // 256) + pair, acc, done)
            release_block(done)

    def runner(gen):
        state = [True]

        def step():
            if state[0]:
                try:
                    next(gen)
                except StopIteration:
                    state[0] = False

        def finish():
            while state[0]:
                step()
        return step, finish

    def rms(src, ready, gains, dst, sq, dst_free):
        t = act.act(sq, src, ACT.Square, after=ready + dst_free)
        use_bank(3)
        acc = ps[:, 3, 0:T]
        pe.wait(t)
        for c in range(NCH):
            last = pe.mm(acc, ones, sq[:, c, :], start=(c == 0), stop=(c == NCH - 1))
        t = pe.mark(last)
        root = sq[:, 0, :]
        t = act.act(root, acc, ACT.Sqrt, after=[t], scale=1.0 / D, bias=Pm("eps_rms"))
        bank_free[3] = [t]
        t = dve.recip(root, root, after=[t])
        for c in range(NCH):
            last = dve.stt(dst[:, c, :], src[:, c, :], Pm(gains, c), root, ALU.mult, ALU.mult,
                           after=[t] + ready + dst_free)
        return last

    xT, hT = at(64, NCH, T), at(80, NCH, T)
    x_tok = at(96, 2, D)
    x_src = x.rearrange("b (t p) d -> p (b t) d", p=P)
    t_small = small.start(nc.scalar, cst, consts)
    t_small = small.start(nc.scalar, par, params)
    t_small = small.start(nc.scalar, x_tok, x_src)
    for _ in range(NSLOT):
        start_load()

    def to_feature_major(tok_view, ready, dst, dst_free, extra=None):
        pe.wait(*ready)
        out_tokens = []
        for c2 in range(NCH // 2):
            b = c2 % 3
            use_bank(b)
            acc = ps[:, b, :].rearrange("p (h t) -> p h t", h=2)
            for half in range(2):
                c = 2 * c2 + half
                for t in range(2):
                    last = pe.mm(acc[:, half, t * P:(t + 1) * P], tok_view[:, t, c * P:(c + 1) * P], ident)
            done = pe.mark(last)
            d = dst[:, 2 * c2:2 * c2 + 2, :]
            if extra is None:
                t = act.act(d, acc, ACT.Copy, after=[done] + dst_free)
            else:
                t = dve.tt(d, acc, extra[:, 2 * c2:2 * c2 + 2, :], ALU.add, after=[done] + dst_free)
            bank_free[b] = [t]
            out_tokens.append(t)
        return out_tokens[-1]

    t_x = to_feature_major(x_tok, [t_small], xT, [])
    t_h = rms(xT, [t_x], "norm_mix", hT, at(112, NCH, T), [])

    NJ = 32
    co = at(185 - 6, 40, NJ)
    (dt_, r_, th, n_, s_, c_, k_re, k_im, m2, tmp) = (co[:, i, :] for i in range(10))
    cT_sb = at(185, 2, NJ, 32)
    cnew = at(64 + 4, 2, NJ, 32)
    start_fence = fence()
    pool.wait(t_small)
    t_c = small.start(nc.scalar, cT_sb, cT)
    a_re, a_im = Pm("a_re", 0, NJ), Pm("a_im", 0, NJ)
    t = act.act(dt_, Pm("log_dt", 0, NJ), ACT.Exp, after=[t_small])
    t1 = dve.tt(r_, a_re, dt_, ALU.mult, after=[t])
    t_r = act.act(r_, r_, ACT.Exp, after=[t1])
    t = dve.tt(th, a_im, dt_, ALU.mult, after=[t1])
    t = dve.ts(n_, th, 1.0 / (2 * np.pi), ALU.mult, ROUND, ALU.add, after=[t])
    t = dve.ts(n_, n_, -ROUND, ALU.add, after=[t])
    for part in TWO_PI:
        t = dve.stt(th, n_, -part, th, ALU.mult, ALU.add, after=[t])
    t = dve.ts(th, th, PI_SAFE, ALU.min, -PI_SAFE, ALU.max, after=[t])
    t_s = act.act(s_, th, ACT.Sin, after=[t])
    t = act.act(c_, th, ACT.Sin, after=[t], scale=0.5)
    t = dve.tt(c_, c_, c_, ALU.mult, after=[t])
    t_cos = dve.ts(c_, c_, -2.0, ALU.mult, 1.0, ALU.add, after=[t])
    t = dve.tt(tmp, r_, c_, ALU.mult, after=[t_cos, t_r])
    t_a = dve.ts(tmp, tmp, -1.0, ALU.add, after=[t])
    t_b = dve.tt(n_, r_, s_, ALU.mult, after=[t_s])
    t = dve.tt(m2, a_re, a_re, ALU.mult)
    t1 = dve.tt(dt_, a_im, a_im, ALU.mult, after=[t_b])
    t = dve.tt(m2, m2, dt_, ALU.add, after=[t1])
    t_m = dve.recip(m2, m2, after=[t])
    t1 = dve.tt(k_re, tmp, a_re, ALU.mult, after=[t_a])
    t = dve.tt(dt_, n_, a_im, ALU.mult, after=[t_m])
    t = dve.tt(k_re, k_re, dt_, ALU.add, after=[t])
    t_k1 = dve.tt(k_re, k_re, m2, ALU.mult, after=[t])
    t1 = dve.tt(k_im, n_, a_re, ALU.mult)
    t = dve.tt(dt_, tmp, a_im, ALU.mult, after=[t_k1])
    t = dve.tt(k_im, k_im, dt_, ALU.subtract, after=[t])
    t_k = dve.tt(k_im, k_im, m2, ALU.mult, after=[t])
    kr = wide(k_re.unsqueeze(2), [P, NJ, 32])
    ki = wide(k_im.unsqueeze(2), [P, NJ, 32])
    cre, cim = cT_sb[:, 0], cT_sb[:, 1]
    t1 = dve.tt(cnew[:, 0], cre, kr, ALU.mult, after=[t_k, t_c] + start_fence)
    t2 = dve.tt(cnew[:, 1], cim, ki, ALU.mult)
    t3 = dve.tt(cnew[:, 0], cnew[:, 0], cnew[:, 1], ALU.subtract, after=[t2])
    t4 = dve.tt(cnew[:, 1], cre, ki, ALU.mult, after=[t3])
    t5 = dve.tt(cre, cim, kr, ALU.mult, after=[t4])
    t6 = dve.stt(cim, cnew[:, 1], -1.0, cre, ALU.mult, ALU.subtract, after=[t5])
    t_cw = dve.copy(cre, cnew[:, 0], after=[t6])

    uT = at(96, 8, T)
    glu = at(104, 8, T + TAPS - 1)
    conv = at(113, 8, T)
    gates = at(121, 32, T)
    stage_free = fence()

    def evac_u(i, acc, done):
        return [act.act(uT[:, 2 * i:2 * i + 2, :], acc, ACT.Copy, after=[done] + stage_free)]

    linear(4, hT, [t_h], evac_u)
    t_u = (act.sem, act.n)
    t_pad = dve.memset(glu[:, :, 0:TAPS - 1], 0.0, after=stage_free)
    glu_ready = []
    sig = at(64 + 14, 2, T)
    value_bank = [None]

    def evac_glu(i, acc, done):
        if i % 2 == 0:
            value_bank[0] = (acc, done)
            return []
        q = i // 2
        t = act.act(sig, acc, ACT.Sigmoid, after=[done] + ([glu_ready[-1]] if glu_ready else stage_free))
        tg = dve.tt(glu[:, 2 * q:2 * q + 2, TAPS - 1:], value_bank[0][0], sig, ALU.mult, after=[t, value_bank[0][1]])
        glu_ready.append(tg)
        glu_banks[0] = [tg]
        return [t]

    glu_banks = [[]]
    for q in range(4):
        b_value = (0, 1, 2)[lin_bank[0] % 3]
        linear(1, hT, [], lambda i, acc, done: evac_glu(0, acc, done))
        linear(1, hT, [], lambda i, acc, done: evac_glu(2 * q + 1, acc, done))
        bank_free[b_value] = glu_banks[0]

    conv_sq = at(104, 8, T)
    conv_done = [None]

    def convolution():
        for c in range(8):
            for k in range(TAPS):
                w = Pm("dw_w", k * 8 + c)
                src = glu[:, c, k:k + T]
                if k == 0:
                    t = dve.ts(conv[:, c, :], src, w, ALU.mult, Pm("dw_b", c), ALU.add,
                               after=[glu_ready[c // 2], t_pad] + stage_free)
                else:
                    t = dve.stt(conv[:, c, :], src, w, conv[:, c, :], ALU.mult, ALU.add, after=[t])
                if k % 8 == 7:
                    yield
        t_conv = t
        use_bank(3)
        pe.wait(t_conv)
        for c in range(8):
            last = pe.mm(ps[:, 3, 0:T], ones, conv[:, c, :], start=(c == 0), stop=(c == 7))
        t = pe.mark(last)
        mean = at(64 + 12, T)
        t = act.act(mean, ps[:, 3, 0:T], ACT.Copy, after=[t] + stage_free, scale=1.0 / 1024)
        bank_free[3] = [t]
        t = dve.tt(conv, conv, wide(mean.unsqueeze(1), [P, 8, T]), ALU.subtract, after=[t])
        yield
        t = act.act(conv_sq, conv, ACT.Square, after=[t])
        use_bank(3)
        pe.wait(t)
        for c in range(8):
            last = pe.mm(ps[:, 3, 0:T], ones, conv_sq[:, c, :], start=(c == 0), stop=(c == 7))
        t = pe.mark(last)
        t = act.act(mean, ps[:, 3, 0:T], ACT.Sqrt, after=[t], scale=1.0 / 1024, bias=Pm("eps_ln"))
        bank_free[3] = [t]
        t = dve.recip(mean, mean, after=[t])
        for c in range(8):
            t1 = dve.stt(conv[:, c, :], conv[:, c, :], Pm("ln_g", c), mean, ALU.mult, ALU.mult, after=[t])
            conv_done[0] = act.act(conv[:, c, :], conv[:, c, :], ACT.Silu, after=[t1], bias=Pm("ln_b", c))
        yield

    phase = [at(153, 2, 4, T), at(161, 2, 4, T)]
    work = [at(169, 2, 4, T), at(64 + 4, 2, 4, T)]
    phase_tmp = at(64, 2, 4, P)
    bT_sb = [at(193, 2, P), at(194, 2, P)]
    bT_sem = [Loads(sem("b_weights0")), Loads(sem("b_weights1"))]
    ssm_done = [None]

    def fill_phase(c, free):
        E = phase[c % 2]
        t1 = pool.copy(E[:, 0, :, 0:1], c_[:, 4 * c:4 * c + 4].unsqueeze(2), after=[t_cos, t_s] + free)
        t = pool.copy(E[:, 1, :, 0:1], s_[:, 4 * c:4 * c + 4].unsqueeze(2))
        n = 1
        while n < T:
            for plane in range(2):
                pool.tt(E[:, plane, :, n:2 * n], E[:, plane, :, 0:n],
                        wide(E[:, 0, :, n - 1:n], [P, 4, n]), ALU.mult, after=[t])
            for plane in range(2):
                tq = pool.tt(phase_tmp[:, plane, :, 0:n], E[:, plane, :, 0:n],
                             wide(E[:, 1, :, n - 1:n], [P, 4, n]), ALU.mult, after=[t])
            pool.tt(E[:, 0, :, n:2 * n], E[:, 0, :, n:2 * n], phase_tmp[:, 1, :, 0:n], ALU.subtract, after=[tq])
            t = pool.tt(E[:, 1, :, n:2 * n], E[:, 1, :, n:2 * n], phase_tmp[:, 0, :, 0:n], ALU.add)
            n *= 2
        return t

    def ssm():
        pool.wait(*stage_free)
        phase_ready = [fill_phase(0, [t_cw]), None]
        y_read = []
        bank4 = ps[:, 4:8, :].rearrange("p i (q t) -> p q i t", q=2)
        t_bt = [bT_sem[0].start(nc.scalar, bT_sb[0], bT[0]), None]
        yield
        for c in range(8):
            if c + 1 < 8:
                act.wait((pe.sem, pe.n))
                t_bt[(c + 1) % 2] = bT_sem[(c + 1) % 2].start(nc.scalar, bT_sb[(c + 1) % 2], bT[c + 1])
                phase_ready[(c + 1) % 2] = fill_phase(c + 1, [(dve.sem, dve.n)])
            for b in range(4, 8):
                use_bank(b)
            pe.wait(t_bt[c % 2], t_u)
            for plane in range(2):
                for i in range(4):
                    rows = slice(32 * i, 32 * i + 32)
                    last = pe.mm(bank4[:, plane, i, :], bT_sb[c % 2][rows, plane, :], uT[rows, c, :])
            t_bu = pe.mark(last)
            yield
            E = phase[c % 2]
            A, B = work[c % 2], work[(c + 1) % 2]
            cosb = wide(E[:, 0].unsqueeze(1), [P, 2, 4, T])
            sinb = wide(E[:, 1].unsqueeze(1), [P, 2, 4, T])
            t = dve.tt(A, bank4, cosb, ALU.mult, after=[t_bu, phase_ready[c % 2]])
            t = dve.tt(B, bank4, sinb, ALU.mult, after=y_read[-1:])
            for b in range(4, 8):
                bank_free[b] = [t]
            yield
            t1 = dve.tt(A[:, 0], A[:, 0], B[:, 1], ALU.add, after=[t])
            t2 = dve.tt(A[:, 1], A[:, 1], B[:, 0], ALU.subtract)
            yield
            for plane in range(2):
                for i in range(4):
                    dve.wait(t1, t2)
                    t = dve.mark(nc.vector.tensor_tensor_scan(
                        B[:, plane, i, :], wide(r_[:, 4 * c + i:4 * c + i + 1], [P, T]), A[:, plane, i, :], 0.0,
                        ALU.mult, ALU.add))
                yield
            t1 = dve.tt(A, B, cosb, ALU.mult, after=[t])
            t2 = dve.tt(B, B, sinb, ALU.mult, after=[t1])
            yield
            t1 = dve.tt(A[:, 0], A[:, 0], B[:, 1], ALU.subtract, after=[t2])
            t2 = dve.tt(A[:, 1], A[:, 1], B[:, 0], ALU.add)
            yield
            use_bank(3)
            pe.wait(t1, t2)
            for plane in range(2):
                for i in range(4):
                    rows = slice(32 * i, 32 * i + 32)
                    last = pe.mm(ps[rows, 3, 0:T], cT_sb[:, plane, 4 * c + i, :], A[:, plane, i, :],
                                 start=(plane == 0), stop=(plane == 1))
            t = pe.mark(last)
            y_read.append(t)
            t = dve.stt(uT[:, c, :], uT[:, c, :], Pm("ssm_d", c), ps[:, 3, 0:T], ALU.mult, ALU.add, after=[t])
            bank_free[3] = [t]
            ssm_done[0] = act.act(uT[:, c, :], uT[:, c, :], ACT.Gelu_apprx_tanh, after=[t])
            yield

    def both_branches():
        a, b = ssm(), convolution()
        alive = [True, True]
        while any(alive):
            for i, g in enumerate((a, b)):
                if alive[i]:
                    try:
                        next(g)
                    except StopIteration:
                        alive[i] = False
            yield

    def evac_gates(i, acc, done):
        for half in range(2):
            f = 2 * i + half
            t = act.act(gates[:, f, :], acc[:, half, :], ACT.Sigmoid, after=[done] + stage_free,
                        bias=Pm("b_gate", f))
        return [t]

    step, finish = runner(both_branches())
    linear(16, hT, [], evac_gates, step, every=4)
    finish()
    t_gates = (act.sem, act.n)
    zT = uT

    x_tok2 = at(153, 2, D)
    reload_free = fence()
    act.wait(*reload_free)
    t_x2 = small.start(nc.scalar, x_tok2, x_src)
    side = at(169, 2, 2, T)
    merged = gates[:, 0:NCH, :]

    def evac_conv(q):
        def evac(i, acc, done):
            f = 4 * q + 2 * i
            return [dve.tt(gates[:, f:f + 2, :], acc, gates[:, f:f + 2, :], ALU.mult, after=[done, t_gates])]
        return evac

    side_free = [reload_free, reload_free]
    side_ready = [None, None]

    def evac_val(q):
        def evac(i, acc, done):
            f = 4 * q + 2 * i
            side_ready[i] = dve.tt(side[:, i], acc, gates[:, NCH + f:NCH + f + 2, :], ALU.mult,
                                   after=[done] + side_free[i])
            return [side_ready[i]]
        return evac

    sg = at(173, 2, 2, T)

    def evac_wgate(q):
        def evac(i, acc, done):
            f = 4 * q + 2 * i
            t = act.act(sg[:, i], acc, ACT.Sigmoid, after=[done] + side_free[i])
            t2 = dve.tt(side[:, i], side[:, i], sg[:, i], ALU.mult, after=[t, side_ready[i]])
            t3 = dve.tt(gates[:, f:f + 2, :], gates[:, f:f + 2, :], side[:, i], ALU.add, after=[t2])
            side_free[i] = [t3]
            return [t]
        return evac

    for q in range(4):
        linear(1, conv, [conv_done[0]], evac_conv(q))
        linear(1, zT, [ssm_done[0]], evac_val(q))
        linear(1, zT, [], evac_wgate(q))
    t_merged = (dve.sem, dve.n)

    x_free = fence()

    def residual_evac(i, acc, done):
        return [act.act(xT[:, 2 * i:2 * i + 2, :], acc, ACT.Copy, after=[done] + x_free)]

    pe.wait(t_merged, t_x2)
    for blk in range(8):
        w, loaded = take_block()
        pe.wait(loaded)
        b = lin_bank[0] % 3
        lin_bank[0] += 1
        use_bank(b)
        acc = ps[:, b, :].rearrange("p (h t) -> p h t", h=2)
        for half in range(2):
            c = 2 * blk + half
            for k in range(NCH):
                pe.mm(acc[:, half, :], w[:, k, half * P:(half + 1) * P], merged[:, k, :],
                      start=(k == 0), stop=False)
            for t in range(2):
                last = pe.mm(acc[:, half, t * P:(t + 1) * P], x_tok2[:, t, c * P:(c + 1) * P], ident,
                             start=False, stop=(t == 1))
        done = pe.mark(last)
        bank_free[b] = residual_evac(blk, acc, done)
        release_block(done)
    t_x1 = (act.sem, act.n)
    t_h = rms(xT, [t_x1], "norm_ffn", hT, at(96, NCH, T), fence())

    HC, NK, TOPK, HEADS = 16, 128, 16, 8
    peer_free = fence()
    qT = at(112, HC, T)
    keys = at(128, HC, NK)
    h_tok = at(136, 2, D)
    scores = at(152, HC, NK)
    cand = at(160, HEADS, TOPK * TOPK)
    onehot = at(152, HEADS * TOPK, TOPK)
    act.wait(*peer_free)
    t_keys = small.start(nc.scalar, keys, keysT)

    def evac_q(i, acc, done):
        return [act.act(qT[:, 2 * i:2 * i + 2, :], acc, ACT.Copy, after=[done] + peer_free)]

    linear(8, hT, [t_h], evac_q)
    t_q = (act.sem, act.n)
    pe.wait(*peer_free)
    for t in range(2):
        for g in range(4):
            b = g % 3
            use_bank(b)
            for i in range(4):
                last = pe.mm(ps[:, b, i * P:(i + 1) * P], hT[:, 4 * g + i, t * P:(t + 1) * P], ident)
            done = pe.mark(last)
            tt_ = act.act(h_tok[:, t, 512 * g:512 * (g + 1)], ps[:, b, :], ACT.Copy, after=[done] + peer_free)
            bank_free[b] = [tt_]
    t_htok = tt_

    small_at = 168
    top = at(small_at, HC, TOPK)
    top_i = at(small_at + 1, HC, TOPK).bitcast(U32)
    top_if = at(small_at + 2, HC, TOPK)
    best = at(small_at + 3, HEADS, TOPK)
    pos = at(small_at + 3.5, HEADS, TOPK).bitcast(U32)
    half_pos = at(small_at + 4, HEADS, TOPK).bitcast(U32)
    half_f = at(small_at + 4.5, HEADS * TOPK)
    e_part = at(small_at + 5, HEADS * TOPK)
    gate_sum = at(small_at + 5.5, HEADS)
    expert = [at(small_at + 6 + t / 2, HEADS * TOPK).bitcast(U32) for t in range(2)]
    route = [at(small_at + 7 + t / 2, HEADS, TOPK) for t in range(2)]
    dots = [at(small_at + 8 + t / 2, HEADS * TOPK) for t in range(2)]
    coef = [at(small_at + 9 + t / 2, HEADS * TOPK) for t in range(2)]

    def top16(values, vals_out, idx_out, ready):
        t = ready
        for r in range(2):
            o, ix = vals_out[:, 8 * r:8 * r + 8], idx_out[:, 8 * r:8 * r + 8]
            dve.wait(*t)
            t1 = dve.mark(nc.vector.max(out=o, in_=values))
            dve.wait(t1)
            t2 = dve.mark(nc.vector.max_index(out=ix, in_max=o, in_values=values))
            t = [t2]
            if r == 0:
                dve.wait(t2)
                t = [dve.mark(nc.vector.match_replace(out=values, in_to_replace=o, in_values=values,
                                                      imm_value=NEG))]
        return t[0]

    scores_read = peer_free
    routed = []
    for t in range(2):
        pe.wait(t_q, t_keys)
        for g in range(4):
            b = 4 + g
            use_bank(b)
            for i in range(4):
                hc = 4 * g + i
                last = pe.mm(ps[:, b, i * P:(i + 1) * P], qT[:, hc, t * P:(t + 1) * P], keys[:, hc, :])
            done = pe.mark(last)
            ts_ = act.act(scores[:, 4 * g:4 * g + 4, :], ps[:, b, :].rearrange("p (i n) -> p i n", i=4),
                          ACT.Copy, after=[done] + scores_read)
            bank_free[b] = [ts_]
        for hc in range(HC):
            tk = top16(scores[:, hc, :], top[:, hc, :], top_i[:, hc, :], [ts_] + peer_free)
        th_ = top.rearrange("p (h c) k -> p h c k", c=2)
        cand4 = cand.rearrange("p h (i j) -> p h i j", i=TOPK)
        tk = dve.tt(cand4, wide(th_[:, :, 0, :].unsqueeze(3), [P, HEADS, TOPK, TOPK]),
                    wide(th_[:, :, 1, :].unsqueeze(2), [P, HEADS, TOPK, TOPK]), ALU.add, after=[tk])
        for h in range(HEADS):
            tk = top16(cand[:, h, :], best[:, h, :], pos[:, h, :], [tk])
        ti = dve.copy(top_if, top_i, after=[tk])
        tif = top_if.rearrange("p (h c) k -> p h c k", c=2)
        prev = ti
        for half, (op, arg) in enumerate(((ALU.logical_shift_right, 4), (ALU.bitwise_and, 15))):
            t1 = dve.ts(half_pos, pos, arg, op, after=[prev])
            t1 = dve.copy(half_f, half_pos.rearrange("p h k -> p (h k)"), after=[t1])
            t1 = dve.tt(onehot, wide(half_f.unsqueeze(2), [P, HEADS * TOPK, TOPK]),
                        wide(C("iota", 0, 16).unsqueeze(1), [P, HEADS * TOPK, TOPK]), ALU.is_equal, after=[t1])
            oh4 = onehot.rearrange("p (h k) i -> p h k i", h=HEADS)
            t1 = dve.tt(oh4, oh4, wide(tif[:, :, half, :].unsqueeze(2), [P, HEADS, TOPK, TOPK]), ALU.mult,
                        after=[t1])
            dve.wait(t1)
            dst = e_part if half == 0 else half_f
            prev = dve.mark(nc.vector.tensor_reduce(dst, onehot, AX_X, ALU.add))
        te = dve.stt(e_part, e_part, float(NK), half_f, ALU.mult, ALU.add, after=[prev])
        te = dve.copy(expert[t], e_part, after=[te])
        mx = gate_sum
        tb = dve.copy(mx, best[:, :, 0], after=[te])
        tb = dve.tt(best, best, wide(mx.unsqueeze(2), [P, HEADS, TOPK]), ALU.subtract, after=[tb])
        tb = act.act(best, best, ACT.Exp, after=[tb])
        dve.wait(tb)
        tb = dve.mark(nc.vector.tensor_reduce(gate_sum, best, AX_X, ALU.add))
        tb = dve.recip(gate_sum, gate_sum, after=[tb])
        tb = dve.tt(route[t], best, wide(gate_sum.unsqueeze(2), [P, HEADS, TOPK]), ALU.mult, after=[tb])
        routed.append((te, tb))
        scores_read = [tb]

    NBUF, GRP = 4, 4
    NSEL = HEADS * TOPK
    u_buf = [at(8 * i, D) for i in range(NBUF)]
    v_buf = [at(32 + 8 * i, D) for i in range(NBUF)]
    u_sem = [Loads(sem(f"u_rows{i}")) for i in range(NBUF)]
    v_sem = [Loads(sem(f"v_rows{i}")) for i in range(NBUF)]
    diag = at(96, 2, GRP, P)
    u_free = [[(pe.sem, pe.n)]] * NBUF
    v_free = [[(pe.sem, pe.n)]] * NBUF
    peer_tok = at(112, 2, D)

    def gather(buf, loads, table, idx, free, ready):
        pool.wait(*free, *ready)
        nc.gpsimd.indirect_dma_start(out=buf, out_offset=None, in_=table,
                                     in_offset=bass.IndirectOffsetOnAxis(ap=idx, axis=0)).then_inc(loads.sem, 16)
        loads.n += 16
        return (loads.sem, loads.n)

    diag_free = [[], []]
    groups = [(t, g) for t in range(2) for g in range(NSEL // GRP)]
    coef_ready = {}

    def u_group(n):
        t, g = groups[n]
        for i in range(GRP):
            k = g * GRP + i
            loaded = gather(u_buf[i], u_sem[i], u_tab, expert[t][:, k:k + 1], u_free[i], [routed[t][0]])
            dve.wait(loaded, t_htok)
            td = dve.mark(nc.vector.tensor_tensor_reduce(
                out=u_buf[i], in0=u_buf[i], in1=h_tok[:, t, :], scale=1.0, scalar=0.0, op0=ALU.mult,
                op1=ALU.add, accum_out=dots[t][:, k:k + 1]))
            u_free[i] = [td]
        ks = slice(g * GRP, (g + 1) * GRP)
        tg = act.act(coef[t][:, ks], dots[t][:, ks], ACT.Gelu_apprx_tanh, after=[td])
        flat = route[t].rearrange("p h k -> p (h k)")
        tc = dve.tt(coef[t][:, ks], coef[t][:, ks], flat[:, ks], ALU.mult, after=[tg, routed[t][1]])
        for i in range(GRP):
            tc2 = dve.ts(diag[:, n % 2, i, :], ident, coef[t][:, g * GRP + i:g * GRP + i + 1], ALU.mult,
                         after=[tc] + diag_free[n % 2] + peer_free)
        coef_ready[n] = tc2

    def v_group(n):
        t, g = groups[n]
        for i in range(GRP):
            k = g * GRP + i
            loaded = gather(v_buf[i], v_sem[i], v_tab, expert[t][:, k:k + 1], v_free[i], [routed[t][0]])
            if g == 0 and i == 0:
                for b in range(4 * t, 4 * t + 4):
                    use_bank(b)
            pe.wait(loaded, coef_ready[n])
            for b in range(4):
                last = pe.mm(ps[:, 4 * t + b, :], diag[:, n % 2, i, :], v_buf[i][:, 512 * b:512 * (b + 1)],
                             start=(k == 0), stop=(k == NSEL - 1))
            done = pe.mark(last)
            v_free[i] = [done]
        diag_free[n % 2] = [done]
        if g == NSEL // GRP - 1:
            for b in range(4):
                te = act.act(peer_tok[:, t, 512 * b:512 * (b + 1)], ps[:, 4 * t + b, :], ACT.Copy,
                             after=[done])
                bank_free[4 * t + b] = [te]
            return te
        return None

    u_group(0)
    for n in range(len(groups)):
        if n + 1 < len(groups):
            u_group(n + 1)
        t_peer = v_group(n)
    gathers_done = fence()
    peer_done[0] = True
    sp.wait(*gathers_done)
    for _ in range(NSLOT):
        start_load()

    t_x = to_feature_major(peer_tok, [t_peer], xT, [], extra=xT)
    t_x = rms(xT, [t_x], "norm_final", xT, at(96, NCH, T), fence())
    t_h = rms(xT, [t_x], "norm2a", hT, at(96, NCH, T), fence())

    NE = 4
    stage_free = fence()
    zg = at(96, NCH, T)
    oT = at(112, NCH, T)
    qkv = [at(128, 6, T), at(134, 6, T)]
    raw = [at(140, 2, T + 3), at(142.5, 2, T + 3)]
    (E_, A_, Am, X_, Y_, Z_, QK, KB_T, VB, WK, V0, S_, WN, QD) = (at(145 + 2 * i, NE, P) for i in range(14))
    sqb = at(173, 4, T)
    KD = at(177, 2, P)
    V1 = at(178, 2, P)
    per_tok = at(179, 12, NH, 2)
    (g_, gc_, beta_, eg_, dk_, nbe_, gx_, gy_) = (per_tok[:, i] for i in range(8))
    neg_a = at(182.5, NH)

    w, loaded = take_block()
    use_bank(0)
    pe.wait(loaded, t_h)
    for t in range(2):
        for k in range(NCH):
            last = pe.mm(ps[:, 0, 32 * t:32 * t + 32], hT[:, k, t * P:(t + 1) * P], w[:, k, :],
                         start=(k == 0), stop=(k == NCH - 1))
    done = pe.mark(last)
    release_block(done)
    ab = ps[:, 0, 0:64].rearrange("p (t s h) -> p h t s", t=2, s=2)
    bias_b = wide(Pm("dt_bias", 0, NH).unsqueeze(2), [P, NH, 2])
    t1 = dve.tt(gx_, ab[:, :, :, 0], bias_b, ALU.add, after=[done] + stage_free)
    t2 = act.act(beta_, ab[:, :, :, 1], ACT.Sigmoid, after=[t1])
    bank_free[0] = [t1, t2]
    t_beta = t2
    t = dve.stt(gy_, gx_, -1.0, gx_, ALU.mult, ALU.min, after=[t1])
    t = act.act(gy_, gy_, ACT.Exp, after=[t])
    t = dve.ts(gy_, gy_, 1.0, ALU.add, after=[t])
    t = act.act(gy_, gy_, ACT.Ln, after=[t])
    t = dve.stt(gx_, gx_, 0.0, gy_, ALU.max, ALU.add, after=[t])
    ta = act.act(neg_a, Pm("a_log", 0, NH), ACT.Exp, after=stage_free)
    ta = dve.ts(neg_a, neg_a, -1.0, ALU.mult, after=[ta])
    t_g = dve.tt(g_, gx_, wide(neg_a.unsqueeze(2), [P, NH, 2]), ALU.mult, after=[t, ta])
    use_bank(1)
    pe.wait(t_g)
    gflat = g_.rearrange("p h t -> p (h t)")
    pe.mm(ps[:, 1, 0:32], upto, gflat)
    done = pe.mark(pe.mm(ps[:, 1, 32:64], ones, gflat))
    gcf = gc_.rearrange("p h t -> p (h t)")
    t_gc = dve.copy(gcf, ps[:, 1, 0:32], after=[done])
    t = dve.tt(dk_.rearrange("p h t -> p (h t)"), ps[:, 1, 32:64], gcf, ALU.subtract, after=[t_gc])
    bank_free[1] = [t]
    t_dk = act.act(dk_, dk_, ACT.Exp, after=[t])
    t = act.act(eg_, gc_, ACT.Exp, after=[t_gc])
    t_nb = dve.stt(nbe_, eg_, -1.0, beta_, ALU.mult, ALU.mult, after=[t, t_beta])

    def evac_z(i, acc, done):
        return [act.act(zg[:, 2 * i:2 * i + 2, :], acc, ACT.Silu, after=[done] + stage_free)]

    linear(8, hT, [], evac_z)
    for r in raw:
        t_pad = dve.memset(r[:, :, 0:3], 0.0, after=stage_free)
    core_read = [stage_free, stage_free]
    raw_free = [stage_free, stage_free]
    qkv_ready = [[], []]

    def evac_qkv(p, part):
        def evac(i, acc, done):
            r = raw[part % 2]
            tr = act.act(r[:, :, 3:], acc, ACT.Copy, after=[done, t_pad] + raw_free[part % 2])
            for hh in range(2):
                f = part * 16 + 2 * p + hh
                d = qkv[p % 2][:, 2 * part + hh, :]
                t = dve.ts(d, r[:, hh, 0:T], Pm("qkv_w", f), ALU.mult, after=[tr] + core_read[p % 2])
                for k in range(1, 4):
                    t = dve.stt(d, r[:, hh, k:k + T], Pm("qkv_w", 48 * k + f), d, ALU.mult, ALU.add, after=[t])
                raw_free[part % 2] = [t]
                qkv_ready[p % 2] = [act.act(d, d, ACT.Silu, after=[t])]
            return [tr]
        return evac

    def bank_e(b):
        return ps[:, b, :].rearrange("p (e n) -> p e n", e=NE)

    def each(b, lhsT, rhs, es=range(NE)):
        for e in es:
            last = pe.mm(bank_e(b)[:, e, :], lhsT(e), rhs(e))
        return pe.mark(last)

    norm_done = [[]]

    def rms_pair(src, n, squares, scale, eps, ready):
        t = act.act(squares, src, ACT.Square, after=ready)
        for j in range(n // 2):
            use_bank(3 + j)
            pe.wait(t)
            last = pe.mm(ps[:, 3 + j, :], ones, squares[:, 2 * j:2 * j + 2, :])
            tp = pe.mark(last)
            ta = act.act(squares[:, 2 * j:2 * j + 2, :], ps[:, 3 + j, :].rearrange("p (a t) -> p a t", a=2),
                         ACT.Sqrt, after=[tp], scale=scale, bias=eps)
            bank_free[3 + j] = [ta]
        return dve.recip(squares, squares, after=[ta])

    def delta_core(p):
        src = qkv[p % 2]
        ready = qkv_ready[p % 2]
        hs = slice(2 * p, 2 * p + 2)
        prev = fence()
        qk4 = src[:, 0:4, :]
        t_r = rms_pair(qk4, 4, sqb, 1.0, Pm("eps_rms"), ready + prev)
        yield
        t_qn = dve.stt(src[:, 0:2], src[:, 0:2], float(P) ** -0.5, sqb[:, 0:2], ALU.mult, ALU.mult, after=[t_r])
        t_kn = dve.tt(src[:, 2:4], src[:, 2:4], sqb[:, 2:4], ALU.mult, after=[t_r])

        def tile(a):
            return lambda e: src[:, 2 * a + e // 2, (e % 2) * P:(e % 2 + 1) * P]

        q_, k_, v_ = tile(0), tile(1), tile(2)

        def col(v):
            return lambda e: wide(v[:, 2 * p + e // 2, e % 2:e % 2 + 1], [P, P])

        yield
        use_bank(5)
        pe.wait(t_beta, t_g)
        tb = each(5, col(beta_), lambda e: ident)
        use_bank(6)
        tg = each(6, col(g_), lambda e: upto)
        t_kb = dve.tt(KB_T, src[:, 2:4].rearrange("p h (t n) -> p (h t) n", t=2), bank_e(5), ALU.mult,
                      after=[tb, t_kn] + prev)
        bank_free[5] = [t_kb]
        for e in range(NE):
            td = dve.ts(E_[:, e, :], bank_e(6)[:, e, :], gc_[:, 2 * p + e // 2, e % 2:e % 2 + 1], ALU.subtract,
                        0.0, ALU.min, after=[tg, t_gc])
        yield
        gc1 = bank_e(6)[:, 1:4:2, :]
        qd2 = QD[:, 0:2, :]
        tq = act.act(qd2, gc1, ACT.Exp, after=[td] + prev)
        bank_free[6] = [td, tq]
        td = act.act(E_, E_, ACT.Exp, after=[td])
        td = pool.tt(E_, E_, wide(upto.unsqueeze(1), [P, NE, P]), ALU.mult, after=[td])
        t_qd = dve.tt(qd2, qd2, src[:, 0:2, P:2 * P], ALU.mult, after=[tq, t_qn])
        use_bank(3)
        pe.wait(t_qn, t_kn)
        tp = each(3, k_, q_)
        t_qk = dve.tt(QK, E_, bank_e(3), ALU.mult, after=[tp, td] + prev)
        bank_free[3] = [t_qk]
        yield
        use_bank(4)
        pe.wait(t_kb)
        tp = each(4, k_, lambda e: KB_T[:, e, :])
        t_a = dve.tt(A_, E_, bank_e(4), ALU.mult, after=[tp])
        bank_free[4] = [t_a]
        level = lambda l: wide(C("level", l).unsqueeze(1), [P, NE, P])
        ti = pool.tt(Am, A_, level(0), ALU.mult, after=[t_a] + prev)
        t_z = dve.stt(Z_, Am, -1.0, wide(ident.unsqueeze(1), [P, NE, P]), ALU.mult, ALU.add, after=[ti])
        am_free = t_z
        yield
        use_bank(7)
        tp = each(7, k_, lambda e: ident)
        kt = bank_e(7)
        dkb = wide(dk_[:, hs, 0:1], [P, 2, P])
        nbb = wide(nbe_[:, hs, 1:2], [P, 2, P])
        t_kd = dve.tt(KD, kt[:, 0:4:2, :], dkb, ALU.mult, after=[tp, t_dk] + prev)
        t_wk = dve.tt(WK[:, 0:2, :], kt[:, 1:4:2, :], nbb, ALU.mult, after=[t_nb])
        bank_free[7] = [t_wk]
        use_bank(5)
        pe.wait(*ready)
        tp = each(5, v_, lambda e: ident)
        t_vb = dve.tt(VB, bank_e(5), wide(beta_[:, hs, :].rearrange("p h t -> p (h t)").unsqueeze(2), [P, NE, P]),
                      ALU.mult, after=[tp])
        bank_free[5] = [t_vb]
        core_read[p % 2] = [t_vb, t_qd, (pe.sem, pe.n)]
        yield
        use_bank(6)
        pe.wait(t_z)
        tp = each(6, lambda e: Z_[:, e, :], lambda e: ident)
        t_x = act.act(X_, bank_e(6), ACT.Copy, after=[tp] + prev)
        bank_free[6] = [t_x]
        for l in range(1, 7):
            tm = pool.tt(Am, A_, level(l), ALU.mult, after=[am_free])
            yield
            use_bank(3)
            pe.wait(tm, t_x)
            tp = each(3, lambda e: Am[:, e, :], lambda e: X_[:, e, :])
            am_free = tp
            ty = act.act(Y_, bank_e(3), ACT.Copy, after=[tp] + prev)
            bank_free[3] = [ty]
            yield
            pe.wait(ty, t_z)
            use_bank(5)
            tz = each(5, lambda e: Y_[:, e, :], lambda e: Z_[:, e, :])
            if l < 6:
                use_bank(4)
                tx = each(4, lambda e: Z_[:, e, :], lambda e: Y_[:, e, :])
                t_x = dve.tt(X_, X_, bank_e(4), ALU.subtract, after=[tx])
                bank_free[4] = [t_x]
                tz = tx
            t_z = dve.tt(Z_, Z_, bank_e(5), ALU.subtract, after=[tz])
            bank_free[5] = [t_z]
            yield
        use_bank(3)
        pe.wait(t_z, t_vb)
        tp = each(3, lambda e: Z_[:, e, :], lambda e: VB[:, e, :], es=(0, 2))
        t_v0 = act.act(V0[:, 0:2, :], bank_e(3)[:, 0:4:2, :], ACT.Copy, after=[tp] + prev)
        bank_free[3] = [t_v0]
        use_bank(4)
        pe.wait(t_wk)
        tp = each(4, lambda e: WK[:, e // 2, :], lambda e: Z_[:, e, :], es=(1, 3))
        t_wn = dve.copy(WN[:, 0:2, :], bank_e(4)[:, 1:4:2, :], after=[tp] + prev)
        bank_free[4] = [t_wn]
        yield
        use_bank(6)
        pe.wait(t_v0, t_kd)
        tp = each(6, lambda e: KD[:, e, :], lambda e: V0[:, e, :], es=(0, 1))
        t_s = act.act(S_[:, 0:2, :], bank_e(6)[:, 0:2, :], ACT.Copy, after=[tp] + prev)
        bank_free[6] = [t_s]
        yield
        use_bank(5)
        pe.wait(t_s, t_wn)
        for hh in range(2):
            pe.mm(bank_e(5)[:, hh, :], Z_[:, 2 * hh + 1, :], VB[:, 2 * hh + 1, :], start=True, stop=False)
            last = pe.mm(bank_e(5)[:, hh, :], WN[:, hh, :], S_[:, hh, :], start=False, stop=True)
        tp = pe.mark(last)
        t_v1 = act.act(V1, bank_e(5)[:, 0:2, :], ACT.Copy, after=[tp] + prev)
        bank_free[5] = [t_v1]
        yield
        use_bank(7)
        pe.wait(t_qk, t_v1, t_qd)
        for hh in range(2):
            pe.mm(bank_e(7)[:, 2 * hh, :], V0[:, hh, :], QK[:, 2 * hh, :])
            pe.mm(bank_e(7)[:, 2 * hh + 1, :], V1[:, hh, :], QK[:, 2 * hh + 1, :], start=True, stop=False)
            last = pe.mm(bank_e(7)[:, 2 * hh + 1, :], S_[:, hh, :], QD[:, hh, :], start=False, stop=True)
        tp = pe.mark(last)
        o2 = ps[:, 7, :].rearrange("p (h t) -> p h t", h=2)
        dst = oT[:, 2 * p:2 * p + 2, :]
        t_o = act.act(dst, o2, ACT.Copy, after=[tp])
        bank_free[7] = [t_o]
        yield
        t_r = rms_pair(dst, 2, sqb[:, 0:2], 1.0 / P, Pm("eps_rms"), [t_o])
        t = dve.stt(dst, dst, Pm("onorm"), sqb[:, 0:2], ALU.mult, ALU.mult, after=[t_r])
        core_last[0] = dve.tt(dst, dst, zg[:, 2 * p:2 * p + 2, :], ALU.mult, after=[t])
        yield

    core_last = [None]
    finish = None
    step = None
    for p in range(NH // 2):
        for part in range(3):
            linear(1, hT, [], evac_qkv(p, part), step, every=4)
        if finish is not None:
            finish()
        step, finish = runner(delta_core(p))
    finish()

    def evac_res(i, acc, done):
        d = xT[:, 2 * i:2 * i + 2, :]
        return [dve.tt(d, d, acc, ALU.add, after=[done])]

    linear(8, oT, [core_last[0]], evac_res)
    t_x = (dve.sem, dve.n)

    t_h = rms(xT, [t_x], "norm2b", hT, at(96, NCH, T), fence())
    stage_free = fence()
    v_tok = at(128, 2, D)
    hankel = at(144, NH, T)
    qk = [at(160, 4, T), at(164, 4, T)]
    sqb = at(168, 4, T)
    prob = at(172, 2, 384)
    probT = at(175, 2, 3, P)
    stat = at(178, 8, 4)
    gain = at(179, 2)
    act.wait(*stage_free)
    rsrc = bass.AP(tensor=rel_rev.tensor, offset=1, ap=[[1, P], [513, NH], [1, T]])
    t_rel = small.start(nc.scalar, hankel, rsrc)
    t_gain = dve.ts(gain[:, 0:1], Pm("qnorm"), float(P) ** -0.5, ALU.mult, after=stage_free)
    t_gain = dve.copy(gain[:, 1:2], Pm("knorm"))

    pe.wait(t_h)
    for blk in range(8):
        w, loaded = take_block()
        pe.wait(loaded)
        b = lin_bank[0] % 3
        lin_bank[0] += 1
        use_bank(b)
        for t in range(2):
            for k in range(NCH):
                last = pe.mm(ps[:, b, 256 * t:256 * t + 256], hT[:, k, t * P:(t + 1) * P], w[:, k, :],
                             start=(k == 0), stop=(k == NCH - 1))
        done = pe.mark(last)
        release_block(done)
        t_v = act.act(v_tok[:, :, 256 * blk:256 * blk + 256], ps[:, b, :].rearrange("p (t n) -> p t n", t=2),
                      ACT.Copy, after=[done] + stage_free)
        bank_free[b] = [t_v]
    linear(8, hT, [], evac_z)
    qk_free = [stage_free, stage_free]
    qk_ready = [[], []]

    def evac_qk(p, part):
        def evac(i, acc, done):
            t = act.act(qk[p % 2][:, 2 * part:2 * part + 2, :], acc, ACT.Copy, after=[done] + qk_free[p % 2])
            qk_ready[p % 2] = [t]
            return [t]
        return evac

    def attention_core(p):
        src = qk[p % 2]
        prev = fence()
        t_r = rms_pair(src, 4, sqb, 1.0 / P, Pm("eps_rms"), qk_ready[p % 2] + prev)
        yield
        for a in range(2):
            t_n = dve.stt(src[:, 2 * a:2 * a + 2], src[:, 2 * a:2 * a + 2], gain[:, a:a + 1],
                          sqb[:, 2 * a:2 * a + 2], ALU.mult, ALU.mult, after=[t_r, t_gain])
        yield
        pe.wait(t_n, t_rel)
        for hh in range(2):
            h = 2 * p + hh
            use_bank(5 + hh)
            s = ps[:, 5 + hh, 0:384]
            qh, kh = src[:, hh, :], src[:, 2 + hh, :]
            pe.mm(s[:, 0:P], qh[:, 0:P], kh[:, 0:P], start=True, stop=False)
            pe.mm(s[:, 0:P], C("flip"), hankel[:, h, P:2 * P], start=False, stop=True)
            pe.mm(s[:, P:384], qh[:, P:T], kh, start=True, stop=False)
            tp = pe.mark(pe.mm(s[:, P:384], C("flip"), hankel[:, h, :], start=False, stop=True))
            t = dve.tt(prob[:, hh, :], s, C("band", 0, 384), ALU.add, after=[tp] + prev)
            bank_free[5 + hh] = [t]
            dve.wait(t)
            for i, cols in enumerate((slice(0, P), slice(P, 384))):
                t = dve.mark(nc.vector.tensor_reduce(stat[:, 0, 2 * hh + i:2 * hh + i + 1], prob[:, hh, cols],
                                                     AX_X, ALU.max, negate=True))
            for i, cols in enumerate((slice(0, P), slice(P, 384))):
                te = act.act(prob[:, hh, cols], prob[:, hh, cols], ACT.Exp, after=[t],
                             bias=stat[:, 0, 2 * hh + i:2 * hh + i + 1],
                             accum_out=stat[:, 1, 2 * hh + i:2 * hh + i + 1])
            yield
        qk_free[p % 2] = [tp]
        t = dve.recip(stat[:, 1], stat[:, 1], after=[te])
        for hh in range(2):
            for i, cols in enumerate((slice(0, P), slice(P, 384))):
                t1 = dve.ts(prob[:, hh, cols], prob[:, hh, cols], stat[:, 1, 2 * hh + i:2 * hh + i + 1],
                            ALU.mult, after=[t])
        yield
        pe.wait(t1)
        for hh in range(2):
            use_bank(5 + hh)
            for j in range(3):
                last = pe.mm(ps[:, 5 + hh, j * P:(j + 1) * P], prob[:, hh, j * P:(j + 1) * P], ident)
            tp = pe.mark(last)
            t2 = act.act(probT[:, hh], ps[:, 5 + hh, 0:384].rearrange("p (j n) -> p j n", j=3), ACT.Copy,
                         after=[tp] + prev)
            bank_free[5 + hh] = [t2]
            yield
        use_bank(7)
        pe.wait(t2, t_v)
        for hh in range(2):
            h = 2 * p + hh
            vh = slice(h * P, (h + 1) * P)
            o = ps[:, 7, 256 * hh:256 * hh + 256]
            pe.mm(o[:, 0:P], v_tok[:, 0, vh], probT[:, hh, 0, :])
            pe.mm(o[:, P:T], v_tok[:, 0, vh], probT[:, hh, 1, :], start=True, stop=False)
            last = pe.mm(o[:, P:T], v_tok[:, 1, vh], probT[:, hh, 2, :], start=False, stop=True)
        tp = pe.mark(last)
        core_last[0] = dve.tt(oT[:, 2 * p:2 * p + 2, :], zg[:, 2 * p:2 * p + 2, :],
                              ps[:, 7, :].rearrange("p (h t) -> p h t", h=2), ALU.mult,
                              after=[tp, (act.sem, z_done)] + stage_free)
        bank_free[7] = [core_last[0]]
        yield

    z_done = act.n
    finish = None
    step = None
    for p in range(NH // 2):
        for part in range(2):
            linear(1, hT, [], evac_qk(p, part), step, every=2)
        if finish is not None:
            finish()
        step, finish = runner(attention_core(p))
    finish()

    y = [at(160, 2, 256), at(162, 2, 256)]
    y_sem = [Loads(sem("y_stored0")), Loads(sem("y_stored1"))]
    y_free = [[], []]
    end_free = fence()
    dst = out.rearrange("b (t p) d -> p (b t) d", p=P)
    pe.wait(core_last[0], t_x)
    for blk in range(8):
        w, loaded = take_block()
        pe.wait(loaded)
        b = lin_bank[0] % 3
        lin_bank[0] += 1
        use_bank(b)
        for t in range(2):
            acc = ps[:, b, 256 * t:256 * t + 256]
            for k in range(NCH):
                pe.mm(acc, oT[:, k, t * P:(t + 1) * P], w[:, k, :], start=(k == 0), stop=False)
            for i in range(2):
                last = pe.mm(acc[:, i * P:(i + 1) * P], xT[:, 2 * blk + i, t * P:(t + 1) * P], ident,
                             start=False, stop=(i == 1))
        done = pe.mark(last)
        release_block(done)
        ty = act.act(y[blk % 2], ps[:, b, :].rearrange("p (t n) -> p t n", t=2), ACT.Copy,
                     after=[done] + y_free[blk % 2] + end_free)
        bank_free[b] = [ty]
        sp.wait(ty)
        y_free[blk % 2] = [y_sem[blk % 2].start(nc.sync, dst[:, :, 256 * blk:256 * blk + 256], y[blk % 2])]
    for loads in y_sem:
        nc.sync.wait_ge(loads.sem, loads.n)
    ctx.close()


def _columns(v):
    return np.ascontiguousarray(v.reshape(-1, P).T)


def _states(a):
    return a.reshape(32, P).T


def _constants():
    c = np.zeros((P, NCONST), np.float32)
    i = np.arange(P)
    row, col = i[:, None], i[None, :]
    c[:, 0:P] = row == col
    c[:, P:2 * P] = 1.0
    c[:, 2 * P:3 * P] = row <= col
    c[:, 3 * P:4 * P] = row + col == P - 1
    for l in range(7):
        b = 1 << l
        c[:, (4 + l) * P:(5 + l) * P] = (row // (2 * b) == col // (2 * b)) & (row % (2 * b) < b) & (col % (2 * b) >= b)
    q = i[:, None] // CHUNK
    c[:, 11 * P:12 * P] = np.where(col // CHUNK <= q, 0.0, NEG)
    k = np.arange(2 * P)[None, :] // CHUNK
    c[:, 12 * P:14 * P] = np.where(k <= q + 2, 0.0, NEG)
    c[:, 14 * P:14 * P + 16] = np.arange(16)
    return c


def _layout(inp):
    f = {k: np.asarray(v) for k, v in inp.items()}
    L = lambda name: f[name][0]
    par = np.zeros((P, NPARAM), np.float32)

    def put(name, v):
        a, n = PCOL[name]
        par[:, a:a + n] = v

    for name, src in (("norm_mix", "norm_mix"), ("b_gate", "b_gate"), ("dw_b", "conv_b_dw"), ("ln_g", "conv_ln_g"),
                      ("ln_b", "conv_ln_b"), ("ssm_d", "ssm_d"), ("norm_ffn", "norm_ffn"),
                      ("norm2a", "norm_w_2"), ("onorm", "a_out_norm_w_2"), ("qnorm", "b_q_norm_w_2"),
                      ("knorm", "b_k_norm_w_2")):
        put(name, _columns(L(src)))
    put("norm_final", _columns(f["norm_final"]))
    put("norm2b", _columns(f["norm_w_2"][1]))
    put("dw_w", _columns(L("conv_w_dw").reshape(-1)))
    put("qkv_w", _columns(L("a_conv_w_2").reshape(-1)))
    put("a_re", _states(L("ssm_a_re")))
    put("a_im", _states(L("ssm_a_im")))
    put("log_dt", _states(np.repeat(L("ssm_log_dt")[:, None], 64, 1)))
    put("a_log", np.broadcast_to(L("a_a_log_2"), (P, 16)))
    put("dt_bias", np.broadcast_to(L("a_dt_bias_2"), (P, 16)))
    put("eps_rms", RMS_EPS)
    put("eps_ln", LN_EPS)
    bT = np.zeros((8, 4, 2, 16, 2, 2, 64), np.float32)
    cT = np.zeros((2, 64, 2, 32, 2, 16), np.float32)
    for plane, (b, c) in enumerate(((L("ssm_b_re"), L("ssm_c_re")), (L("ssm_b_im"), L("ssm_c_im")))):
        b5 = b.reshape(8, 4, 2, 64, 16)
        c4 = c.reshape(32, 2, 16, 64)
        for g in range(2):
            bT[:, :, g, :, plane, g, :] = b5[:, :, g].transpose(0, 1, 3, 2)
            cT[g, :, plane, :, g, :] = c4[:, g].transpose(2, 0, 1)
    keysT = L("peer_sub_keys").reshape(16, 128, 128).transpose(2, 0, 1)
    return {
        "x": f["x"], "consts": _constants(), "params": par, "w_in": L("w_in"), "conv_out": L("conv_w_out"),
        "bT": bT.reshape(8, P, 2, P), "cT": cT.reshape(P, 2, 32, 32), "w_val": L("ssm_w_val"),
        "w_gate": L("ssm_w_gate"), "w_out": L("w_out"), "w_q": L("peer_w_q"), "keysT": keysT,
        "u_tab": L("peer_u"), "v_tab": L("peer_v"), "a_in": L("a_w_in_2"), "a_out": L("a_w_out_2"),
        "b_in": L("b_w_in_2"), "rel_rev": L("b_rel_bias_2")[:, ::-1], "b_out": L("b_w_out_2"),
    }


def kernel(**inputs):
    import concourse.bacc as bacc
    from concourse.bass_utils import run_bass_kernel_spmd

    nc = bacc.Bacc("TRN2", target_bir_lowering=False, num_devices=1)
    arrays = {k: np.ascontiguousarray(v) for k, v in _layout(inputs).items()}
    args = {k: nc.dram_tensor(k, v.shape, mybir.dt.from_np(v.dtype), kind="ExternalInput").ap()
            for k, v in arrays.items()}
    out = nc.dram_tensor("out", (1, 256, 2048), F32, kind="ExternalOutput").ap()
    build(nc, out=out, **args)
    got = run_bass_kernel_spmd(nc, [arrays], core_ids=[0])
    return got.results[0]["out"]
```

```python
from contextlib import ExitStack

import concourse.bass as bass
import concourse.mybir as mybir
import numpy as np
from concourse.alu_op_type import AluOpType as ALU

F32 = mybir.dt.float32
F32R = mybir.dt.float32r
U32 = mybir.dt.uint32
ACT = mybir.ActivationFunctionType
AX_X = mybir.AxisListType.X

P = 128
KB = 256
NEG = -3.0e38
RMS_EPS, LN_EPS = 1e-6, 1e-5
CHUNK = 64
PI_SAFE = 3.1415925
ROUND = 12582912.0
TWO_PI = (6.28125, 0.0019350051879882812, 3.019916050561733e-07)


class Engine:

    def __init__(self, handle, semaphore):
        self.e, self.sem, self.n, self.seen = handle, semaphore, 0, {}

    def wait(self, *tokens):
        for sem, value in tokens:
            if self.seen.get(sem.name, 0) < value:
                self.e.wait_ge(sem, value)
                self.seen[sem.name] = value

    def mark(self, instruction):
        instruction.then_inc(self.sem, 1)
        self.n += 1
        return (self.sem, self.n)


class Vec(Engine):

    def tt(self, out, a, b, op, after=()):
        self.wait(*after)
        return self.mark(self.e.tensor_tensor(out, a, b, op))

    def ts(self, out, a, s1, op0, s2=None, op1=None, after=()):
        self.wait(*after)
        if op1 is None:
            return self.mark(self.e.tensor_scalar(out, a, s1, None, op0))
        return self.mark(self.e.tensor_scalar(out, a, s1, s2, op0, op1))

    def stt(self, out, a, s, b, op0, op1, after=()):
        self.wait(*after)
        return self.mark(self.e.scalar_tensor_tensor(out=out, in0=a, scalar=s, in1=b, op0=op0, op1=op1))

    def copy(self, out, a, after=()):
        self.wait(*after)
        return self.mark(self.e.tensor_copy(out, a))

    def memset(self, out, value, after=()):
        self.wait(*after)
        return self.mark(self.e.memset(out, value))

    def recip(self, out, a, after=()):
        self.wait(*after)
        return self.mark(self.e.reciprocal(out, a))


class Scalar(Engine):

    def act(self, out, a, func, after=(), **kw):
        self.wait(*after)
        return self.mark(self.e.activation(out, a, func, **kw))


class Tensor(Engine):

    def mm(self, out, lhsT, rhs, start=True, stop=True, after=()):
        self.wait(*after)
        return self.e.matmul(out, lhsT, rhs, start=start, stop=stop, skip_group_check=True)


class Loads:

    def __init__(self, semaphore):
        self.sem, self.n = semaphore, 0

    def start(self, queue, out, in_):
        queue.dma_start(out, in_).then_inc(self.sem, 16)
        self.n += 16
        return (self.sem, self.n)


def wide(ap, shape):
    return ap.broadcast_to(shape)


def param_columns():
    at, cols = 0, {}
    for name, n in (("norm_mix", 16), ("b_gate", 32), ("dw_w", 31 * 8), ("dw_b", 8), ("ln_g", 8), ("ln_b", 8),
                    ("a_re", 32), ("a_im", 32), ("log_dt", 32), ("ssm_d", 8), ("norm_ffn", 16),
                    ("norm_final", 16), ("norm2a", 16), ("norm2b", 16), ("qkv_w", 4 * 48), ("onorm", 1),
                    ("qnorm", 1), ("knorm", 1), ("a_log", 16), ("dt_bias", 16), ("eps_rms", 1), ("eps_ln", 1)):
        cols[name] = (at, n)
        at += n
    return cols, at


PCOL, NPARAM = param_columns()


def weight_plan():
    plan = []

    def add(name, first, n, k=2048):
        width = 2048 * P // k
        plan.extend((name, first + c * width, width) for c in range(n // width))

    add("w_in", 2048, 1024)
    for q in range(4):
        add("w_in", 256 * q, 256)
        add("w_in", 1024 + 256 * q, 256)
    add("w_in", 3072 + 2048, 2048)
    for q in range(4):
        add("w_in", 3072 + 512 * q, 512)
        add("conv_out", 512 * q, 512, 1024)
    for q in range(4):
        add("w_val", 512 * q, 512, 1024)
        add("w_gate", 512 * q, 512, 1024)
    add("w_out", 0, 2048)
    add("w_q", 0, 2048)
    before_peer = len(plan)
    for h in range(8):
        for part in range(4):
            add("a_in", part * 2048 + 256 * h, 256)
    add("a_out", 0, 2048)
    for h in range(8):
        for part in range(4):
            add("b_in", part * 2048 + 256 * h, 256)
    add("b_out", 0, 2048)
    return plan, before_peer


PLAN, N_BEFORE_PEER = weight_plan()
CCOL = {"ident": (0, P), "ones": (P, P), "upto": (2 * P, P), "flip": (3 * P, P), "level": (4 * P, 7 * P),
        "band": (11 * P, 3 * P), "iota": (14 * P, 16)}
NCONST = 14 * P + 16


def build(nc, x, consts, params, weights, bcT, keysT, u_tab, v_tab, a_small, rel_rev, out):
    D, T, NCH = 2048, 256, 16
    TAPS = 31
    NH = 16
    ctx = ExitStack()

    def sem(name):
        return ctx.enter_context(nc.semaphore(name))

    ps = ctx.enter_context(nc.psum_tensor("ps", [P, 8, 512], F32))

    pe = Tensor(nc.tensor, sem("pe_done"))
    dve = Vec(nc.vector, sem("dve_done"))
    pool = Vec(nc.gpsimd, sem("pool_done"))
    act = Scalar(nc.scalar, sem("act_done"))
    sp = Engine(nc.sync, None)
    small = Loads(sem("small_loads"))

    LOW = 64
    placed = {}

    def place(kb, size, dtype):
        if (kb, size, dtype) not in placed:
            with ExitStack() as frame:
                if kb:
                    frame.enter_context(nc.sbuf_tensor(f"filler{len(placed)}", [P, int(kb * KB)], F32))
                placed[kb, size, dtype] = frame.enter_context(
                    nc.sbuf_tensor(f"{dtype.name}_at_{len(placed)}", [P, int(size * KB)], dtype))
        return placed[kb, size, dtype]

    def at(kb, *shape, dtype=F32):
        n = int(np.prod(shape))
        if dtype == F32:
            base, size = (0, LOW) if kb < LOW else (LOW, 206 - LOW)
        else:
            base, size = kb, n / KB
        first = int((kb - base) * KB)
        assert first + n <= size * KB, (kb, shape)
        v = place(base, size, dtype)[:, first:first + n]
        if len(shape) == 1:
            return v
        names = "abcd"[:len(shape)]
        sizes = {k: s for k, s in zip(names[1:], shape[1:])}
        return v.rearrange(f"p ({' '.join(names)}) -> p {' '.join(names)}", **sizes)

    def rat(kb, *shape):
        return at(kb, *shape, dtype=F32R)

    def fence():
        return [(e.sem, e.n) for e in (pe, dve, pool, act) if e.n]

    cst = at(196, NCONST)
    par = at(196 + NCONST / KB, NPARAM)
    assert 196 * KB + NCONST + NPARAM <= 206 * KB

    def C(name, k=0, n=P):
        a = CCOL[name][0] + k * P
        return cst[:, a:a + n]

    def Pm(name, k=0, n=1):
        a = PCOL[name][0] + k
        return par[:, a:a + n]

    ident, ones, upto = C("ident"), C("ones"), C("upto")

    NSLOT, NHI, BLOCK = 5, 3, 2048
    slot_sem = [sem(f"weights{s}") for s in range(NSLOT)]
    started, used, split = [0], [0], [0]
    limit = [N_BEFORE_PEER]
    block_done = {}
    block_split = {}
    pool_quarters = [1]

    def start_load():
        n = started[0]
        nc.sync.dma_start(at(8 * (n % NSLOT), BLOCK), weights[n]).then_inc(slot_sem[n % NSLOT], 16)
        started[0] += 1

    def split_quarter():
        n, q = split[0] // 4, split[0] % 4
        split[0] += 1
        cols = slice(q * BLOCK // 4, (q + 1) * BLOCK // 4)
        w, lo = at(8 * (n % NSLOT), BLOCK)[:, cols], rat(8 * (n % NSLOT), BLOCK)[:, cols]
        hi = rat(40 + 8 * (n % NHI), BLOCK)[:, cols]
        loaded = (slot_sem[n % NSLOT], 16 * (n // NSLOT + 1))
        free = [block_done[n - NHI]] if n >= NHI else []
        th = act.act(hi, w, ACT.Copy, after=[loaded] + free)
        on_pool = q < pool_quarters[0]
        tl = (pool if on_pool else dve).tt(lo, w, hi, ALU.subtract, after=[th])
        block_split.setdefault(n, {})["pool" if on_pool else "dve"] = tl
        block_split[n]["act"] = th

    def split_ahead(upto):
        while split[0] < min(upto, 4 * limit[0]):
            split_quarter()

    def take_block():
        n = used[0]
        used[0] += 1
        split_ahead(4 * (n + NHI - 1))
        width = PLAN[n][2]
        pe.wait(*block_split.pop(n).values())
        return tuple(v.rearrange("p (k n) -> p k n", n=width)
                     for v in (rat(40 + 8 * (n % NHI), BLOCK), rat(8 * (n % NSLOT), BLOCK)))

    def split_goal(sixteenths):
        return 4 * (used[0] + NHI - 2) + sixteenths // 4 + 1

    def release_block(last_use):
        block_done[used[0] - 1] = last_use
        if started[0] < limit[0]:
            sp.wait(last_use)
            start_load()

    bank_free = {b: [] for b in range(8)}

    def use_bank(b):
        pe.wait(*bank_free[b])
        bank_free[b] = []

    lin_bank = [0]

    def next_bank():
        b = lin_bank[0] % 3
        lin_bank[0] += 1
        use_bank(b)
        return b

    class Halves:

        def __init__(self, hi_kb, lo_kb, n, ready=None):
            self.hi, self.lo, self.n = rat(hi_kb, n, T), rat(lo_kb, n, T), n
            self.f32 = at(lo_kb, n, T)
            self.ready = ready or [[] for _ in range(n)]

        def split(self, c, m, after, lo_engine=None):
            th = act.act(self.hi[:, c:c + m], self.f32[:, c:c + m], ACT.Copy, after=after)
            tl = (lo_engine or dve).tt(self.lo[:, c:c + m], self.f32[:, c:c + m], self.hi[:, c:c + m],
                                       ALU.subtract, after=[th])
            for i in range(m):
                self.ready[c + i] = [th, tl]
            return tl

    def passes(w, x, out_, wk, xk, start, stop, weights_move=False):
        pairs = ((w[0], x[0]), (w[0], x[1]), (w[1], x[0])) if not weights_move else \
            ((w[0], x[0]), (w[1], x[0]), (w[0], x[1]))
        for i, (a, b) in enumerate(pairs):
            lhs, rhs = (wk(a), xk(b)) if not weights_move else (xk(b), wk(a))
            last = pe.mm(out_, lhs, rhs, start=start and i == 0, stop=stop and i == 2)
        return last

    def linear(n_chunks, src, evacuate, step=None, every=4, tail=None):
        kn = src.n
        per_block = BLOCK // kn // P
        count = 0
        for f in range(n_chunks):
            if f % per_block == 0:
                w = take_block()
            if f % 2 == 0:
                b = next_bank()
                acc = ps[:, b, :].rearrange("p (h t) -> p h t", h=2)
            col = (f % per_block) * P
            for k in range(kn):
                if k % 4 == 0:
                    split_ahead(split_goal(f % per_block * kn + k))
                pe.wait(*src.ready[k])
                last = passes(w, (src.hi, src.lo), acc[:, f % 2, :], lambda a: a[:, k, col:col + P],
                              lambda x_: x_[:, k, :], k == 0, k == kn - 1 and tail is None)
                count += 1
                if k == kn - 1:
                    if tail is not None:
                        last = tail(f, acc[:, f % 2, :])
                    done = pe.mark(last)
                if step is not None and count % every == 0:
                    step()
            if f % per_block == per_block - 1:
                release_block(done)
            if f % 2 == 1:
                bank_free[b] = evacuate(f // 2, acc, done)

    class InFlight:

        def __init__(self):
            self.gens, self.turn = [], 0

        def start(self, gen):
            while len(self.gens) >= 2:
                n = len(self.gens)
                self.turn = 0
                self.step()
                if len(self.gens) == n and n == 2:
                    self.turn = 0
            self.gens.append(gen)

        def step(self):
            if self.gens:
                i = self.turn % len(self.gens)
                self.turn += 1
                try:
                    next(self.gens[i])
                except StopIteration:
                    self.gens.pop(i)
                    self.turn = 0

        def finish(self):
            while self.gens:
                self.step()

    def runner(gen):
        state = [True]

        def step():
            if state[0]:
                try:
                    next(gen)
                except StopIteration:
                    state[0] = False

        def finish():
            while state[0]:
                step()
        return step, finish

    class SumSquares:

        def __init__(self, src, sq):
            self.src, self.sq, self.pending, self.n, self.done = src, sq, [], 0, None

        def add(self, c, after):
            t = act.act(self.sq[:, c:c + 2], self.src[:, c:c + 2], ACT.Square, after=after)
            self.pending.append((c, t))

        def flush(self, keep=0):
            while len(self.pending) > keep:
                c, t = self.pending.pop(0)
                if self.n == 0:
                    use_bank(3)
                pe.wait(t)
                for i in range(2):
                    last = pe.mm(ps[:, 3, 0:T], ones, self.sq[:, c + i, :], start=(self.n == 0),
                                 stop=(self.n == NCH - 1))
                    self.n += 1
                self.done = pe.mark(last)

    def inverse_rms(sums):
        sums.flush()
        root = sums.sq[:, 0, :]
        t = act.act(root, ps[:, 3, 0:T], ACT.Sqrt, after=[sums.done], scale=1.0 / D, bias=Pm("eps_rms"))
        bank_free[3] = [t]
        return root, dve.recip(root, root, after=[t])

    def rms_halves(src, ready, sums, gains, dst, dst_free):
        root, t = inverse_rms(sums)
        for c in range(NCH):
            t1 = dve.stt(dst.f32[:, c, :], src[:, c, :], Pm(gains, c), root, ALU.mult, ALU.mult,
                         after=[t] + ready + dst_free)
            if c % 4 == 3:
                dst.split(c - 3, 4, [t1] + dst_free, pool if c % 8 == 7 else dve)

    xT = at(96, NCH, T)
    x_tok = at(112, 2, D)
    x_src = x.rearrange("b (t p) d -> p (b t) d", p=P)
    identr = rat(195.5, P)
    t_const = small.start(nc.scalar, cst, consts)
    x_loads = [Loads(sem("x_loaded0")), Loads(sem("x_loaded1"))]
    t_xl = [x_loads[i].start(nc.scalar, x_tok[:, :, i * 1024:(i + 1) * 1024], x_src[:, :, i * 1024:(i + 1) * 1024])
            for i in range(2)]
    t_small = small.start(nc.scalar, par, params)
    for _ in range(NSLOT):
        start_load()

    def to_feature_major(tok_view, ready, dst, sums, after_evac, extra=None):
        for c2 in range(NCH // 2):
            pe.wait(*ready[c2 // 4])
            b = next_bank()
            acc = ps[:, b, :].rearrange("p (h t) -> p h t", h=2)
            for half in range(2):
                c = 2 * c2 + half
                for t in range(2):
                    last = pe.mm(acc[:, half, t * P:(t + 1) * P], tok_view[:, t, c * P:(c + 1) * P], ident)
            done = pe.mark(last)
            d = dst[:, 2 * c2:2 * c2 + 2, :]
            if extra is None:
                t = dve.copy(d, acc, after=[done])
            else:
                t = dve.tt(d, acc, extra[:, 2 * c2:2 * c2 + 2, :], ALU.add, after=[done])
            bank_free[b] = [t]
            sums.add(2 * c2, [t] + after_evac)
            sums.flush(keep=1)
        return t

    pe.wait(t_const)
    sums = SumSquares(xT, at(128, NCH, T))
    t_x = to_feature_major(x_tok, [[t_xl[0]], [t_xl[1]]], xT, sums, [])
    t_idr = act.act(identr, ident, ACT.Copy, after=[t_const])
    act.wait(t_small)
    dve.wait(t_small)
    hT = Halves(64, 80, NCH)
    rms_halves(xT, [t_x], sums, "norm_mix", hT, [])

    NJ = 32
    co = at(181, 10, NJ)
    (dt_, r_, th, n_, s_, c_, k_re, k_im, m2, tmp) = (co[:, i, :] for i in range(10))
    a_re, a_im = Pm("a_re", 0, NJ), Pm("a_im", 0, NJ)
    t = act.act(dt_, Pm("log_dt", 0, NJ), ACT.Exp, after=[t_small])
    t1 = dve.tt(r_, a_re, dt_, ALU.mult, after=[t])
    t_r = act.act(r_, r_, ACT.Exp, after=[t1])
    t = dve.tt(th, a_im, dt_, ALU.mult, after=[t1])
    t = dve.ts(n_, th, 1.0 / (2 * np.pi), ALU.mult, ROUND, ALU.add, after=[t])
    t = dve.ts(n_, n_, -ROUND, ALU.add, after=[t])
    for part in TWO_PI:
        t = dve.stt(th, n_, -part, th, ALU.mult, ALU.add, after=[t])
    t = dve.ts(th, th, PI_SAFE, ALU.min, -PI_SAFE, ALU.max, after=[t])
    t_s = act.act(s_, th, ACT.Sin, after=[t])
    t = act.act(c_, th, ACT.Sin, after=[t], scale=0.5)
    t = dve.tt(c_, c_, c_, ALU.mult, after=[t])
    t_cos = dve.ts(c_, c_, -2.0, ALU.mult, 1.0, ALU.add, after=[t])
    t = dve.tt(tmp, r_, c_, ALU.mult, after=[t_cos, t_r])
    t_a = dve.ts(tmp, tmp, -1.0, ALU.add, after=[t])
    t_b = dve.tt(n_, r_, s_, ALU.mult, after=[t_s])
    t = dve.tt(m2, a_re, a_re, ALU.mult)
    t1 = dve.tt(dt_, a_im, a_im, ALU.mult, after=[t_b])
    t = dve.tt(m2, m2, dt_, ALU.add, after=[t1])
    t_m = dve.recip(m2, m2, after=[t])
    t1 = dve.tt(k_re, tmp, a_re, ALU.mult, after=[t_a])
    t = dve.tt(dt_, n_, a_im, ALU.mult, after=[t_m])
    t = dve.tt(k_re, k_re, dt_, ALU.add, after=[t])
    t_k1 = dve.tt(k_re, k_re, m2, ALU.mult, after=[t])
    t1 = dve.tt(k_im, n_, a_re, ALU.mult)
    t = dve.tt(dt_, tmp, a_im, ALU.mult, after=[t_k1])
    t = dve.tt(k_im, k_im, dt_, ALU.subtract, after=[t])
    t_k = dve.tt(k_im, k_im, m2, ALU.mult, after=[t])
    uT = at(96, 8, T)
    glu = at(104, 8, T + TAPS - 1)
    conv = Halves(185, 113, 8)
    conv32 = conv.f32
    gates = at(121, 32, T)
    sig, mean = at(161, 2, T), at(163, T)
    stage_free = fence()
    pool_quarters[0] = 2

    def evac_u(i, acc, done):
        return [act.act(uT[:, 2 * i:2 * i + 2, :], acc, ACT.Copy, after=[done] + stage_free)]

    linear(8, hT, evac_u)
    t_u = (act.sem, act.n)
    t_pad = dve.memset(glu[:, :, 0:TAPS - 1], 0.0, after=stage_free)
    glu_ready = []
    value = [None]

    def evac_value(i, acc, done):
        value[0] = (acc, done, (lin_bank[0] - 1) % 3)
        return []

    def evac_glu(i, acc, done):
        q = len(glu_ready)
        t = act.act(sig, acc, ACT.Sigmoid, after=[done] + glu_ready[-1:] + stage_free)
        glu_ready.append(dve.tt(glu[:, 2 * q:2 * q + 2, TAPS - 1:], value[0][0], sig, ALU.mult,
                                after=[t, value[0][1]] + stage_free))
        bank_free[value[0][2]] = glu_ready[-1:]
        return [t]

    def convolution():
        for c in range(8):
            while len(glu_ready) <= c // 2:
                yield
            for k in range(TAPS):
                w = Pm("dw_w", k * 8 + c)
                src = glu[:, c, k:k + T]
                if k == 0:
                    t = dve.ts(conv32[:, c, :], src, w, ALU.mult, Pm("dw_b", c), ALU.add,
                               after=[glu_ready[c // 2], t_pad] + stage_free)
                else:
                    t = dve.stt(conv32[:, c, :], src, w, conv32[:, c, :], ALU.mult, ALU.add, after=[t])
                if k % 8 == 7:
                    yield
        use_bank(3)
        pe.wait(t)
        for c in range(8):
            last = pe.mm(ps[:, 3, 0:T], ones, conv32[:, c, :], start=(c == 0), stop=(c == 7))
        tm = pe.mark(last)
        tm = act.act(mean, ps[:, 3, 0:T], ACT.Copy, after=[tm], scale=1.0 / 1024)
        bank_free[3] = [tm]
        t = dve.tt(conv32, conv32, wide(mean.unsqueeze(1), [P, 8, T]), ALU.subtract, after=[tm])
        yield
        squares = at(104, 8, T)
        t = act.act(squares, conv32, ACT.Square, after=[t])
        yield
        use_bank(3)
        pe.wait(t)
        for c in range(8):
            last = pe.mm(ps[:, 3, 0:T], ones, squares[:, c, :], start=(c == 0), stop=(c == 7))
        t = pe.mark(last)
        squares_read[0] = t
        t = act.act(mean, ps[:, 3, 0:T], ACT.Sqrt, after=[t], scale=1.0 / 1024, bias=Pm("eps_ln"))
        bank_free[3] = [t]
        t = dve.recip(mean, mean, after=[t])
        for c in range(8):
            t1 = dve.stt(conv32[:, c, :], conv32[:, c, :], Pm("ln_g", c), mean, ALU.mult, ALU.mult, after=[t])
            t1 = act.act(conv32[:, c, :], conv32[:, c, :], ACT.Silu, after=[t1], bias=Pm("ln_b", c))
            if c % 4 == 3:
                conv.split(c - 3, 4, [t1])
                yield

    squares_read = [None]

    phase = [at(153, 2, 4, T), at(104, 2, 4, T)]
    work = [at(161, 2, 4, T), at(169, 2, 4, T)]
    phase_tmp = at(177, 2, 4, P)
    bc_sb = [at(193, 2, 2, P), at(182.25, 2, 2, P)]
    cnew = [at(184.25, 4, 32), at(195, 4, 32)]
    bc_loads = [Loads(sem("ssm_weights0")), Loads(sem("ssm_weights1"))]
    ssm_done = [None]

    phase_ready = [None, None]

    def fill_phase(c, free):
        E = phase[c % 2]
        pool.copy(E[:, 0, :, 0:1], c_[:, 4 * c:4 * c + 4].unsqueeze(2), after=[t_cos, t_s] + free)
        t = pool.copy(E[:, 1, :, 0:1], s_[:, 4 * c:4 * c + 4].unsqueeze(2))
        n = 1
        while n < T:
            for plane in range(2):
                pool.tt(E[:, plane, :, n:2 * n], E[:, plane, :, 0:n],
                        wide(E[:, 0, :, n - 1:n], [P, 4, n]), ALU.mult, after=[t])
            for plane in range(2):
                tq = pool.tt(phase_tmp[:, plane, :, 0:n], E[:, plane, :, 0:n],
                             wide(E[:, 1, :, n - 1:n], [P, 4, n]), ALU.mult, after=[t])
            pool.tt(E[:, 0, :, n:2 * n], E[:, 0, :, n:2 * n], phase_tmp[:, 1, :, 0:n], ALU.subtract, after=[tq])
            t = pool.tt(E[:, 1, :, n:2 * n], E[:, 1, :, n:2 * n], phase_tmp[:, 0, :, 0:n], ALU.add)
            n *= 2
            yield
        phase_ready[c % 2] = t

    def load_bc(c):
        act.wait((pe.sem, pe.n), (dve.sem, dve.n))
        return bc_loads[c % 2].start(nc.scalar, bc_sb[c % 2], bcT[c])

    def ssm():
        y_read = []
        bank4 = ps[:, 4:8, :].rearrange("p i (q t) -> p q i t", q=2)
        t_bt = [load_bc(0), None]
        last_out = [squares_read[0]]
        yield
        fill = iter(())
        for c in range(8):
            for _ in fill:
                pass
            if c + 1 < 8:
                t_bt[(c + 1) % 2] = load_bc(c + 1)
                fill = fill_phase(c + 1, last_out + [squares_read[0]])
            bT, cT = bc_sb[c % 2][:, 0], bc_sb[c % 2][:, 1].rearrange("p q (i n) -> p q i n", i=4)
            for b in range(4, 8):
                use_bank(b)
            pe.wait(t_bt[c % 2], t_u)
            for plane in range(2):
                for i in range(4):
                    rows = slice(32 * i, 32 * i + 32)
                    last = pe.mm(bank4[:, plane, i, :], bT[rows, plane, :], uT[rows, c, :])
            t_bu = pe.mark(last)
            yield
            kr, ki = (wide(k[:, 4 * c:4 * c + 4].unsqueeze(2), [P, 4, 32]) for k in (k_re, k_im))
            t1 = dve.tt(cnew[0], cT[:, 0], kr, ALU.mult, after=[t_bt[c % 2], t_k] + y_read[-1:])
            t2 = dve.tt(cnew[1], cT[:, 1], ki, ALU.mult)
            t3 = dve.tt(cnew[0], cnew[0], cnew[1], ALU.subtract, after=[t1, t2])
            t4 = dve.tt(cnew[1], cT[:, 0], ki, ALU.mult, after=[t3])
            t5 = dve.tt(cT[:, 0], cT[:, 1], kr, ALU.mult, after=[t4])
            t_cw = dve.stt(cnew[1], cnew[1], -1.0, cT[:, 0], ALU.mult, ALU.subtract, after=[t5])
            yield
            E = phase[c % 2]
            A, B = work[c % 2], work[(c + 1) % 2]
            cosb = wide(E[:, 0].unsqueeze(1), [P, 2, 4, T])
            sinb = wide(E[:, 1].unsqueeze(1), [P, 2, 4, T])
            t = dve.tt(A, bank4, cosb, ALU.mult, after=[t_bu, phase_ready[c % 2]])
            t = dve.tt(B, bank4, sinb, ALU.mult, after=y_read[-1:])
            for b in range(4, 8):
                bank_free[b] = [t]
            next(fill, None)
            yield
            t1 = dve.tt(A[:, 0], A[:, 0], B[:, 1], ALU.add, after=[t])
            t2 = dve.tt(A[:, 1], A[:, 1], B[:, 0], ALU.subtract)
            next(fill, None)
            yield
            for plane in range(2):
                for i in range(4):
                    dve.wait(t1, t2)
                    t = dve.mark(nc.vector.tensor_tensor_scan(
                        B[:, plane, i, :], wide(r_[:, 4 * c + i:4 * c + i + 1], [P, T]), A[:, plane, i, :], 0.0,
                        ALU.mult, ALU.add))
                next(fill, None)
                yield
            t1 = dve.tt(A, B, cosb, ALU.mult, after=[t])
            t2 = dve.tt(B, B, sinb, ALU.mult, after=[t1])
            last_out[0] = t2
            next(fill, None)
            yield
            t1 = dve.tt(A[:, 0], A[:, 0], B[:, 1], ALU.subtract, after=[t2])
            t2 = dve.tt(A[:, 1], A[:, 1], B[:, 0], ALU.add)
            next(fill, None)
            yield
            use_bank(3)
            pe.wait(t1, t2, t_cw)
            for plane in range(2):
                for i in range(4):
                    rows = slice(32 * i, 32 * i + 32)
                    last = pe.mm(ps[rows, 3, 0:T], cnew[plane][:, i, :], A[:, plane, i, :],
                                 start=(plane == 0), stop=(plane == 1))
            t = pe.mark(last)
            y_read.append(t)
            t = dve.stt(uT[:, c, :], uT[:, c, :], Pm("ssm_d", c), ps[:, 3, 0:T], ALU.mult, ALU.add, after=[t])
            bank_free[3] = [t]
            ssm_done[0] = act.act(uT[:, c, :], uT[:, c, :], ACT.Gelu_apprx_tanh, after=[t])
            next(fill, None)
            yield

    for _ in fill_phase(0, stage_free):
        pass

    def branches():
        yield from convolution()
        yield from ssm()

    def evac_gates(first):
        def evac(i, acc, done):
            for half in range(2):
                f = first + 2 * i + half
                t = act.act(gates[:, f, :], acc[:, half, :], ACT.Sigmoid, after=[done] + stage_free,
                            bias=Pm("b_gate", f))
            return [t]
        return evac

    def evac_conv(q):
        def evac(i, acc, done):
            f = 4 * q + 2 * i
            return [dve.tt(gates[:, f:f + 2, :], acc, gates[:, f:f + 2, :], ALU.mult, after=[done, gate_done[0]])]
        return evac

    gate_done = [None]
    step, finish = runner(branches())
    for q in range(4):
        linear(2, hT, evac_value, step, every=8)
        linear(2, hT, evac_glu, step, every=8)
    linear(16, hT, evac_gates(NCH), step, every=8)
    while not conv.ready[7]:
        step()
    for q in range(4):
        linear(4, hT, evac_gates(4 * q), step, every=8)
        gate_done[0] = (act.sem, act.n)
        linear(4, conv, evac_conv(q), step, every=8)
    finish()
    hT_read = fence()
    zT = Halves(104, 96, 8)
    zT.split(0, 4, [ssm_done[0]] + hT_read)
    zT.split(4, 4, [ssm_done[0]] + hT_read)

    pool_quarters[0] = 1
    x_tok2 = at(153, 2, D)
    act.wait(*hT_read)
    t_x2 = small.start(nc.scalar, x_tok2, x_src)
    merged = Halves(64, 121, NCH)
    side, sg = at(169, 2, 2, T), at(173, 2, 2, T)
    side_free = [hT_read, hT_read]
    side_ready = [None, None]

    def evac_val(q):
        def evac(i, acc, done):
            f = 4 * q + 2 * i
            side_ready[i] = dve.tt(side[:, i], acc, gates[:, NCH + f:NCH + f + 2, :], ALU.mult,
                                   after=[done] + side_free[i])
            return [side_ready[i]]
        return evac

    def evac_wgate(q):
        def evac(i, acc, done):
            f = 4 * q + 2 * i
            t = act.act(sg[:, i], acc, ACT.Sigmoid, after=[done] + side_free[i])
            t2 = dve.tt(side[:, i], side[:, i], sg[:, i], ALU.mult, after=[t, side_ready[i]])
            t3 = dve.tt(gates[:, f:f + 2, :], gates[:, f:f + 2, :], side[:, i], ALU.add, after=[t2])
            side_free[i] = [t3]
            merged.split(f, 2, [t3])
            return [t]
        return evac

    for q in range(4):
        linear(4, zT, evac_val(q))
        linear(4, zT, evac_wgate(q))

    x_free = fence()
    sums = SumSquares(xT, at(177, NCH, T))

    def add_x(tok_view):
        def tail(f, acc):
            for t in range(2):
                last = pe.mm(acc[:, t * P:(t + 1) * P], tok_view[:, t, f * P:(f + 1) * P], ident,
                             start=False, stop=(t == 1))
            return last
        return tail

    def evac_x1(i, acc, done):
        t = act.act(xT[:, 2 * i:2 * i + 2, :], acc, ACT.Copy, after=[done] + x_free)
        sums.add(2 * i, [t])
        sums.flush(keep=1)
        return [t]

    pe.wait(t_x2)
    linear(16, merged, evac_x1, tail=add_x(x_tok2))
    t_x1 = (act.sem, act.n)
    hT = Halves(64, 80, NCH)
    rms_halves(xT, [t_x1], sums, "norm_ffn", hT, fence())

    HC, NK, TOPK, HEADS = 16, 128, 16, 8
    peer_free = fence()
    qT = at(112, HC, T)
    keys = at(128, HC, NK)
    h_tok = at(136, 2, D)
    NBUF, GRP = 4, 4
    u_buf = [at(152 + 8 * i, D) for i in range(NBUF)]
    v_buf = [at(8 * i, D) for i in range(NBUF)]
    diag = at(64, 2, GRP, P)
    peer_tok = at(112, 2, D)
    scores = at(184, 2, NK)
    cand = at(185, TOPK * TOPK)
    onehot = at(186, TOPK, TOPK)
    top = at(187, 2, TOPK)
    top_i = at(187.25, 2, TOPK).bitcast(U32)
    top_if = at(187.5, 2, TOPK)
    best = at(187.75, TOPK)
    pos = at(188, TOPK).bitcast(U32)
    half_pos = at(188.25, TOPK).bitcast(U32)
    half_f, e_part = at(188.5, TOPK), at(188.75, TOPK)
    gate_sum = at(189, 2)
    expert = [at(190 + t / 2, HEADS * TOPK).bitcast(U32) for t in range(2)]
    route = [at(191 + t / 2, HEADS * TOPK) for t in range(2)]
    dots = [at(192 + t / 2, HEADS * TOPK) for t in range(2)]
    coef = [at(193 + t / 2, HEADS * TOPK) for t in range(2)]
    act.wait(*peer_free)
    t_keys = small.start(nc.scalar, keys, keysT)
    q_ready = []

    def evac_q(i, acc, done):
        t = act.act(qT[:, 2 * i:2 * i + 2, :], acc, ACT.Copy, after=[done] + peer_free)
        q_ready.append(t)
        return [t]

    def top16(values, vals_out, idx_out, ready):
        t = ready
        for r in range(2):
            o, ix = vals_out[:, 8 * r:8 * r + 8], idx_out[:, 8 * r:8 * r + 8]
            dve.wait(*t)
            t1 = dve.mark(nc.vector.max(out=o, in_=values))
            dve.wait(t1)
            t = [dve.mark(nc.vector.max_index(out=ix, in_max=o, in_values=values))]
            if r == 0:
                dve.wait(*t)
                t = [dve.mark(nc.vector.match_replace(out=values, in_to_replace=o, in_values=values,
                                                      imm_value=NEG))]
        return t[0]

    routed = {}
    scores_read = [peer_free]

    def routing(t, h):
        pe.wait(q_ready[h], t_keys)
        use_bank(3)
        for c in range(2):
            last = pe.mm(ps[:, 3, c * P:(c + 1) * P], qT[:, 2 * h + c, t * P:(t + 1) * P], keys[:, 2 * h + c, :])
        done = pe.mark(last)
        ts_ = act.act(scores, ps[:, 3, 0:2 * P].rearrange("p (c n) -> p c n", c=2), ACT.Copy,
                      after=[done] + scores_read[0])
        bank_free[3] = [ts_]
        yield
        for c in range(2):
            tk = top16(scores[:, c, :], top[:, c, :], top_i[:, c, :], [ts_] + peer_free)
        scores_read[0] = [tk]
        yield
        sq = [P, TOPK, TOPK]
        tk = dve.tt(cand.rearrange("p (i j) -> p i j", i=TOPK), wide(top[:, 0].unsqueeze(2), sq),
                    wide(top[:, 1].unsqueeze(1), sq), ALU.add, after=[tk])
        tk = top16(cand, best, pos, [tk])
        prev = dve.copy(top_if, top_i, after=[tk])
        for half, (op, arg) in enumerate(((ALU.logical_shift_right, 4), (ALU.bitwise_and, 15))):
            t1 = dve.ts(half_pos, pos, arg, op, after=[prev])
            dst = e_part if half == 0 else half_f
            t1 = dve.copy(dst, half_pos, after=[t1])
            t1 = dve.tt(onehot, wide(dst.unsqueeze(2), sq), wide(C("iota", 0, 16).unsqueeze(1), sq),
                        ALU.is_equal, after=[t1])
            t1 = dve.tt(onehot, onehot, wide(top_if[:, half].unsqueeze(1), sq), ALU.mult, after=[t1])
            dve.wait(t1)
            prev = dve.mark(nc.vector.tensor_reduce(dst, onehot, AX_X, ALU.add))
        te = dve.stt(e_part, e_part, float(NK), half_f, ALU.mult, ALU.add, after=[prev])
        hk = slice(TOPK * h, TOPK * (h + 1))
        te = dve.copy(expert[t][:, hk], e_part, after=[te])
        yield
        tb = dve.ts(gate_sum[:, 0:1], best[:, 0:1], -1.0, ALU.mult, after=[te])
        tb = act.act(best, best, ACT.Exp, after=[tb], bias=gate_sum[:, 0:1], accum_out=gate_sum[:, 1:2])
        tb = dve.recip(gate_sum[:, 1:2], gate_sum[:, 1:2], after=[tb])
        tb = dve.ts(route[t][:, hk], best, gate_sum[:, 1:2], ALU.mult, after=[tb])
        routed[t, h] = (te, tb)
        yield

    NSEL = HEADS * TOPK
    u_sem = [Loads(sem(f"u_rows{i}")) for i in range(NBUF)]
    v_sem = [Loads(sem(f"v_rows{i}")) for i in range(NBUF)]
    u_free = [peer_free] * NBUF

    def gather(buf, loads, table, idx, free, ready):
        pool.wait(*free, *ready)
        nc.gpsimd.indirect_dma_start(out=buf, out_offset=None, in_=table,
                                     in_offset=bass.IndirectOffsetOnAxis(ap=idx, axis=0)).then_inc(loads.sem, 16)
        loads.n += 16
        return (loads.sem, loads.n)

    diag_free = [[], []]
    groups = [(t, g) for t in range(2) for g in range(NSEL // GRP)]
    coef_ready = {}
    u_loaded = {}

    def u_gather(n):
        t, g = groups[n]
        for i in range(GRP):
            k = g * GRP + i
            u_loaded[n, i] = gather(u_buf[i], u_sem[i], u_tab, expert[t][:, k:k + 1], u_free[i],
                                    [routed[t, k // TOPK][0]])

    def u_group(n, gathered=False):
        t, g = groups[n]
        for i in range(GRP):
            k = g * GRP + i
            if not gathered:
                u_loaded[n, i] = gather(u_buf[i], u_sem[i], u_tab, expert[t][:, k:k + 1], u_free[i],
                                        [routed[t, k // TOPK][0]])
            dve.wait(u_loaded[n, i], t_htok)
            td = dve.mark(nc.vector.tensor_tensor_reduce(
                out=u_buf[i], in0=u_buf[i], in1=h_tok[:, t, :], scale=1.0, scalar=0.0, op0=ALU.mult,
                op1=ALU.add, accum_out=dots[t][:, k:k + 1]))
            u_free[i] = [td]
        ks = slice(g * GRP, (g + 1) * GRP)
        tg = act.act(coef[t][:, ks], dots[t][:, ks], ACT.Gelu_apprx_tanh, after=[td])
        tc = dve.tt(coef[t][:, ks], coef[t][:, ks], route[t][:, ks], ALU.mult, after=[tg, routed[t, g // 4][1]])
        for i in range(GRP):
            k = g * GRP + i
            tc2 = act.act(diag[:, n % 2, i, :], ident, ACT.Copy, after=[tc] + diag_free[n % 2] + hT_read,
                          scale=coef[t][:, k:k + 1])
        coef_ready[n] = tc2

    def v_group(n):
        t, g = groups[n]
        for i in range(GRP):
            k = g * GRP + i
            loaded = gather(v_buf[i], v_sem[i], v_tab, expert[t][:, k:k + 1], v_free[i], [])
            if g == 0 and i == 0:
                for b in range(4):
                    use_bank(4 + b)
            pe.wait(loaded, coef_ready[n])
            for b in range(4):
                last = pe.mm(ps[:, 4 + b, :], diag[:, n % 2, i, :], v_buf[i][:, 512 * b:512 * (b + 1)],
                             start=(k == 0), stop=(k == NSEL - 1))
            done = pe.mark(last)
            v_free[i] = [done]
        diag_free[n % 2] = [done]
        if g == NSEL // GRP - 1:
            for b in range(4):
                te = act.act(peer_tok[:, t, 512 * b:512 * (b + 1)], ps[:, 4 + b, :], ACT.Copy,
                             after=[done, qT_read[0]])
                bank_free[4 + b] = [te]
            return te
        return None

    def h_token_major():
        for t in range(2):
            for g in range(4):
                b = 4 + g
                use_bank(b)
                pe.wait(t_idr, *hT.ready[15], *hT.ready[3])
                for i in range(4):
                    for j, half in enumerate((hT.hi, hT.lo)):
                        last = pe.mm(ps[:, b, i * P:(i + 1) * P], half[:, 4 * g + i, t * P:(t + 1) * P], identr,
                                     start=(j == 0), stop=(j == 1))
                done = pe.mark(last)
                tt_ = act.act(h_tok[:, t, 512 * g:512 * (g + 1)], ps[:, b, :], ACT.Copy, after=[done] + peer_free)
                bank_free[b] = [tt_]
                yield
        htok_done.append(tt_)

    htok_done = []

    def early_routing():
        for h in range(HEADS):
            while len(q_ready) <= h:
                yield
            yield from routing(0, h)
            if h == 0:
                yield from h_token_major()

    step, finish = runner(early_routing())
    linear(16, hT, evac_q, step, every=4)
    while (0, 0) not in routed:
        step()
    finish()
    hT_read = fence()
    v_free = [hT_read] * NBUF
    t_htok = htok_done[0]
    qT_read = [None]

    def late_routing():
        for h in range(HEADS):
            yield from routing(1, h)
        qT_read[0] = (pe.sem, pe.n)

    step, finish = runner(late_routing())
    u_group(0)
    for n in range(len(groups)):
        step()
        step()
        if n == NSEL // GRP - 2:
            finish()
        if n + 1 < len(groups):
            u_group(n + 1)
        t_peer = v_group(n) or None
    limit[0] = len(PLAN)
    sp.wait(*fence())
    for _ in range(NSLOT):
        start_load()

    sums = SumSquares(xT, at(136, NCH, T))
    t_x = to_feature_major(peer_tok, [[t_peer], [t_peer]], xT, sums, fence(), extra=xT)
    root, t = inverse_rms(sums)
    sums2 = SumSquares(xT, at(153, NCH, T))
    for c in range(NCH):
        t_x = dve.stt(xT[:, c, :], xT[:, c, :], Pm("norm_final", c), root, ALU.mult, ALU.mult,
                      after=[t, t_x])
        if c % 2 == 1:
            sums2.add(c - 1, [t_x])
            sums2.flush(keep=1)
    hT = Halves(64, 80, NCH)
    rms_halves(xT, [t_x], sums2, "norm2a", hT, fence())

    NE = 4
    stage_free = fence()
    oT = Halves(64, 112, NCH)
    o32 = oT.f32
    zg = [at(128 + 2 * i, 2, T) for i in range(3)]
    qkv = [at(134, 6, T), at(140, 6, T)]
    raw = [at(146, 2, T + 3), at(148.25, 2, T + 3)]
    core_mem = [150.5, 171.5]
    per_tok = at(192.5, 8, NH, 2)
    (g_, gc_, beta_, eg_, dk_, nbe_, gx_, gy_) = (per_tok[:, i] for i in range(8))
    neg_a = at(193.75, NH)
    small_w = at(134, NCH, 32)
    small_hi = rat(136, NCH, 32)
    small_lo = rat(134, NCH, 32)

    act.wait(*stage_free)
    t_sw = small.start(nc.scalar, small_w, a_small)
    th = act.act(small_hi, small_w, ACT.Copy, after=[t_sw])
    tl = dve.tt(small_lo, small_w, small_hi, ALU.subtract, after=[th])
    use_bank(4)
    pe.wait(th, tl)
    for t in range(2):
        for k in range(NCH):
            pe.wait(*hT.ready[k])
            last = passes((small_hi, small_lo), (hT.hi, hT.lo), ps[:, 4, 32 * t:32 * t + 32],
                          lambda a: a[:, k, :], lambda x_: x_[:, k, t * P:(t + 1) * P], k == 0, k == NCH - 1,
                          weights_move=True)
    done = pe.mark(last)
    ab = ps[:, 4, 0:64].rearrange("p (t s h) -> p h t s", t=2, s=2)
    bias_b = wide(Pm("dt_bias", 0, NH).unsqueeze(2), [P, NH, 2])
    t1 = dve.tt(gx_, ab[:, :, :, 0], bias_b, ALU.add, after=[done] + stage_free)
    t2 = act.act(beta_, ab[:, :, :, 1], ACT.Sigmoid, after=[t1])
    bank_free[4] = [t1, t2]
    t_beta = t2

    def decays():
        t = dve.stt(gy_, gx_, -1.0, gx_, ALU.mult, ALU.min, after=[t1])
        t = act.act(gy_, gy_, ACT.Exp, after=[t])
        t = dve.ts(gy_, gy_, 1.0, ALU.add, after=[t])
        t = act.act(gy_, gy_, ACT.Ln, after=[t])
        t = dve.stt(gx_, gx_, 0.0, gy_, ALU.max, ALU.add, after=[t])
        ta = act.act(neg_a, Pm("a_log", 0, NH), ACT.Exp, after=stage_free)
        ta = dve.ts(neg_a, neg_a, -1.0, ALU.mult, after=[ta])
        t_g = dve.tt(g_, gx_, wide(neg_a.unsqueeze(2), [P, NH, 2]), ALU.mult, after=[t, ta])
        yield
        use_bank(4)
        pe.wait(t_g)
        gflat = g_.rearrange("p h t -> p (h t)")
        pe.mm(ps[:, 4, 0:32], upto, gflat)
        done = pe.mark(pe.mm(ps[:, 4, 32:64], ones, gflat))
        gcf = gc_.rearrange("p h t -> p (h t)")
        t_gc = dve.copy(gcf, ps[:, 4, 0:32], after=[done])
        t = dve.tt(dk_.rearrange("p h t -> p (h t)"), ps[:, 4, 32:64], gcf, ALU.subtract, after=[t_gc])
        bank_free[4] = [t]
        t_dk = act.act(dk_, dk_, ACT.Exp, after=[t])
        t = act.act(eg_, gc_, ACT.Exp, after=[t_gc])
        t_nb = dve.stt(nbe_, eg_, -1.0, beta_, ALU.mult, ALU.mult, after=[t, t_beta])
        decay_tokens.extend((t_g, t_gc, t_dk, t_nb))
        yield

    decay_tokens = []

    z_ready = {}
    core_last = []

    def evac_z(p):
        def evac(i, acc, done):
            z_ready[p] = act.act(zg[p % 3], acc, ACT.Silu, after=[done] + (core_last[p - 3:p - 2] or stage_free))
            return [z_ready[p]]
        return evac

    for r in raw:
        t_pad = dve.memset(r[:, :, 0:3], 0.0, after=stage_free)
    small_free = [(pe.sem, pe.n)]
    core_read = [stage_free + small_free, stage_free + small_free]
    raw_free = [stage_free, stage_free]
    qkv_ready = [[], []]

    def evac_qkv(p, part):
        def evac(i, acc, done):
            r = raw[part % 2]
            tr = act.act(r[:, :, 3:], acc, ACT.Copy, after=[done, t_pad] + raw_free[part % 2])
            for hh in range(2):
                f = part * 16 + 2 * p + hh
                d = qkv[p % 2][:, 2 * part + hh, :]
                t = dve.ts(d, r[:, hh, 0:T], Pm("qkv_w", f), ALU.mult, after=[tr] + core_read[p % 2])
                for k in range(1, 4):
                    t = dve.stt(d, r[:, hh, k:k + T], Pm("qkv_w", 48 * k + f), d, ALU.mult, ALU.add, after=[t])
                raw_free[part % 2] = [t]
                qkv_ready[p % 2] = [act.act(d, d, ACT.Silu, after=[t])]
            return [tr]
        return evac

    def bank_e(b):
        return ps[:, b, :].rearrange("p (e n) -> p e n", e=NE)

    def each(b, lhsT, rhs, es=range(NE)):
        for e in es:
            last = pe.mm(bank_e(b)[:, e, :], lhsT(e), rhs(e))
        return pe.mark(last)

    norm_done = [[]]

    def rms_pair(src, n, squares, scale, eps, ready, banks):
        t = act.act(squares, src, ACT.Square, after=ready)
        for j in range(n // 2):
            use_bank(banks[j])
            pe.wait(t)
            last = pe.mm(ps[:, banks[j], :], ones, squares[:, 2 * j:2 * j + 2, :])
            tp = pe.mark(last)
            ta = act.act(squares[:, 2 * j:2 * j + 2, :], ps[:, banks[j], :].rearrange("p (a t) -> p a t", a=2),
                         ACT.Sqrt, after=[tp], scale=scale, bias=eps)
            bank_free[banks[j]] = [ta]
        return dve.recip(squares, squares, after=[ta])

    def delta_core(p):
        src = qkv[p % 2]
        ready = qkv_ready[p % 2]
        hs = slice(2 * p, 2 * p + 2)
        prev = core_last[p - 2:p - 1] if p >= 2 else stage_free
        b0, b1 = (3, 4) if p % 2 == 0 else (5, 6)
        at0 = core_mem[p % 2]
        (E_, A_, Am, X_, Z_, QK, VB) = (at(at0 + 2 * i, NE, P) for i in range(7))
        Y_, KB_T = E_, VB
        sqb = at(at0, 4, T)
        (WK, V0, S_, WN, QD, KD, V1) = (at(at0 + 14 + i, 2, P) for i in range(7))
        qk4 = src[:, 0:4, :]
        t_r = rms_pair(qk4, 4, sqb, 1.0, Pm("eps_rms"), ready + prev, (b0, b1))
        yield
        t_qn = dve.stt(src[:, 0:2], src[:, 0:2], float(P) ** -0.5, sqb[:, 0:2], ALU.mult, ALU.mult, after=[t_r])
        t_kn = dve.tt(src[:, 2:4], src[:, 2:4], sqb[:, 2:4], ALU.mult, after=[t_r])

        def tile(a):
            return lambda e: src[:, 2 * a + e // 2, (e % 2) * P:(e % 2 + 1) * P]

        q_, k_, v_ = tile(0), tile(1), tile(2)

        def col(v):
            return lambda e: wide(v[:, 2 * p + e // 2, e % 2:e % 2 + 1], [P, P])

        yield
        use_bank(b0)
        pe.wait(t_beta, t_g)
        tb = each(b0, col(beta_), lambda e: ident)
        use_bank(b1)
        tg = each(b1, col(g_), lambda e: upto)
        t_kb = dve.tt(KB_T, src[:, 2:4].rearrange("p h (t n) -> p (h t) n", t=2), bank_e(b0), ALU.mult,
                      after=[tb, t_kn] + prev)
        bank_free[b0] = [t_kb]
        for e in range(NE):
            td = dve.ts(E_[:, e, :], bank_e(b1)[:, e, :], gc_[:, 2 * p + e // 2, e % 2:e % 2 + 1], ALU.subtract,
                        0.0, ALU.min, after=[tg, t_gc, t_qn, t_kn])
        yield
        gc1 = bank_e(b1)[:, 1:4:2, :]
        qd2 = QD[:, 0:2, :]
        tq = act.act(qd2, gc1, ACT.Exp, after=[td] + prev)
        bank_free[b1] = [td, tq]
        td = act.act(E_, E_, ACT.Exp, after=[td])
        td = pool.tt(E_, E_, wide(upto.unsqueeze(1), [P, NE, P]), ALU.mult, after=[td])
        t_qd = dve.tt(qd2, qd2, src[:, 0:2, P:2 * P], ALU.mult, after=[tq, t_qn])
        use_bank(7)
        pe.wait(t_qn, t_kn)
        tp = each(7, k_, q_)
        t_qk = dve.tt(QK, E_, bank_e(7), ALU.mult, after=[tp, td] + prev)
        bank_free[7] = [t_qk]
        yield
        use_bank(b0)
        pe.wait(t_kb)
        tp = each(b0, k_, lambda e: KB_T[:, e, :])
        t_a = dve.tt(A_, E_, bank_e(b0), ALU.mult, after=[tp])
        bank_free[b0] = [t_a]
        level = lambda l: wide(C("level", l).unsqueeze(1), [P, NE, P])
        ti = pool.tt(Am, A_, level(0), ALU.mult, after=[t_a] + prev)
        t_z = dve.stt(Z_, Am, -1.0, wide(ident.unsqueeze(1), [P, NE, P]), ALU.mult, ALU.add, after=[ti])
        am_free = t_z
        yield
        use_bank(b1)
        tp = each(b1, k_, lambda e: ident)
        kt = bank_e(b1)
        dkb = wide(dk_[:, hs, 0:1], [P, 2, P])
        nbb = wide(nbe_[:, hs, 1:2], [P, 2, P])
        t_kd = dve.tt(KD, kt[:, 0:4:2, :], dkb, ALU.mult, after=[tp, t_dk] + prev)
        t_wk = dve.tt(WK[:, 0:2, :], kt[:, 1:4:2, :], nbb, ALU.mult, after=[t_nb])
        bank_free[b1] = [t_wk]
        use_bank(b0)
        pe.wait(*ready)
        tp = each(b0, v_, lambda e: ident)
        t_vb = dve.tt(VB, bank_e(b0), wide(beta_[:, hs, :].rearrange("p h t -> p (h t)").unsqueeze(2), [P, NE, P]),
                      ALU.mult, after=[tp])
        bank_free[b0] = [t_vb]
        core_read[p % 2] = [t_vb, t_qd, (pe.sem, pe.n)]
        yield
        use_bank(b1)
        pe.wait(t_z)
        tp = each(b1, lambda e: Z_[:, e, :], lambda e: ident)
        t_x = act.act(X_, bank_e(b1), ACT.Copy, after=[tp] + prev)
        bank_free[b1] = [t_x]
        for l in range(1, 7):
            tm = pool.tt(Am, A_, level(l), ALU.mult, after=[am_free])
            yield
            b2 = 1 << l

            def halves(v, s_):
                return v.rearrange("p (n s b) -> p n s b", s=2, b=b2)[:, :, s_, :]

            def halves_e(v, s_):
                return v.rearrange("p e (n s b) -> p e n s b", s=2, b=b2)[:, :, :, s_, :]

            def narrow(i):
                return ps[:, b1, i * 256:i * 256 + 256].rearrange("p (e n) -> p e n", e=NE)

            use_bank(b0)
            pe.wait(tm, t_x)
            tp = each(b0, lambda e: Am[:, e, :], lambda e: X_[:, e, :])
            am_free = tp
            ty = act.act(Y_, bank_e(b0), ACT.Copy, after=[tp, t_a])
            bank_free[b0] = [ty]
            yield
            pe.wait(ty, t_z)
            use_bank(b1)
            for e in range(NE):
                tz = pe.mm(narrow(0)[:, e, :], Y_[:, e, :], halves(Z_[:, e, :], 1))
            if l < 6:
                for e in range(NE):
                    tz = pe.mm(narrow(1)[:, e, :], Z_[:, e, :], halves(Y_[:, e, :], 0))
            tz = pe.mark(tz)
            zh = halves_e(Z_, 1)
            if l < 6:
                xh = halves_e(X_, 0)
                t_x = dve.tt(xh, xh, narrow(1).rearrange("p e (n b) -> p e n b", b=b2), ALU.subtract,
                             after=[tz])
            t_z = dve.tt(zh, zh, narrow(0).rearrange("p e (n b) -> p e n b", b=b2), ALU.subtract, after=[tz])
            bank_free[b1] = [t_z]
            yield
        use_bank(b0)
        pe.wait(t_z, t_vb)
        tp = each(b0, lambda e: Z_[:, e, :], lambda e: VB[:, e, :], es=(0, 2))
        t_v0 = act.act(V0[:, 0:2, :], bank_e(b0)[:, 0:4:2, :], ACT.Copy, after=[tp] + prev)
        bank_free[b0] = [t_v0]
        use_bank(b1)
        pe.wait(t_wk)
        tp = each(b1, lambda e: WK[:, e // 2, :], lambda e: Z_[:, e, :], es=(1, 3))
        t_wn = dve.copy(WN[:, 0:2, :], bank_e(b1)[:, 1:4:2, :], after=[tp] + prev)
        bank_free[b1] = [t_wn]
        yield
        use_bank(b0)
        pe.wait(t_v0, t_kd)
        tp = each(b0, lambda e: KD[:, e, :], lambda e: V0[:, e, :], es=(0, 1))
        t_s = act.act(S_[:, 0:2, :], bank_e(b0)[:, 0:2, :], ACT.Copy, after=[tp] + prev)
        bank_free[b0] = [t_s]
        yield
        use_bank(b1)
        pe.wait(t_s, t_wn)
        for hh in range(2):
            pe.mm(bank_e(b1)[:, hh, :], Z_[:, 2 * hh + 1, :], VB[:, 2 * hh + 1, :], start=True, stop=False)
            last = pe.mm(bank_e(b1)[:, hh, :], WN[:, hh, :], S_[:, hh, :], start=False, stop=True)
        tp = pe.mark(last)
        t_v1 = act.act(V1, bank_e(b1)[:, 0:2, :], ACT.Copy, after=[tp] + prev)
        bank_free[b1] = [t_v1]
        yield
        use_bank(b0)
        pe.wait(t_qk, t_v1, t_qd)
        for hh in range(2):
            pe.mm(bank_e(b0)[:, 2 * hh, :], V0[:, hh, :], QK[:, 2 * hh, :])
            pe.mm(bank_e(b0)[:, 2 * hh + 1, :], V1[:, hh, :], QK[:, 2 * hh + 1, :], start=True, stop=False)
            last = pe.mm(bank_e(b0)[:, 2 * hh + 1, :], S_[:, hh, :], QD[:, hh, :], start=False, stop=True)
        tp = pe.mark(last)
        o2 = ps[:, b0, :].rearrange("p (h t) -> p h t", h=2)
        dst = o32[:, 2 * p:2 * p + 2, :]
        t_o = act.act(dst, o2, ACT.Copy, after=[tp])
        bank_free[b0] = [t_o]
        yield
        t_r = rms_pair(dst, 2, sqb[:, 0:2], 1.0 / P, Pm("eps_rms"), [t_o], (b1,))
        t = dve.stt(dst, dst, Pm("onorm"), sqb[:, 0:2], ALU.mult, ALU.mult, after=[t_r])
        core_last.append(dve.tt(dst, dst, zg[p % 3], ALU.mult, after=[t, z_ready[p]]))
        yield

    cores = InFlight()
    step, finish = runner(decays())
    for p in range(NH // 2):
        for part in range(3):
            linear(2, hT, evac_qkv(p, part), step, every=5)
        linear(2, hT, evac_z(p), step, every=5)
        if p == 0:
            finish()
            t_g, t_gc, t_dk, t_nb = decay_tokens
        cores.start(delta_core(p))
        step = cores.step
    hT_read = (pe.sem, pe.n)
    cores.finish()
    for p in range(NH // 2):
        oT.split(2 * p, 2, [core_last[p], hT_read], pool if p % 2 else dve)

    def evac_res(i, acc, done):
        d = xT[:, 2 * i:2 * i + 2, :]
        t = dve.tt(d, d, acc, ALU.add, after=[done])
        sums.add(2 * i, [t] + sq_free)
        sums.flush(keep=1)
        return [t]

    sums = SumSquares(xT, at(145, NCH, T))
    sq_free = fence()

    linear(16, oT, evac_res)
    t_x = (dve.sem, dve.n)

    hT = Halves(64, 80, NCH)
    rms_halves(xT, [t_x], sums, "norm2b", hT, fence())
    stage_free = fence()
    oT = Halves(64, 112, NCH)
    o32 = oT.f32
    hankel = at(128, NH, T)
    zg = [at(144 + 2 * i, 2, T) for i in range(3)]
    v_tok = [at(150 + 2 * i, 2, 2 * P) for i in range(3)]
    qk = [at(156 + 4 * i, 4, T) for i in range(3)]
    core_mem = [168, 180]
    gain = at(194, 2)
    act.wait(*stage_free)
    rsrc = bass.AP(tensor=rel_rev.tensor, offset=1, ap=[[1, P], [513, NH], [1, T]])
    t_rel = small.start(nc.scalar, hankel, rsrc)
    t_gain = dve.ts(gain[:, 0:1], Pm("qnorm"), float(P) ** -0.5, ALU.mult, after=stage_free)
    t_gain = dve.copy(gain[:, 1:2], Pm("knorm"))

    def token_major(n_blocks, src, evacuate, step=None, every=4, tail=None):
        for blk in range(n_blocks):
            w = take_block()
            if blk % 2 == 0:
                b = next_bank()
            for t in range(2):
                acc = ps[:, b, 256 * (blk % 2) + P * t:256 * (blk % 2) + P * t + P]
                for k in range(NCH):
                    if k % 8 == 0:
                        split_ahead(split_goal(8 * t + k // 2))
                    pe.wait(*src.ready[k])
                    last = passes(w, (src.hi, src.lo), acc, lambda a: a[:, k, :],
                                  lambda x_: x_[:, k, t * P:(t + 1) * P], k == 0, k == NCH - 1 and tail is None,
                                  weights_move=True)
                    if k % every == every - 1 and k < NCH - 1 and step is not None:
                        step()
                if tail is not None:
                    last = tail(blk, t, acc)
            done = pe.mark(last)
            release_block(done)
            if blk % 2 == 1:
                bank_free[b] = evacuate(blk // 2, ps[:, b, :].rearrange("p (n t f) -> p t n f", n=2, t=2), done)

    z_ready.clear()
    core_last.clear()
    v_ready = {}

    def evac_v(p):
        def evac(i, acc, done):
            d = v_tok[p % 3].rearrange("p t (n f) -> p t n f", n=2)
            v_ready[p] = act.act(d, acc, ACT.Copy, after=[done] + (core_last[p - 3:p - 2] or stage_free))
            return [v_ready[p]]
        return evac

    qk_ready = {}

    def evac_qk(p, part):
        def evac(i, acc, done):
            t = act.act(qk[p % 3][:, 2 * part:2 * part + 2, :], acc, ACT.Copy,
                        after=[done] + (core_last[p - 3:p - 2] or stage_free))
            qk_ready[p] = [t]
            return [t]
        return evac

    def attention_core(p):
        src = qk[p % 3]
        prev = core_last[p - 2:p - 1] if p >= 2 else stage_free
        b0, b1 = (3, 4) if p % 2 == 0 else (5, 6)
        at0 = core_mem[p % 2]
        sqb, prob, probT = at(at0, 4, T), at(at0 + 4, 2, 384), at(at0 + 7, 2, 3, P)
        stat = at(at0 + 10, 2, 4)
        t_r = rms_pair(src, 4, sqb, 1.0 / P, Pm("eps_rms"), qk_ready[p] + prev, (b0, b1))
        yield
        for a in range(2):
            t_n = dve.stt(src[:, 2 * a:2 * a + 2], src[:, 2 * a:2 * a + 2], gain[:, a:a + 1],
                          sqb[:, 2 * a:2 * a + 2], ALU.mult, ALU.mult, after=[t_r, t_gain])
        yield
        pe.wait(t_n, t_rel)
        for hh in range(2):
            h = 2 * p + hh
            use_bank((b0, b1)[hh])
            s = ps[:, (b0, b1)[hh], 0:384]
            qh, kh = src[:, hh, :], src[:, 2 + hh, :]
            pe.mm(s[:, 0:P], qh[:, 0:P], kh[:, 0:P], start=True, stop=False)
            pe.mm(s[:, 0:P], C("flip"), hankel[:, h, P:2 * P], start=False, stop=True)
            pe.mm(s[:, P:384], qh[:, P:T], kh, start=True, stop=False)
            tp = pe.mark(pe.mm(s[:, P:384], C("flip"), hankel[:, h, :], start=False, stop=True))
            t = dve.tt(prob[:, hh, :], s, C("band", 0, 384), ALU.add, after=[tp] + prev)
            bank_free[(b0, b1)[hh]] = [t]
            dve.wait(t)
            for i, cols in enumerate((slice(0, P), slice(P, 384))):
                t = dve.mark(nc.vector.tensor_reduce(stat[:, 0, 2 * hh + i:2 * hh + i + 1], prob[:, hh, cols],
                                                     AX_X, ALU.max, negate=True))
            for i, cols in enumerate((slice(0, P), slice(P, 384))):
                te = act.act(prob[:, hh, cols], prob[:, hh, cols], ACT.Exp, after=[t],
                             bias=stat[:, 0, 2 * hh + i:2 * hh + i + 1],
                             accum_out=stat[:, 1, 2 * hh + i:2 * hh + i + 1])
            yield
        t = dve.recip(stat[:, 1], stat[:, 1], after=[te])
        for hh in range(2):
            for i, cols in enumerate((slice(0, P), slice(P, 384))):
                t1 = dve.ts(prob[:, hh, cols], prob[:, hh, cols], stat[:, 1, 2 * hh + i:2 * hh + i + 1],
                            ALU.mult, after=[t])
        yield
        pe.wait(t1)
        for hh in range(2):
            use_bank((b0, b1)[hh])
            for j in range(3):
                last = pe.mm(ps[:, (b0, b1)[hh], j * P:(j + 1) * P], prob[:, hh, j * P:(j + 1) * P], ident)
            tp = pe.mark(last)
            t2 = act.act(probT[:, hh], ps[:, (b0, b1)[hh], 0:384].rearrange("p (j n) -> p j n", j=3), ACT.Copy,
                         after=[tp] + prev)
            bank_free[(b0, b1)[hh]] = [t2]
            yield
        use_bank(7)
        pe.wait(t2, v_ready[p])
        for hh in range(2):
            vh = slice(hh * P, (hh + 1) * P)
            o = ps[:, 7, 256 * hh:256 * hh + 256]
            pe.mm(o[:, 0:P], v_tok[p % 3][:, 0, vh], probT[:, hh, 0, :])
            pe.mm(o[:, P:T], v_tok[p % 3][:, 0, vh], probT[:, hh, 1, :], start=True, stop=False)
            last = pe.mm(o[:, P:T], v_tok[p % 3][:, 1, vh], probT[:, hh, 2, :], start=False, stop=True)
        tp = pe.mark(last)
        t = dve.tt(o32[:, 2 * p:2 * p + 2, :], zg[p % 3],
                              ps[:, 7, :].rearrange("p (h t) -> p h t", h=2), ALU.mult,
                              after=[tp, z_ready[p]] + stage_free)
        core_last.append(t)
        bank_free[7] = [t]
        yield

    cores = InFlight()
    step = None
    for p in range(NH // 2):
        for part in range(2):
            linear(2, hT, evac_qk(p, part), step, every=8)
        token_major(2, hT, evac_v(p), step, every=8)
        linear(2, hT, evac_z(p), step, every=8)
        cores.start(attention_core(p))
        step = cores.step
    hT_read = (pe.sem, pe.n)
    cores.finish()
    for p in range(NH // 2):
        oT.split(2 * p, 2, [core_last[p], hT_read], pool if p % 2 else dve)

    y = [at(144, 2, 256), at(146, 2, 256)]
    y_sem = [Loads(sem("y_stored0")), Loads(sem("y_stored1"))]
    y_free = [[], []]
    end_free = fence()
    dst = out.rearrange("b (t p) d -> p (b t) d", p=P)

    def add_residual(blk, t, acc):
        return pe.mm(acc, xT[:, blk, t * P:(t + 1) * P], ident, start=False, stop=True)

    def evac_y(i, acc, done):
        ty = act.act(y[i % 2].rearrange("p t (n f) -> p t n f", n=2), acc, ACT.Copy,
                     after=[done] + y_free[i % 2] + end_free)
        sp.wait(ty)
        y_free[i % 2] = [y_sem[i % 2].start(nc.sync, dst[:, :, 256 * i:256 * i + 256], y[i % 2])]
        return [ty]

    pe.wait(t_x)
    token_major(16, oT, evac_y, tail=add_residual)
    for loads in y_sem:
        nc.sync.wait_ge(loads.sem, loads.n)
    ctx.close()


def _columns(v):
    return np.ascontiguousarray(v.reshape(-1, P).T)


def _states(a):
    return a.reshape(32, P).T


def _constants():
    c = np.zeros((P, NCONST), np.float32)
    i = np.arange(P)
    row, col = i[:, None], i[None, :]
    c[:, 0:P] = row == col
    c[:, P:2 * P] = 1.0
    c[:, 2 * P:3 * P] = row <= col
    c[:, 3 * P:4 * P] = row + col == P - 1
    for l in range(7):
        b = 1 << l
        c[:, (4 + l) * P:(5 + l) * P] = (row // (2 * b) == col // (2 * b)) & (row % (2 * b) < b) & (col % (2 * b) >= b)
    q = i[:, None] // CHUNK
    c[:, 11 * P:12 * P] = np.where(col // CHUNK <= q, 0.0, NEG)
    k = np.arange(2 * P)[None, :] // CHUNK
    c[:, 12 * P:14 * P] = np.where(k <= q + 2, 0.0, NEG)
    c[:, 14 * P:14 * P + 16] = np.arange(16)
    return c


def _layout(inp):
    f = {k: np.asarray(v) for k, v in inp.items()}
    L = lambda name: f[name][0]
    par = np.zeros((P, NPARAM), np.float32)

    def put(name, v):
        a, n = PCOL[name]
        par[:, a:a + n] = v

    for name, src in (("norm_mix", "norm_mix"), ("b_gate", "b_gate"), ("dw_b", "conv_b_dw"), ("ln_g", "conv_ln_g"),
                      ("ln_b", "conv_ln_b"), ("ssm_d", "ssm_d"), ("norm_ffn", "norm_ffn"),
                      ("norm2a", "norm_w_2"), ("onorm", "a_out_norm_w_2"), ("qnorm", "b_q_norm_w_2"),
                      ("knorm", "b_k_norm_w_2")):
        put(name, _columns(L(src)))
    put("norm_final", _columns(f["norm_final"]))
    put("norm2b", _columns(f["norm_w_2"][1]))
    put("dw_w", _columns(L("conv_w_dw").reshape(-1)))
    put("qkv_w", _columns(L("a_conv_w_2").reshape(-1)))
    put("a_re", _states(L("ssm_a_re")))
    put("a_im", _states(L("ssm_a_im")))
    put("log_dt", _states(np.repeat(L("ssm_log_dt")[:, None], 64, 1)))
    put("a_log", np.broadcast_to(L("a_a_log_2"), (P, 16)))
    put("dt_bias", np.broadcast_to(L("a_dt_bias_2"), (P, 16)))
    put("eps_rms", RMS_EPS)
    put("eps_ln", LN_EPS)
    bT = np.zeros((8, 4, 2, 16, 2, 2, 64), np.float32)
    cT = np.zeros((2, 64, 2, 32, 2, 16), np.float32)
    for plane, (b, c) in enumerate(((L("ssm_b_re"), L("ssm_c_re")), (L("ssm_b_im"), L("ssm_c_im")))):
        b5 = b.reshape(8, 4, 2, 64, 16)
        c4 = c.reshape(32, 2, 16, 64)
        for g in range(2):
            bT[:, :, g, :, plane, g, :] = b5[:, :, g].transpose(0, 1, 3, 2)
            cT[g, :, plane, :, g, :] = c4[:, g].transpose(2, 0, 1)
    keysT = L("peer_sub_keys").reshape(16, 128, 128).transpose(2, 0, 1)
    bc = np.stack([bT.reshape(8, P, 2, P), cT.reshape(P, 2, 8, 4, 32).transpose(2, 0, 1, 3, 4).reshape(8, P, 2, P)],
                  axis=2)
    matrices = {"w_in": L("w_in"), "conv_out": L("conv_w_out"), "w_val": L("ssm_w_val"), "w_gate": L("ssm_w_gate"),
                "w_out": L("w_out"), "w_q": L("peer_w_q"), "a_in": L("a_w_in_2"), "a_out": L("a_w_out_2"),
                "b_in": L("b_w_in_2"), "b_out": L("b_w_out_2")}
    weights = np.stack([matrices[m][:, c:c + n].reshape(-1, P, n).transpose(1, 0, 2).reshape(P, 2048)
                        for m, c, n in PLAN])
    a_small = L("a_w_in_2")[:, 8192:].reshape(16, P, 32).transpose(1, 0, 2)
    return {
        "x": f["x"], "consts": _constants(), "params": par, "weights": weights, "bcT": bc, "keysT": keysT,
        "u_tab": L("peer_u"), "v_tab": L("peer_v"), "a_small": a_small, "rel_rev": L("b_rel_bias_2")[:, ::-1],
    }


def kernel(**inputs):
    import concourse.bacc as bacc
    from concourse.bass_utils import run_bass_kernel_spmd

    nc = bacc.Bacc("TRN2", target_bir_lowering=False, num_devices=1)
    arrays = {k: np.ascontiguousarray(v) for k, v in _layout(inputs).items()}
    args = {k: nc.dram_tensor(k, v.shape, mybir.dt.from_np(v.dtype), kind="ExternalInput").ap()
            for k, v in arrays.items()}
    out = nc.dram_tensor("out", (1, 256, 2048), F32, kind="ExternalOutput").ap()
    build(nc, out=out, **args)
    got = run_bass_kernel_spmd(nc, [arrays], core_ids=[0])
    return got.results[0]["out"]
```

```python
from contextlib import ExitStack

import concourse.bass as bass
import concourse.mybir as mybir
import numpy as np
from concourse.alu_op_type import AluOpType as ALU

F32 = mybir.dt.float32
F32R = mybir.dt.float32r
U32 = mybir.dt.uint32
ACT = mybir.ActivationFunctionType
AX_X = mybir.AxisListType.X

P = 128
KB = 256
NEG = -3.0e38
RMS_EPS, LN_EPS = 1e-6, 1e-5
CHUNK = 64
PI_SAFE = 3.1415925
ROUND = 12582912.0
TWO_PI = (6.28125, 0.0019350051879882812, 3.019916050561733e-07)


class Engine:

    def __init__(self, handle, semaphore):
        self.e, self.sem, self.n, self.seen = handle, semaphore, 0, {}

    def wait(self, *tokens):
        for sem, value in tokens:
            if self.seen.get(sem.name, 0) < value:
                self.e.wait_ge(sem, value)
                self.seen[sem.name] = value

    def mark(self, instruction):
        instruction.then_inc(self.sem, 1)
        self.n += 1
        return (self.sem, self.n)


class Vec(Engine):

    def tt(self, out, a, b, op, after=()):
        self.wait(*after)
        return self.mark(self.e.tensor_tensor(out, a, b, op))

    def ts(self, out, a, s1, op0, s2=None, op1=None, after=()):
        self.wait(*after)
        if op1 is None:
            return self.mark(self.e.tensor_scalar(out, a, s1, None, op0))
        return self.mark(self.e.tensor_scalar(out, a, s1, s2, op0, op1))

    def stt(self, out, a, s, b, op0, op1, after=()):
        self.wait(*after)
        return self.mark(self.e.scalar_tensor_tensor(out=out, in0=a, scalar=s, in1=b, op0=op0, op1=op1))

    def copy(self, out, a, after=()):
        self.wait(*after)
        return self.mark(self.e.tensor_copy(out, a))

    def memset(self, out, value, after=()):
        self.wait(*after)
        return self.mark(self.e.memset(out, value))

    def recip(self, out, a, after=()):
        self.wait(*after)
        return self.mark(self.e.reciprocal(out, a))


class Scalar(Engine):

    def act(self, out, a, func, after=(), **kw):
        self.wait(*after)
        return self.mark(self.e.activation(out, a, func, **kw))


class Tensor(Engine):

    def mm(self, out, lhsT, rhs, start=True, stop=True, after=()):
        self.wait(*after)
        return self.e.matmul(out, lhsT, rhs, start=start, stop=stop, skip_group_check=True)


    def transpose(self, out, in_, identity):
        return self.e.transpose(out, in_, identity)


class Loads:

    def __init__(self, semaphore):
        self.sem, self.n = semaphore, 0

    def start(self, queue, out, in_):
        queue.dma_start(out, in_).then_inc(self.sem, 16)
        self.n += 16
        return (self.sem, self.n)


def wide(ap, shape):
    return ap.broadcast_to(shape)


def param_columns():
    at, cols = 0, {}
    for name, n in (("norm_mix", 16), ("b_gate", 32), ("dw_w", 31 * 8), ("dw_b", 8), ("ln_g", 8), ("ln_b", 8),
                    ("a_re", 32), ("a_im", 32), ("log_dt", 32), ("ssm_d", 8), ("norm_ffn", 16),
                    ("norm_final", 16), ("norm2a", 16), ("norm2b", 16), ("qkv_w", 4 * 48), ("onorm", 1),
                    ("qnorm", 1), ("knorm", 1), ("a_log", 16), ("dt_bias", 16), ("eps_rms", 1), ("eps_ln", 1)):
        cols[name] = (at, n)
        at += n
    return cols, at


PCOL, NPARAM = param_columns()


Z_LATE_A, Z_LATE_B = 2, 2
OUT_ORDER = [(0, 0), (0, 1), (0, 2), (1, 0), (1, 1), (1, 2), (0, 3), (1, 3)] + \
    [(g, k) for g in (2, 3) for k in range(4)]


def weight_plan():
    plan = []

    def add(name, first, n, k=2048):
        width = 2048 * P // k
        plan.extend((name, 0, first + c * width, width) for c in range(n // width))

    add("w_in", 2048, 1024)
    for q in range(4):
        add("w_in", 256 * q, 256)
        add("w_in", 1024 + 256 * q, 256)
    add("w_in", 3072 + 2048, 2048)
    for q in range(4):
        add("w_in", 3072 + 512 * q, 512)
        add("conv_out", 512 * q, 512, 1024)
    for q in range(4):
        add("w_val", 512 * q, 512, 1024)
        add("w_gate", 512 * q, 512, 1024)
    add("w_out", 0, 2048)
    add("w_q", 0, 2048)
    before_peer = len(plan)
    for p in range(8 + Z_LATE_A):
        if p >= Z_LATE_A:
            add("a_in", 3 * 2048 + 256 * (p - Z_LATE_A), 256)
        if p < 8:
            for part in range(3):
                add("a_in", part * 2048 + 256 * p, 256)
    plan.extend(("a_out", 512 * k, 512 * g, 512) for g, k in OUT_ORDER)
    for p in range(8 + Z_LATE_B):
        if p >= Z_LATE_B:
            add("b_in", 3 * 2048 + 256 * (p - Z_LATE_B), 256)
        if p < 8:
            for part in range(2):
                add("b_in", part * 2048 + 256 * p, 256)
            plan.extend(("b_in", 1024 * half, 2 * 2048 + 256 * p, 256) for half in range(2))
    plan.extend(("b_out", 512 * k, 512 * g, 512) for g, k in OUT_ORDER)
    return plan, before_peer


PLAN, N_BEFORE_PEER = weight_plan()
CCOL = {"ident": (0, P), "ones": (P, P), "upto": (2 * P, P), "flip": (3 * P, P), "level": (4 * P, 7 * P),
        "band": (11 * P, 3 * P), "iota": (14 * P, 16)}
NCONST = 14 * P + 16


def build(nc, x, consts, params, weights, bcT, keysT, u_tab, v_tab, a_small, rel_rev, out):
    D, T, NCH = 2048, 256, 16
    EA, EB, EO = 8, 12, 2
    QUARTERS_CONV, QUARTERS_SSM = 4, 2
    EQ, EP = 18, 2
    TAPS = 31
    NH = 16
    ctx = ExitStack()

    def sem(name):
        return ctx.enter_context(nc.semaphore(name))

    ps = ctx.enter_context(nc.psum_tensor("ps", [P, 8, 512], F32))

    pe = Tensor(nc.tensor, sem("pe_done"))
    dve = Vec(nc.vector, sem("dve_done"))
    pool = Vec(nc.gpsimd, sem("pool_done"))
    act = Scalar(nc.scalar, sem("act_done"))
    sp = Engine(nc.sync, None)
    small = Loads(sem("small_loads"))

    LOW = 64
    placed = {}

    def place(kb, size, dtype):
        if (kb, size, dtype) not in placed:
            with ExitStack() as frame:
                if kb:
                    frame.enter_context(nc.sbuf_tensor(f"filler{len(placed)}", [P, int(kb * KB)], F32))
                placed[kb, size, dtype] = frame.enter_context(
                    nc.sbuf_tensor(f"{dtype.name}_at_{len(placed)}", [P, int(size * KB)], dtype))
        return placed[kb, size, dtype]

    def at(kb, *shape, dtype=F32):
        n = int(np.prod(shape))
        if dtype == F32:
            base, size = (0, LOW) if kb < LOW else (LOW, 206 - LOW)
        else:
            base, size = kb, n / KB
        first = int((kb - base) * KB)
        assert first + n <= size * KB, (kb, shape)
        v = place(base, size, dtype)[:, first:first + n]
        if len(shape) == 1:
            return v
        names = "abcd"[:len(shape)]
        sizes = {k: s for k, s in zip(names[1:], shape[1:])}
        return v.rearrange(f"p ({' '.join(names)}) -> p {' '.join(names)}", **sizes)

    def rat(kb, *shape):
        return at(kb, *shape, dtype=F32R)

    def fence():
        return [(e.sem, e.n) for e in (pe, dve, pool, act) if e.n]

    cst = at(196, NCONST)
    par = at(196 + NCONST / KB, NPARAM)
    assert 196 * KB + NCONST + NPARAM <= 206 * KB

    def C(name, k=0, n=P):
        a = CCOL[name][0] + k * P
        return cst[:, a:a + n]

    def Pm(name, k=0, n=1):
        a = PCOL[name][0] + k
        return par[:, a:a + n]

    ident, ones, upto = C("ident"), C("ones"), C("upto")

    NSLOT, NHI, BLOCK = 5, 3, 2048
    slot_sem = [sem(f"weights{s}") for s in range(NSLOT)]
    started, used, split = [0], [0], [0]
    limit = [N_BEFORE_PEER]
    block_done = {}
    block_split = {}
    pool_quarters = [1]

    def start_load():
        n = started[0]
        nc.sync.dma_start(at(8 * (n % NSLOT), BLOCK), weights[n]).then_inc(slot_sem[n % NSLOT], 16)
        started[0] += 1

    def split_quarter():
        n, q = split[0] // 4, split[0] % 4
        split[0] += 1
        cols = slice(q * BLOCK // 4, (q + 1) * BLOCK // 4)
        w, lo = at(8 * (n % NSLOT), BLOCK)[:, cols], rat(8 * (n % NSLOT), BLOCK)[:, cols]
        hi = rat(40 + 8 * (n % NHI), BLOCK)[:, cols]
        loaded = (slot_sem[n % NSLOT], 16 * (n // NSLOT + 1))
        free = [block_done[n - NHI]] if n >= NHI else []
        th = act.act(hi, w, ACT.Copy, after=[loaded] + free)
        on_pool = q < pool_quarters[0]
        tl = (pool if on_pool else dve).tt(lo, w, hi, ALU.subtract, after=[th])
        block_split.setdefault(n, {})["pool" if on_pool else "dve"] = tl
        block_split[n]["act"] = th

    def split_ahead(upto):
        while split[0] < min(upto, 4 * limit[0]):
            split_quarter()

    def take_block():
        n = used[0]
        used[0] += 1
        split_ahead(4 * (n + NHI - 1))
        width = PLAN[n][3]
        pe.wait(*block_split.pop(n).values())
        return tuple(v.rearrange("p (k n) -> p k n", n=width)
                     for v in (rat(40 + 8 * (n % NHI), BLOCK), rat(8 * (n % NSLOT), BLOCK)))

    def split_goal(sixteenths):
        return 4 * (used[0] + NHI - 2) + sixteenths // 4 + 1

    def release_block(last_use):
        block_done[used[0] - 1] = last_use
        if started[0] < limit[0]:
            sp.wait(last_use)
            start_load()

    bank_free = {b: [] for b in range(8)}

    def use_bank(b):
        pe.wait(*bank_free[b])
        bank_free[b] = []

    lin_bank = [0]

    def next_bank():
        b = lin_bank[0] % 3
        lin_bank[0] += 1
        use_bank(b)
        return b

    class Halves:

        def __init__(self, hi_kb, lo_kb, n, ready=None):
            self.hi, self.lo, self.n = rat(hi_kb, n, T), rat(lo_kb, n, T), n
            self.f32 = at(lo_kb, n, T)
            self.ready = ready or [[] for _ in range(n)]

        def split(self, c, m, after, lo_engine=None, cols=slice(0, T)):
            hi, lo, whole = (v[:, c:c + m, cols] for v in (self.hi, self.lo, self.f32))
            th = act.act(hi, whole, ACT.Copy, after=after)
            tl = (lo_engine or dve).tt(lo, whole, hi, ALU.subtract, after=[th])
            for i in range(m):
                self.ready[c + i] = self.ready[c + i] * (cols.start > 0) + [th, tl]
            return tl

    def passes(w, x, out_, wk, xk, start, stop, weights_move=False):
        pairs = ((w[0], x[0]), (w[0], x[1]), (w[1], x[0])) if not weights_move else \
            ((w[0], x[0]), (w[1], x[0]), (w[0], x[1]))
        for i, (a, b) in enumerate(pairs):
            lhs, rhs = (wk(a), xk(b)) if not weights_move else (xk(b), wk(a))
            last = pe.mm(out_, lhs, rhs, start=start and i == 0, stop=stop and i == 2)
        return last

    def linear(n_chunks, src, evacuate, step=None, every=4, tail=None):
        kn = src.n
        per_block = BLOCK // kn // P
        count = 0
        for f in range(n_chunks):
            if f % per_block == 0:
                w = take_block()
            if f % 2 == 0:
                b = next_bank()
                acc = ps[:, b, :].rearrange("p (h t) -> p h t", h=2)
            col = (f % per_block) * P
            for k in range(kn):
                if k % 4 == 0:
                    split_ahead(split_goal(f % per_block * kn + k))
                pe.wait(*src.ready[k])
                last = passes(w, (src.hi, src.lo), acc[:, f % 2, :], lambda a: a[:, k, col:col + P],
                              lambda x_: x_[:, k, :], k == 0, k == kn - 1 and tail is None)
                count += 1
                if k == kn - 1:
                    if tail is not None:
                        last = tail(f, acc[:, f % 2, :])
                    done = pe.mark(last)
                if step is not None and count % every == 0:
                    step()
            if f % per_block == per_block - 1:
                release_block(done)
            if f % 2 == 1:
                bank_free[b] = evacuate(f // 2, acc, done)

    def out_products(src, token_major, evacuate, before=None, step=None, every=4):
        count = 0
        for g, kq in OUT_ORDER:
            banks = ((0, 1), (2, 7))[g % 2]
            w = take_block()
            if kq == 0:
                for b in banks:
                    use_bank(b)
            for k in range(4 * kq, 4 * kq + 4):
                while not src.ready[k]:
                    step()
            for i, b in enumerate(banks):
                if kq == 0 and before is not None:
                    before(g, i, ps[:, b, :])
                for n in range(1 if token_major else 2):
                    for kl in range(4):
                        k = 4 * kq + kl
                        split_ahead(split_goal(8 * i + (2 * kl if token_major else 4 * n + kl)))
                        pe.wait(*src.ready[k])
                        first = kq == 0 and kl == 0 and n == 0 and before is None
                        if token_major:
                            last = passes(w, (src.hi, src.lo), ps[:, b, :], lambda a: a[:, kl, :],
                                          lambda x_: x_[:, k, i * P:(i + 1) * P], first, k == NCH - 1,
                                          weights_move=True)
                        else:
                            col = (2 * i + n) * P
                            last = passes(w, (src.hi, src.lo), ps[:, b, n * T:(n + 1) * T],
                                          lambda a: a[:, kl, col:col + P], lambda x_: x_[:, k, :],
                                          first, k == NCH - 1)
                        if kl == 3 and n == (0 if token_major else 1):
                            done = pe.mark(last)
                        count += 2 if token_major else 1
                        if step is not None and count % every == 0:
                            step()
                if kq == 3:
                    bank_free[b] = evacuate(g, i, ps[:, b, :], done)
            release_block(done)

    class InFlight:

        def __init__(self):
            self.gens, self.turn = [], 0

        def start(self, gen):
            while len(self.gens) >= 2:
                n = len(self.gens)
                self.turn = 0
                self.step()
                if len(self.gens) == n and n == 2:
                    self.turn = 0
            self.gens.append(gen)

        def step(self):
            if self.gens:
                i = self.turn % len(self.gens)
                self.turn += 1
                try:
                    next(self.gens[i])
                except StopIteration:
                    self.gens.pop(i)
                    self.turn = 0

        def finish(self):
            while self.gens:
                self.step()

    def runner(gen):
        state = [True]

        def step():
            if state[0]:
                try:
                    next(gen)
                except StopIteration:
                    state[0] = False

        def finish():
            while state[0]:
                step()
        return step, finish

    class SumSquares:

        def __init__(self, src, sq):
            self.src, self.sq, self.pending, self.n, self.done = src, sq, [], 0, None

        def add(self, c, after):
            t = act.act(self.sq[:, c:c + 2], self.src[:, c:c + 2], ACT.Square, after=after)
            self.pending.append((c, t))

        def flush(self, keep=0):
            while len(self.pending) > keep:
                c, t = self.pending.pop(0)
                if self.n == 0:
                    use_bank(3)
                pe.wait(t)
                for i in range(2):
                    last = pe.mm(ps[:, 3, 0:T], ones, self.sq[:, c + i, :], start=(self.n == 0),
                                 stop=(self.n == NCH - 1))
                    self.n += 1
                self.done = pe.mark(last)

    def inverse_rms(sums):
        sums.flush()
        root = sums.sq[:, 0, :]
        t = act.act(root, ps[:, 3, 0:T], ACT.Sqrt, after=[sums.done], scale=1.0 / D, bias=Pm("eps_rms"))
        bank_free[3] = [t]
        return root, dve.recip(root, root, after=[t])

    def rms_halves(src, ready, sums, gains, dst, dst_free):
        root, t = inverse_rms(sums)
        for c in range(NCH):
            t1 = dve.stt(dst.f32[:, c, :], src[:, c, :], Pm(gains, c), root, ALU.mult, ALU.mult,
                         after=[t] + ready + dst_free)
            if c % 4 == 3:
                dst.split(c - 3, 4, [t1] + dst_free, pool if c % 8 == 7 else dve)

    xT = at(96, NCH, T)
    x_tok = at(112, 2, D)
    x_src = x.rearrange("b (t p) d -> p (b t) d", p=P)
    identr = rat(195.5, P)
    t_const = small.start(nc.scalar, cst, consts)
    x_loads = [Loads(sem("x_loaded0")), Loads(sem("x_loaded1"))]
    t_xl = [x_loads[i].start(nc.scalar, x_tok[:, :, i * 1024:(i + 1) * 1024], x_src[:, :, i * 1024:(i + 1) * 1024])
            for i in range(2)]
    t_small = small.start(nc.scalar, par, params)
    for _ in range(NSLOT):
        start_load()

    def to_feature_major(tok_view, ready, dst, sums, after_evac, extra=None):
        for c2 in range(NCH // 2):
            pe.wait(*ready[c2 // 4])
            b = next_bank()
            acc = ps[:, b, :].rearrange("p (h t) -> p h t", h=2)
            for half in range(2):
                c = 2 * c2 + half
                for t in range(2):
                    last = pe.transpose(acc[:, half, t * P:(t + 1) * P], tok_view[:, t, c * P:(c + 1) * P], ident)
            done = pe.mark(last)
            d = dst[:, 2 * c2:2 * c2 + 2, :]
            if extra is None:
                t = dve.copy(d, acc, after=[done])
            else:
                t = dve.tt(d, acc, extra[:, 2 * c2:2 * c2 + 2, :], ALU.add, after=[done])
            bank_free[b] = [t]
            sums.add(2 * c2, [t] + after_evac)
            sums.flush(keep=1)
        return t

    pe.wait(t_const)
    sums = SumSquares(xT, at(128, NCH, T))
    t_x = to_feature_major(x_tok, [[t_xl[0]], [t_xl[1]]], xT, sums, [])
    t_idr = act.act(identr, ident, ACT.Copy, after=[t_const])
    act.wait(t_small)
    dve.wait(t_small)
    hT = Halves(64, 80, NCH)
    split_ahead(4 * (NHI - 1))
    rms_halves(xT, [t_x], sums, "norm_mix", hT, [])

    uT = at(96, 8, T)
    glu = at(104, 8, T + TAPS - 1)
    conv = Halves(185, 113, 8)
    conv32 = conv.f32
    gates = at(121, 32, T)
    sig, mean = at(161, 2, T), at(163, T)
    stage_free = fence()

    def evac_u(i, acc, done):
        return [act.act(uT[:, 2 * i:2 * i + 2, :], acc, ACT.Copy, after=[done] + stage_free)]

    linear(8, hT, evac_u)
    t_u = (act.sem, act.n)

    NJ = 32
    co = at(181, 10, NJ)
    (dt_, r_, th, n_, s_, c_, k_re, k_im, m2, tmp) = (co[:, i, :] for i in range(10))
    a_re, a_im = Pm("a_re", 0, NJ), Pm("a_im", 0, NJ)
    t = act.act(dt_, Pm("log_dt", 0, NJ), ACT.Exp, after=[t_small])
    t1 = dve.tt(r_, a_re, dt_, ALU.mult, after=[t])
    t_r = act.act(r_, r_, ACT.Exp, after=[t1])
    t = dve.tt(th, a_im, dt_, ALU.mult, after=[t1])
    t = dve.ts(n_, th, 1.0 / (2 * np.pi), ALU.mult, ROUND, ALU.add, after=[t])
    t = dve.ts(n_, n_, -ROUND, ALU.add, after=[t])
    for part in TWO_PI:
        t = dve.stt(th, n_, -part, th, ALU.mult, ALU.add, after=[t])
    t = dve.ts(th, th, PI_SAFE, ALU.min, -PI_SAFE, ALU.max, after=[t])
    t_s = act.act(s_, th, ACT.Sin, after=[t])
    t = act.act(c_, th, ACT.Sin, after=[t], scale=0.5)
    t = dve.tt(c_, c_, c_, ALU.mult, after=[t])
    t_cos = dve.ts(c_, c_, -2.0, ALU.mult, 1.0, ALU.add, after=[t])
    t = dve.tt(tmp, r_, c_, ALU.mult, after=[t_cos, t_r])
    t_a = dve.ts(tmp, tmp, -1.0, ALU.add, after=[t])
    t_b = dve.tt(n_, r_, s_, ALU.mult, after=[t_s])
    t = dve.tt(m2, a_re, a_re, ALU.mult)
    t1 = dve.tt(dt_, a_im, a_im, ALU.mult, after=[t_b])
    t = dve.tt(m2, m2, dt_, ALU.add, after=[t1])
    t_m = dve.recip(m2, m2, after=[t])
    t1 = dve.tt(k_re, tmp, a_re, ALU.mult, after=[t_a])
    t = dve.tt(dt_, n_, a_im, ALU.mult, after=[t_m])
    t = dve.tt(k_re, k_re, dt_, ALU.add, after=[t])
    t_k1 = dve.tt(k_re, k_re, m2, ALU.mult, after=[t])
    t1 = dve.tt(k_im, n_, a_re, ALU.mult)
    t = dve.tt(dt_, tmp, a_im, ALU.mult, after=[t_k1])
    t = dve.tt(k_im, k_im, dt_, ALU.subtract, after=[t])
    t_k = dve.tt(k_im, k_im, m2, ALU.mult, after=[t])

    t_pad = dve.memset(glu[:, :, 0:TAPS - 1], 0.0, after=stage_free)
    glu_ready = []
    value = [None]

    def evac_value(i, acc, done):
        value[0] = (acc, done, (lin_bank[0] - 1) % 3)
        return []

    def evac_glu(i, acc, done):
        q = len(glu_ready)
        t = act.act(sig, acc, ACT.Sigmoid, after=[done] + glu_ready[-1:] + stage_free)
        glu_ready.append(dve.tt(glu[:, 2 * q:2 * q + 2, TAPS - 1:], value[0][0], sig, ALU.mult,
                                after=[t, value[0][1]] + stage_free))
        bank_free[value[0][2]] = glu_ready[-1:]
        return [t]

    def convolution():
        for c in range(8):
            while len(glu_ready) <= c // 2:
                yield
            for k in range(TAPS):
                w = Pm("dw_w", k * 8 + c)
                src = glu[:, c, k:k + T]
                if k == 0:
                    t = dve.ts(conv32[:, c, :], src, w, ALU.mult, Pm("dw_b", c), ALU.add,
                               after=[glu_ready[c // 2], t_pad] + stage_free)
                else:
                    t = dve.stt(conv32[:, c, :], src, w, conv32[:, c, :], ALU.mult, ALU.add, after=[t])
                if k % 8 == 7:
                    yield
        use_bank(3)
        pe.wait(t)
        for c in range(8):
            last = pe.mm(ps[:, 3, 0:T], ones, conv32[:, c, :], start=(c == 0), stop=(c == 7))
        tm = pe.mark(last)
        tm = act.act(mean, ps[:, 3, 0:T], ACT.Copy, after=[tm], scale=1.0 / 1024)
        bank_free[3] = [tm]
        t = dve.tt(conv32, conv32, wide(mean.unsqueeze(1), [P, 8, T]), ALU.subtract, after=[tm])
        yield
        squares = at(104, 8, T)
        t = act.act(squares, conv32, ACT.Square, after=[t])
        yield
        use_bank(3)
        pe.wait(t)
        for c in range(8):
            last = pe.mm(ps[:, 3, 0:T], ones, squares[:, c, :], start=(c == 0), stop=(c == 7))
        t = pe.mark(last)
        squares_read[0] = t
        t = act.act(mean, ps[:, 3, 0:T], ACT.Sqrt, after=[t], scale=1.0 / 1024, bias=Pm("eps_ln"))
        bank_free[3] = [t]
        t = dve.recip(mean, mean, after=[t])
        for c in range(8):
            t1 = dve.stt(conv32[:, c, :], conv32[:, c, :], Pm("ln_g", c), mean, ALU.mult, ALU.mult, after=[t])
            t1 = act.act(conv32[:, c, :], conv32[:, c, :], ACT.Silu, after=[t1], bias=Pm("ln_b", c))
            if c % 4 == 3:
                conv.split(c - 3, 4, [t1])
                yield

    squares_read = [None]

    phase = [at(153, 2, 4, T), at(104, 2, 4, T)]
    work = [at(161, 2, 4, T), at(169, 2, 4, T)]
    phase_tmp = at(177, 2, 4, P)
    bc_sb = [at(193, 2, 2, P), at(182.25, 2, 2, P)]
    cnew = [at(184.25, 4, 32), at(195, 4, 32)]
    bc_loads = [Loads(sem("ssm_weights0")), Loads(sem("ssm_weights1"))]
    ssm_done = [None]

    phase_ready = [None, None]

    def fill_phase(c, free):
        E = phase[c % 2]
        pool.copy(E[:, 0, :, 0:1], c_[:, 4 * c:4 * c + 4].unsqueeze(2), after=[t_cos, t_s] + free)
        t = pool.copy(E[:, 1, :, 0:1], s_[:, 4 * c:4 * c + 4].unsqueeze(2))
        n = 1
        while n < T:
            for plane in range(2):
                pool.tt(E[:, plane, :, n:2 * n], E[:, plane, :, 0:n],
                        wide(E[:, 0, :, n - 1:n], [P, 4, n]), ALU.mult, after=[t])
            for plane in range(2):
                tq = pool.tt(phase_tmp[:, plane, :, 0:n], E[:, plane, :, 0:n],
                             wide(E[:, 1, :, n - 1:n], [P, 4, n]), ALU.mult, after=[t])
            pool.tt(E[:, 0, :, n:2 * n], E[:, 0, :, n:2 * n], phase_tmp[:, 1, :, 0:n], ALU.subtract, after=[tq])
            t = pool.tt(E[:, 1, :, n:2 * n], E[:, 1, :, n:2 * n], phase_tmp[:, 0, :, 0:n], ALU.add)
            n *= 2
            yield
        phase_ready[c % 2] = t

    def load_bc(c):
        act.wait((pe.sem, pe.n), (dve.sem, dve.n))
        return bc_loads[c % 2].start(nc.scalar, bc_sb[c % 2], bcT[c])

    def ssm():
        y_read = []
        bank4 = ps[:, 4:8, :].rearrange("p i (q t) -> p q i t", q=2)
        t_bt = [load_bc(0), None]
        last_out = [squares_read[0]]
        yield
        fill = iter(())
        for c in range(8):
            for _ in fill:
                pass
            if c + 1 < 8:
                t_bt[(c + 1) % 2] = load_bc(c + 1)
                fill = fill_phase(c + 1, last_out + [squares_read[0]])
            bT, cT = bc_sb[c % 2][:, 0], bc_sb[c % 2][:, 1].rearrange("p q (i n) -> p q i n", i=4)
            for b in range(4, 8):
                use_bank(b)
            pe.wait(t_bt[c % 2], t_u)
            for plane in range(2):
                for i in range(4):
                    rows = slice(32 * i, 32 * i + 32)
                    last = pe.mm(bank4[:, plane, i, :], bT[rows, plane, :], uT[rows, c, :])
            t_bu = pe.mark(last)
            yield
            kr, ki = (wide(k[:, 4 * c:4 * c + 4].unsqueeze(2), [P, 4, 32]) for k in (k_re, k_im))
            t1 = dve.tt(cnew[0], cT[:, 0], kr, ALU.mult, after=[t_bt[c % 2], t_k] + y_read[-1:])
            t2 = dve.tt(cnew[1], cT[:, 1], ki, ALU.mult)
            t3 = dve.tt(cnew[0], cnew[0], cnew[1], ALU.subtract, after=[t1, t2])
            t4 = dve.tt(cnew[1], cT[:, 0], ki, ALU.mult, after=[t3])
            t5 = dve.tt(cT[:, 0], cT[:, 1], kr, ALU.mult, after=[t4])
            t_cw = dve.stt(cnew[1], cnew[1], -1.0, cT[:, 0], ALU.mult, ALU.subtract, after=[t5])
            yield
            E = phase[c % 2]
            A, B = work[c % 2], work[(c + 1) % 2]
            cosb = wide(E[:, 0].unsqueeze(1), [P, 2, 4, T])
            sinb = wide(E[:, 1].unsqueeze(1), [P, 2, 4, T])
            t = dve.tt(A, bank4, cosb, ALU.mult, after=[t_bu, phase_ready[c % 2]])
            t = dve.tt(B, bank4, sinb, ALU.mult, after=y_read[-1:])
            for b in range(4, 8):
                bank_free[b] = [t]
            next(fill, None)
            yield
            t1 = dve.tt(A[:, 0], A[:, 0], B[:, 1], ALU.add, after=[t])
            t2 = dve.tt(A[:, 1], A[:, 1], B[:, 0], ALU.subtract)
            next(fill, None)
            yield
            for plane in range(2):
                for i in range(4):
                    dve.wait(t1, t2)
                    t = dve.mark(nc.vector.tensor_tensor_scan(
                        B[:, plane, i, :], wide(r_[:, 4 * c + i:4 * c + i + 1], [P, T]), A[:, plane, i, :], 0.0,
                        ALU.mult, ALU.add))
                next(fill, None)
                yield
            t1 = dve.tt(A, B, cosb, ALU.mult, after=[t])
            t2 = dve.tt(B, B, sinb, ALU.mult, after=[t1])
            last_out[0] = t2
            next(fill, None)
            yield
            t1 = dve.tt(A[:, 0], A[:, 0], B[:, 1], ALU.subtract, after=[t2])
            t2 = dve.tt(A[:, 1], A[:, 1], B[:, 0], ALU.add)
            next(fill, None)
            yield
            use_bank(3)
            pe.wait(t1, t2, t_cw)
            for plane in range(2):
                for i in range(4):
                    rows = slice(32 * i, 32 * i + 32)
                    last = pe.mm(ps[rows, 3, 0:T], cnew[plane][:, i, :], A[:, plane, i, :],
                                 start=(plane == 0), stop=(plane == 1))
            t = pe.mark(last)
            y_read.append(t)
            t = dve.stt(uT[:, c, :], uT[:, c, :], Pm("ssm_d", c), ps[:, 3, 0:T], ALU.mult, ALU.add, after=[t])
            bank_free[3] = [t]
            ssm_done[0] = act.act(uT[:, c, :], uT[:, c, :], ACT.Gelu_apprx_tanh, after=[t])
            next(fill, None)
            yield

    for _ in fill_phase(0, stage_free):
        pass

    def branches():
        yield from convolution()
        pool_quarters[0] = QUARTERS_SSM
        yield from ssm()

    def evac_gates(first):
        def evac(i, acc, done):
            for half in range(2):
                f = first + 2 * i + half
                t = act.act(gates[:, f, :], acc[:, half, :], ACT.Sigmoid, after=[done] + stage_free,
                            bias=Pm("b_gate", f))
            return [t]
        return evac

    def evac_conv(q):
        def evac(i, acc, done):
            f = 4 * q + 2 * i
            return [dve.tt(gates[:, f:f + 2, :], acc, gates[:, f:f + 2, :], ALU.mult, after=[done, gate_done[0]])]
        return evac

    gate_done = [None]
    step, finish = runner(branches())
    for q in range(4):
        pool_quarters[0] = QUARTERS_CONV if q else 0
        linear(2, hT, evac_value, step, every=8)
        linear(2, hT, evac_glu, step, every=8)
    linear(16, hT, evac_gates(NCH), step, every=8)
    while not conv.ready[7]:
        step()
    for q in range(4):
        linear(4, hT, evac_gates(4 * q), step, every=8)
        gate_done[0] = (act.sem, act.n)
        linear(4, conv, evac_conv(q), step, every=8)
    finish()
    hT_read = fence()
    zT = Halves(104, 96, 8)
    zT.split(0, 4, [ssm_done[0]] + hT_read)
    zT.split(4, 4, [ssm_done[0]] + hT_read)

    pool_quarters[0] = 1
    x_tok2 = at(153, 2, D)
    act.wait(*hT_read)
    t_x2 = small.start(nc.scalar, x_tok2, x_src)
    merged = Halves(64, 121, NCH)
    side, sg = at(169, 2, 2, T), at(173, 2, 2, T)
    side_free = [hT_read, hT_read]
    side_ready = [None, None]

    def evac_val(q):
        def evac(i, acc, done):
            f = 4 * q + 2 * i
            side_ready[i] = dve.tt(side[:, i], acc, gates[:, NCH + f:NCH + f + 2, :], ALU.mult,
                                   after=[done] + side_free[i])
            return [side_ready[i]]
        return evac

    def evac_wgate(q):
        def evac(i, acc, done):
            f = 4 * q + 2 * i
            t = act.act(sg[:, i], acc, ACT.Sigmoid, after=[done] + side_free[i])
            t2 = dve.tt(side[:, i], side[:, i], sg[:, i], ALU.mult, after=[t, side_ready[i]])
            t3 = dve.tt(gates[:, f:f + 2, :], gates[:, f:f + 2, :], side[:, i], ALU.add, after=[t2])
            side_free[i] = [t3]
            merged.split(f, 2, [t3])
            return [t]
        return evac

    for q in range(4):
        linear(4, zT, evac_val(q))
        linear(4, zT, evac_wgate(q))

    x_free = fence()
    sums = SumSquares(xT, at(177, NCH, T))

    def add_x(tok_view):
        def tail(f, acc):
            for t in range(2):
                last = pe.mm(acc[:, t * P:(t + 1) * P], tok_view[:, t, f * P:(f + 1) * P], ident,
                             start=False, stop=(t == 1))
            return last
        return tail

    def evac_x1(i, acc, done):
        t = act.act(xT[:, 2 * i:2 * i + 2, :], acc, ACT.Copy, after=[done] + x_free)
        sums.add(2 * i, [t])
        sums.flush(keep=1)
        return [t]

    pe.wait(t_x2)
    linear(16, merged, evac_x1, tail=add_x(x_tok2))
    t_x1 = (act.sem, act.n)
    hT = Halves(64, 80, NCH)
    rms_halves(xT, [t_x1], sums, "norm_ffn", hT, fence())

    HC, NK, TOPK, HEADS = 16, 128, 16, 8
    peer_free = fence()
    qT = at(112, HC, T)
    keys = at(128, HC, NK)
    h_tok = at(136, 2, D)
    NBUF, GRP = 4, 4
    u_buf = [at(152 + 8 * i, D) for i in range(NBUF)]
    v_buf = [at(8 * i, D) for i in range(NBUF)]
    diag = at(32, 2, GRP, P)
    peer_tok = at(112, 2, D)
    scores = at(184, 2, NK)
    cand = at(185, TOPK * TOPK)
    onehot = at(186, TOPK, TOPK)
    top = at(187, 2, TOPK)
    top_i = at(187.25, 2, TOPK).bitcast(U32)
    top_if = at(187.5, 2, TOPK)
    best = at(187.75, TOPK)
    pos = at(188, TOPK).bitcast(U32)
    half_pos = at(188.25, TOPK).bitcast(U32)
    half_f, e_part = at(188.5, TOPK), at(188.75, TOPK)
    gate_sum = at(189, 2)
    expert = [at(190 + t / 2, HEADS * TOPK).bitcast(U32) for t in range(2)]
    route = [at(191 + t / 2, HEADS * TOPK) for t in range(2)]
    dots = [at(192 + t / 2, HEADS * TOPK) for t in range(2)]
    coef = [at(193 + t / 2, HEADS * TOPK) for t in range(2)]
    act.wait(*peer_free)
    t_keys = small.start(nc.scalar, keys, keysT)
    q_ready = []

    def evac_q(i, acc, done):
        t = act.act(qT[:, 2 * i:2 * i + 2, :], acc, ACT.Copy, after=[done] + peer_free)
        q_ready.append(t)
        return [t]

    def top16(values, vals_out, idx_out, ready):
        t = ready
        for r in range(2):
            o, ix = vals_out[:, 8 * r:8 * r + 8], idx_out[:, 8 * r:8 * r + 8]
            dve.wait(*t)
            t1 = dve.mark(nc.vector.max(out=o, in_=values))
            dve.wait(t1)
            t = [dve.mark(nc.vector.max_index(out=ix, in_max=o, in_values=values))]
            if r == 0:
                dve.wait(*t)
                t = [dve.mark(nc.vector.match_replace(out=values, in_to_replace=o, in_values=values,
                                                      imm_value=NEG))]
        return t[0]

    routed = {}
    scores_read = [peer_free]

    def routing(t, h):
        pe.wait(q_ready[h], t_keys)
        use_bank(3)
        for c in range(2):
            last = pe.mm(ps[:, 3, c * P:(c + 1) * P], qT[:, 2 * h + c, t * P:(t + 1) * P], keys[:, 2 * h + c, :])
        done = pe.mark(last)
        ts_ = act.act(scores, ps[:, 3, 0:2 * P].rearrange("p (c n) -> p c n", c=2), ACT.Copy,
                      after=[done] + scores_read[0])
        bank_free[3] = [ts_]
        yield
        for c in range(2):
            tk = top16(scores[:, c, :], top[:, c, :], top_i[:, c, :], [ts_] + peer_free)
        scores_read[0] = [tk]
        yield
        sq = [P, TOPK, TOPK]
        tk = dve.tt(cand.rearrange("p (i j) -> p i j", i=TOPK), wide(top[:, 0].unsqueeze(2), sq),
                    wide(top[:, 1].unsqueeze(1), sq), ALU.add, after=[tk])
        tk = top16(cand, best, pos, [tk])
        prev = dve.copy(top_if, top_i, after=[tk])
        for half, (op, arg) in enumerate(((ALU.logical_shift_right, 4), (ALU.bitwise_and, 15))):
            t1 = dve.ts(half_pos, pos, arg, op, after=[prev])
            dst = e_part if half == 0 else half_f
            t1 = dve.copy(dst, half_pos, after=[t1])
            t1 = dve.tt(onehot, wide(dst.unsqueeze(2), sq), wide(C("iota", 0, 16).unsqueeze(1), sq),
                        ALU.is_equal, after=[t1])
            t1 = dve.tt(onehot, onehot, wide(top_if[:, half].unsqueeze(1), sq), ALU.mult, after=[t1])
            dve.wait(t1)
            prev = dve.mark(nc.vector.tensor_reduce(dst, onehot, AX_X, ALU.add))
        te = dve.stt(e_part, e_part, float(NK), half_f, ALU.mult, ALU.add, after=[prev])
        hk = slice(TOPK * h, TOPK * (h + 1))
        te = dve.copy(expert[t][:, hk], e_part, after=[te])
        yield
        tb = dve.ts(gate_sum[:, 0:1], best[:, 0:1], -1.0, ALU.mult, after=[te])
        tb = act.act(best, best, ACT.Exp, after=[tb], bias=gate_sum[:, 0:1], accum_out=gate_sum[:, 1:2])
        tb = dve.recip(gate_sum[:, 1:2], gate_sum[:, 1:2], after=[tb])
        tb = dve.ts(route[t][:, hk], best, gate_sum[:, 1:2], ALU.mult, after=[tb])
        routed[t, h] = (te, tb)
        yield

    NSEL = HEADS * TOPK
    u_sem = [Loads(sem(f"u_rows{i}")) for i in range(NBUF)]
    v_sem = [Loads(sem(f"v_rows{i}")) for i in range(NBUF)]
    u_free = [peer_free] * NBUF

    def gather(buf, loads, table, idx, free, ready):
        pool.wait(*free, *ready)
        nc.gpsimd.indirect_dma_start(out=buf, out_offset=None, in_=table,
                                     in_offset=bass.IndirectOffsetOnAxis(ap=idx, axis=0)).then_inc(loads.sem, 16)
        loads.n += 16
        return (loads.sem, loads.n)

    diag_free = [[], []]
    groups = [(t, g) for t in range(2) for g in range(NSEL // GRP)]
    coef_ready = {}
    u_loaded = {}

    def u_gathers(n):
        t, g = groups[n]
        for i in range(GRP):
            k = g * GRP + i
            u_loaded[n, i] = gather(u_buf[i], u_sem[i], u_tab, expert[t][:, k:k + 1], u_free[i],
                                    [routed[t, k // TOPK][0]])

    def u_dots(n):
        t, g = groups[n]
        for i in range(GRP):
            k = g * GRP + i
            dve.wait(u_loaded[n, i], htok_done[0])
            td = dve.mark(nc.vector.tensor_tensor_reduce(
                out=u_buf[i], in0=u_buf[i], in1=h_tok[:, t, :], scale=1.0, scalar=0.0, op0=ALU.mult,
                op1=ALU.add, accum_out=dots[t][:, k:k + 1]))
            u_free[i] = [td]
        ks = slice(g * GRP, (g + 1) * GRP)
        tg = act.act(coef[t][:, ks], dots[t][:, ks], ACT.Gelu_apprx_tanh, after=[td])
        coef_done[n] = dve.tt(coef[t][:, ks], coef[t][:, ks], route[t][:, ks], ALU.mult,
                              after=[tg, routed[t, g // 4][1]])

    def diagonals(n):
        t, g = groups[n]
        for i in range(GRP):
            k = g * GRP + i
            coef_ready[n] = act.act(diag[:, n % 2, i, :], ident, ACT.Copy,
                                    after=[coef_done[n]] + diag_free[n % 2] + hT_read, scale=coef[t][:, k:k + 1])

    coef_done = {}

    def v_group(n):
        t, g = groups[n]
        for i in range(GRP):
            k = g * GRP + i
            loaded = gather(v_buf[i], v_sem[i], v_tab, expert[t][:, k:k + 1], v_free[i], [])
            if g == 0 and i == 0:
                for b in range(4):
                    use_bank(4 + b)
            pe.wait(loaded, coef_ready[n])
            summed = []
            for b in range(4):
                last = pe.mm(ps[:, 4 + b, :], diag[:, n % 2, i, :], v_buf[i][:, 512 * b:512 * (b + 1)],
                             start=(k == 0), stop=(k == NSEL - 1))
                if k == NSEL - 1 or b == 3:
                    summed.append(pe.mark(last))
            v_free[i] = summed[-1:]
        diag_free[n % 2] = summed[-1:]
        if g < NSEL // GRP - 1:
            return None
        stored = []
        for b in range(4):
            te = act.act(peer_tok[:, t, 512 * b:512 * (b + 1)], ps[:, 4 + b, :], ACT.Copy,
                         after=[summed[b], qT_read[0]])
            bank_free[4 + b] = [te]
            stored.append(te)
        return stored

    def h_token_major():
        for t in range(2):
            for g in range(4):
                b = 4 + g
                use_bank(b)
                pe.wait(t_idr, *hT.ready[15], *hT.ready[3])
                for i in range(4):
                    for j, half in enumerate((hT.hi, hT.lo)):
                        last = pe.mm(ps[:, b, i * P:(i + 1) * P], half[:, 4 * g + i, t * P:(t + 1) * P], identr,
                                     start=(j == 0), stop=(j == 1))
                done = pe.mark(last)
                tt_ = act.act(h_tok[:, t, 512 * g:512 * (g + 1)], ps[:, b, :], ACT.Copy, after=[done] + peer_free)
                bank_free[b] = [tt_]
                yield
        htok_done.append(tt_)

    htok_done = []

    u_done, beside_q, u_pending = [0], [True], [False]

    def finish_dots():
        if u_pending[0]:
            u_dots(u_done[0])
            u_done[0] += 1
            u_pending[0] = False

    def all_routing():
        for h in range(HEADS):
            while len(q_ready) <= h:
                yield
            yield from routing(0, h)
            if h == 0:
                yield from h_token_major()
            if beside_q[0]:
                finish_dots()
                u_gathers(u_done[0])
                u_pending[0] = True
        for h in range(HEADS):
            yield from routing(1, h)
        qT_read[0] = (pe.sem, pe.n)

    qT_read = [None]
    step, finish = runner(all_routing())
    linear(16, hT, evac_q, step, every=EQ)
    while not htok_done:
        step()
    beside_q[0] = False
    finish_dots()
    hT_read = fence()
    v_free = [hT_read] * NBUF

    hT = Halves(64, 80, NCH)

    def finish_tile(t, stored):
        cols = slice(t * P, (t + 1) * P)
        x_ = xT[:, :, cols]
        free = fence()
        squares = at(136, 2, NCH, P) if t == 1 else at(40, 2, NCH, P)
        sums = ps[:, 3, 0:2 * P].rearrange("p (a n) -> p a n", a=2)
        squared = []
        for g in range(4):
            pe.wait(stored[g])
            b = next_bank()
            for i in range(4):
                c = 4 * g + i
                last = pe.transpose(ps[:, b, i * P:(i + 1) * P], peer_tok[:, t, c * P:(c + 1) * P], ident)
            done = pe.mark(last)
            d = x_[:, 4 * g:4 * g + 4]
            ta = dve.tt(d, d, ps[:, b, :].rearrange("p (i n) -> p i n", i=4), ALU.add, after=[done])
            bank_free[b] = [ta]
            act.act(squares[:, 0, 4 * g:4 * g + 4, :], d, ACT.Square, after=[ta] + free)
            for c in range(4 * g, 4 * g + 4):
                tq = act.act(squares[:, 1, c, :], x_[:, c, :], ACT.Square, scale=Pm("norm_final", c))
            squared.append(tq)
            yield
        use_bank(3)
        for c in range(NCH):
            pe.wait(squared[c // 4])
            last = pe.mm(sums, ones, squares[:, :, c, :], start=(c == 0), stop=(c == NCH - 1))
        t_sum = pe.mark(last)
        root, root2 = squares[:, 0, 0, :], squares[:, 1, 0, :]
        tr = act.act(root, sums[:, 0, :], ACT.Sqrt, after=[t_sum], scale=1.0 / D, bias=Pm("eps_rms"))
        tr = dve.recip(root, root, after=[tr])
        t2 = dve.tt(root2, sums[:, 1, :], root, ALU.mult, after=[tr])
        bank_free[3] = [t2]
        t2 = dve.tt(root2, root2, root, ALU.mult, after=[t2])
        t2 = act.act(root2, root2, ACT.Sqrt, after=[t2], scale=1.0 / D, bias=Pm("eps_rms"))
        yield
        for c in range(NCH):
            ta = dve.stt(x_[:, c, :], x_[:, c, :], Pm("norm_final", c), root, ALU.mult, ALU.mult, after=[tr, tq])
            if c % 4 == 3:
                yield
        x2_done[t] = ta
        tr = dve.recip(root2, root2, after=[t2])
        for g in range(4):
            for c in range(4 * g, 4 * g + 4):
                ta = dve.stt(hT.f32[:, c, cols], x_[:, c, :], Pm("norm2a", c), root2, ALU.mult, ALU.mult,
                             after=[tr] + hT_read)
            hT.split(4 * g, 4, [ta] + hT_read, pool if t == 1 and g % 2 else dve, cols)
            yield

    x2_done = [None, None]
    ahead = u_done[0] + 1
    for n in range(len(groups)):
        for _ in range(EP):
            step()
        if n == NSEL // GRP - 2:
            finish()
        goal = min(len(groups), ahead + n * (len(groups) - ahead) // (len(groups) - 2))
        while u_done[0] < goal:
            t, g = groups[u_done[0]]
            while (t, g * GRP // TOPK) not in routed:
                step()
            u_gathers(u_done[0])
            u_dots(u_done[0])
            u_done[0] += 1
        if n == 0:
            diagonals(0)
        if n + 1 < len(groups):
            diagonals(n + 1)
        t_peer = v_group(n)
        if n == NSEL // GRP - 1:
            step, finish = runner(finish_tile(0, t_peer))
    finish()
    limit[0] = len(PLAN)
    sp.wait(*fence())
    for _ in range(NSLOT):
        start_load()
    for _ in finish_tile(1, t_peer):
        pass
    t_x = x2_done[1]

    NE = 4
    stage_free = fence()
    oT = Halves(64, 112, NCH)
    o32 = oT.f32
    zg = [at(128 + 2 * i, 2, T) for i in range(3)]
    qkv = [at(134, 6, T), at(140, 6, T)]
    raw = [at(146, 2, T + 3), at(148.25, 2, T + 3)]
    core_mem = [150.5, 171.5]
    per_tok = at(192.5, 8, NH, 2)
    (g_, gc_, beta_, eg_, dk_, nbe_, gx_, gy_) = (per_tok[:, i] for i in range(8))
    neg_a = at(193.75, NH)
    small_w = at(134, NCH, 32)
    small_hi = rat(136, NCH, 32)
    small_lo = rat(134, NCH, 32)

    act.wait(*stage_free)
    t_sw = small.start(nc.scalar, small_w, a_small)
    th = act.act(small_hi, small_w, ACT.Copy, after=[t_sw])
    tl = dve.tt(small_lo, small_w, small_hi, ALU.subtract, after=[th])
    use_bank(4)
    pe.wait(th, tl)
    for t in range(2):
        for k in range(NCH):
            pe.wait(*hT.ready[k])
            last = passes((small_hi, small_lo), (hT.hi, hT.lo), ps[:, 4, 32 * t:32 * t + 32],
                          lambda a: a[:, k, :], lambda x_: x_[:, k, t * P:(t + 1) * P], k == 0, k == NCH - 1,
                          weights_move=True)
    done = pe.mark(last)
    ab = ps[:, 4, 0:64].rearrange("p (t s h) -> p h t s", t=2, s=2)
    bias_b = wide(Pm("dt_bias", 0, NH).unsqueeze(2), [P, NH, 2])
    t1 = dve.tt(gx_, ab[:, :, :, 0], bias_b, ALU.add, after=[done] + stage_free)
    t2 = act.act(beta_, ab[:, :, :, 1], ACT.Sigmoid, after=[t1])
    bank_free[4] = [t1, t2]
    t_beta = t2

    def decays():
        t = dve.stt(gy_, gx_, -1.0, gx_, ALU.mult, ALU.min, after=[t1])
        t = act.act(gy_, gy_, ACT.Exp, after=[t])
        t = dve.ts(gy_, gy_, 1.0, ALU.add, after=[t])
        t = act.act(gy_, gy_, ACT.Ln, after=[t])
        t = dve.stt(gx_, gx_, 0.0, gy_, ALU.max, ALU.add, after=[t])
        ta = act.act(neg_a, Pm("a_log", 0, NH), ACT.Exp, after=stage_free)
        ta = dve.ts(neg_a, neg_a, -1.0, ALU.mult, after=[ta])
        t_g = dve.tt(g_, gx_, wide(neg_a.unsqueeze(2), [P, NH, 2]), ALU.mult, after=[t, ta])
        yield
        use_bank(4)
        pe.wait(t_g)
        gflat = g_.rearrange("p h t -> p (h t)")
        pe.mm(ps[:, 4, 0:32], upto, gflat)
        done = pe.mark(pe.mm(ps[:, 4, 32:64], ones, gflat))
        gcf = gc_.rearrange("p h t -> p (h t)")
        t_gc = dve.copy(gcf, ps[:, 4, 0:32], after=[done])
        t = dve.tt(dk_.rearrange("p h t -> p (h t)"), ps[:, 4, 32:64], gcf, ALU.subtract, after=[t_gc])
        bank_free[4] = [t]
        t_dk = act.act(dk_, dk_, ACT.Exp, after=[t])
        t = act.act(eg_, gc_, ACT.Exp, after=[t_gc])
        t_nb = dve.stt(nbe_, eg_, -1.0, beta_, ALU.mult, ALU.mult, after=[t, t_beta])
        decay_tokens.extend((t_g, t_gc, t_dk, t_nb))
        yield

    decay_tokens = []

    z_ready = {}
    core_last = []

    def evac_z(p):
        def evac(i, acc, done):
            z_ready[p] = act.act(zg[p % 3], acc, ACT.Silu, after=[done] + (core_last[p - 3:p - 2] or stage_free))
            return [z_ready[p]]
        return evac

    for r in raw:
        t_pad = dve.memset(r[:, :, 0:3], 0.0, after=stage_free)
    small_free = [(pe.sem, pe.n)]
    core_read = [stage_free + small_free, stage_free + small_free]
    raw_free = [stage_free, stage_free]
    qkv_ready = [[], []]

    def evac_qkv(p, part):
        def evac(i, acc, done):
            r = raw[part % 2]
            tr = act.act(r[:, :, 3:], acc, ACT.Copy, after=[done, t_pad] + raw_free[part % 2])
            for hh in range(2):
                f = part * 16 + 2 * p + hh
                d = qkv[p % 2][:, 2 * part + hh, :]
                t = dve.ts(d, r[:, hh, 0:T], Pm("qkv_w", f), ALU.mult, after=[tr] + core_read[p % 2])
                for k in range(1, 4):
                    t = dve.stt(d, r[:, hh, k:k + T], Pm("qkv_w", 48 * k + f), d, ALU.mult, ALU.add, after=[t])
                raw_free[part % 2] = [t]
                qkv_ready[p % 2] = [act.act(d, d, ACT.Silu, after=[t])]
            return [tr]
        return evac

    def bank_e(b):
        return ps[:, b, :].rearrange("p (e n) -> p e n", e=NE)

    def each(b, lhsT, rhs, es=range(NE)):
        for e in es:
            last = pe.mm(bank_e(b)[:, e, :], lhsT(e), rhs(e))
        return pe.mark(last)

    def transposes(b, src):
        for e in range(NE):
            last = pe.transpose(bank_e(b)[:, e, :], src(e), ident)
        return pe.mark(last)

    def rms_pair(src, n, squares, scale, eps, ready, banks):
        t = act.act(squares, src, ACT.Square, after=ready)
        for j in range(n // 2):
            use_bank(banks[j])
            pe.wait(t)
            last = pe.mm(ps[:, banks[j], :], ones, squares[:, 2 * j:2 * j + 2, :])
            tp = pe.mark(last)
            ta = act.act(squares[:, 2 * j:2 * j + 2, :], ps[:, banks[j], :].rearrange("p (a t) -> p a t", a=2),
                         ACT.Sqrt, after=[tp], scale=scale, bias=eps)
            bank_free[banks[j]] = [ta]
        return dve.recip(squares, squares, after=[ta])

    def delta_core(p):
        src = qkv[p % 2]
        ready = qkv_ready[p % 2]
        hs = slice(2 * p, 2 * p + 2)
        prev = core_last[p - 2:p - 1] if p >= 2 else stage_free
        b0, b1 = (3, 4) if p % 2 == 0 else (5, 6)
        at0 = core_mem[p % 2]
        (E_, A_, Am, X_, Z_, QK, VB) = (at(at0 + 2 * i, NE, P) for i in range(7))
        Y_, KB_T = E_, VB
        sqb = at(at0, 4, T)
        (WK, V0, S_, WN, QD, KD, V1) = (at(at0 + 14 + i, 2, P) for i in range(7))
        qk4 = src[:, 0:4, :]
        t_r = rms_pair(qk4, 4, sqb, 1.0, Pm("eps_rms"), ready + prev, (b0, b1))
        yield
        t_qn = dve.stt(src[:, 0:2], src[:, 0:2], float(P) ** -0.5, sqb[:, 0:2], ALU.mult, ALU.mult, after=[t_r])
        t_kn = dve.tt(src[:, 2:4], src[:, 2:4], sqb[:, 2:4], ALU.mult, after=[t_r])

        def tile(a):
            return lambda e: src[:, 2 * a + e // 2, (e % 2) * P:(e % 2 + 1) * P]

        q_, k_, v_ = tile(0), tile(1), tile(2)

        def col(v):
            return lambda e: wide(v[:, 2 * p + e // 2, e % 2:e % 2 + 1], [P, P])

        yield
        use_bank(b0)
        pe.wait(t_beta, t_g)
        tb = each(b0, col(beta_), lambda e: ident)
        use_bank(b1)
        tg = each(b1, col(g_), lambda e: upto)
        t_kb = dve.tt(KB_T, src[:, 2:4].rearrange("p h (t n) -> p (h t) n", t=2), bank_e(b0), ALU.mult,
                      after=[tb, t_kn] + prev)
        bank_free[b0] = [t_kb]
        for e in range(NE):
            td = dve.ts(E_[:, e, :], bank_e(b1)[:, e, :], gc_[:, 2 * p + e // 2, e % 2:e % 2 + 1], ALU.subtract,
                        0.0, ALU.min, after=[tg, t_gc, t_qn, t_kn])
        yield
        gc1 = bank_e(b1)[:, 1:4:2, :]
        qd2 = QD[:, 0:2, :]
        tq = act.act(qd2, gc1, ACT.Exp, after=[td] + prev)
        bank_free[b1] = [td, tq]
        td = act.act(E_, E_, ACT.Exp, after=[td])
        td = pool.tt(E_, E_, wide(upto.unsqueeze(1), [P, NE, P]), ALU.mult, after=[td])
        t_qd = dve.tt(qd2, qd2, src[:, 0:2, P:2 * P], ALU.mult, after=[tq, t_qn])
        use_bank(7)
        pe.wait(t_qn, t_kn)
        tp = each(7, k_, q_)
        t_qk = dve.tt(QK, E_, bank_e(7), ALU.mult, after=[tp, td] + prev)
        bank_free[7] = [t_qk]
        yield
        use_bank(b0)
        pe.wait(t_kb)
        tp = each(b0, k_, lambda e: KB_T[:, e, :])
        t_a = dve.tt(A_, E_, bank_e(b0), ALU.mult, after=[tp])
        bank_free[b0] = [t_a]
        level = lambda l: wide(C("level", l).unsqueeze(1), [P, NE, P])
        ti = pool.tt(Am, A_, level(0), ALU.mult, after=[t_a] + prev)
        t_z = dve.stt(Z_, Am, -1.0, wide(ident.unsqueeze(1), [P, NE, P]), ALU.mult, ALU.add, after=[ti])
        am_free = t_z
        yield
        use_bank(b1)
        tp = transposes(b1, k_)
        kt = bank_e(b1)
        dkb = wide(dk_[:, hs, 0:1], [P, 2, P])
        nbb = wide(nbe_[:, hs, 1:2], [P, 2, P])
        t_kd = dve.tt(KD, kt[:, 0:4:2, :], dkb, ALU.mult, after=[tp, t_dk] + prev)
        t_wk = dve.tt(WK[:, 0:2, :], kt[:, 1:4:2, :], nbb, ALU.mult, after=[t_nb])
        bank_free[b1] = [t_wk]
        use_bank(b0)
        pe.wait(*ready)
        tp = transposes(b0, v_)
        t_vb = dve.tt(VB, bank_e(b0), wide(beta_[:, hs, :].rearrange("p h t -> p (h t)").unsqueeze(2), [P, NE, P]),
                      ALU.mult, after=[tp])
        bank_free[b0] = [t_vb]
        core_read[p % 2] = [t_vb, t_qd, (pe.sem, pe.n)]
        yield
        use_bank(b1)
        pe.wait(t_z)
        tp = transposes(b1, lambda e: Z_[:, e, :])
        t_x = act.act(X_, bank_e(b1), ACT.Copy, after=[tp] + prev)
        bank_free[b1] = [t_x]
        for l in range(1, 7):
            tm = pool.tt(Am, A_, level(l), ALU.mult, after=[am_free])
            yield
            b2 = 1 << l

            def halves(v, s_):
                return v.rearrange("p (n s b) -> p n s b", s=2, b=b2)[:, :, s_, :]

            def halves_e(v, s_):
                return v.rearrange("p e (n s b) -> p e n s b", s=2, b=b2)[:, :, :, s_, :]

            def narrow(i):
                return ps[:, b1, i * 256:i * 256 + 256].rearrange("p (e n) -> p e n", e=NE)

            use_bank(b0)
            pe.wait(tm, t_x)
            tp = each(b0, lambda e: Am[:, e, :], lambda e: X_[:, e, :])
            am_free = tp
            ty = act.act(Y_, bank_e(b0), ACT.Copy, after=[tp, t_a])
            bank_free[b0] = [ty]
            yield
            pe.wait(ty, t_z)
            use_bank(b1)
            for e in range(NE):
                tz = pe.mm(narrow(0)[:, e, :], Y_[:, e, :], halves(Z_[:, e, :], 1))
            if l < 6:
                for e in range(NE):
                    tz = pe.mm(narrow(1)[:, e, :], Z_[:, e, :], halves(Y_[:, e, :], 0))
            tz = pe.mark(tz)
            zh = halves_e(Z_, 1)
            if l < 6:
                xh = halves_e(X_, 0)
                t_x = dve.tt(xh, xh, narrow(1).rearrange("p e (n b) -> p e n b", b=b2), ALU.subtract,
                             after=[tz])
            t_z = dve.tt(zh, zh, narrow(0).rearrange("p e (n b) -> p e n b", b=b2), ALU.subtract, after=[tz])
            bank_free[b1] = [t_z]
            yield
        use_bank(b0)
        pe.wait(t_z, t_vb)
        tp = each(b0, lambda e: Z_[:, e, :], lambda e: VB[:, e, :], es=(0, 2))
        t_v0 = act.act(V0[:, 0:2, :], bank_e(b0)[:, 0:4:2, :], ACT.Copy, after=[tp] + prev)
        bank_free[b0] = [t_v0]
        use_bank(b1)
        pe.wait(t_wk)
        tp = each(b1, lambda e: WK[:, e // 2, :], lambda e: Z_[:, e, :], es=(1, 3))
        t_wn = dve.copy(WN[:, 0:2, :], bank_e(b1)[:, 1:4:2, :], after=[tp] + prev)
        bank_free[b1] = [t_wn]
        yield
        use_bank(b0)
        pe.wait(t_v0, t_kd)
        tp = each(b0, lambda e: KD[:, e, :], lambda e: V0[:, e, :], es=(0, 1))
        t_s = act.act(S_[:, 0:2, :], bank_e(b0)[:, 0:2, :], ACT.Copy, after=[tp] + prev)
        bank_free[b0] = [t_s]
        yield
        use_bank(b1)
        pe.wait(t_s, t_wn)
        for hh in range(2):
            pe.mm(bank_e(b1)[:, hh, :], Z_[:, 2 * hh + 1, :], VB[:, 2 * hh + 1, :], start=True, stop=False)
            last = pe.mm(bank_e(b1)[:, hh, :], WN[:, hh, :], S_[:, hh, :], start=False, stop=True)
        tp = pe.mark(last)
        t_v1 = act.act(V1, bank_e(b1)[:, 0:2, :], ACT.Copy, after=[tp] + prev)
        bank_free[b1] = [t_v1]
        yield
        use_bank(b0)
        pe.wait(t_qk, t_v1, t_qd)
        for hh in range(2):
            pe.mm(bank_e(b0)[:, 2 * hh, :], V0[:, hh, :], QK[:, 2 * hh, :])
            pe.mm(bank_e(b0)[:, 2 * hh + 1, :], V1[:, hh, :], QK[:, 2 * hh + 1, :], start=True, stop=False)
            last = pe.mm(bank_e(b0)[:, 2 * hh + 1, :], S_[:, hh, :], QD[:, hh, :], start=False, stop=True)
        tp = pe.mark(last)
        o2 = ps[:, b0, :].rearrange("p (h t) -> p h t", h=2)
        dst = o32[:, 2 * p:2 * p + 2, :]
        t_o = act.act(dst, o2, ACT.Copy, after=[tp])
        bank_free[b0] = [t_o]
        yield
        t_r = rms_pair(dst, 2, sqb[:, 0:2], 1.0 / P, Pm("eps_rms"), [t_o], (b1,))
        t = dve.stt(dst, dst, Pm("onorm"), sqb[:, 0:2], ALU.mult, ALU.mult, after=[t_r])
        while p not in z_ready:
            yield
        core_last.append(dve.tt(dst, dst, zg[p % 3], ALU.mult, after=[t, z_ready[p]]))
        yield

    cores = InFlight()
    step, finish = runner(decays())
    for p in range(NH // 2 + Z_LATE_A):
        if p >= Z_LATE_A:
            linear(2, hT, evac_z(p - Z_LATE_A), step, every=EA)
        if p < NH // 2:
            for part in range(3):
                linear(2, hT, evac_qkv(p, part), step, every=EA)
            if p == 0:
                finish()
                t_g, t_gc, t_dk, t_nb = decay_tokens
            cores.start(delta_core(p))
            step = cores.step
    hT_read = (pe.sem, pe.n)

    def output_halves():
        for p in range(NH // 2):
            while len(core_last) <= p:
                cores.step()
                yield
            oT.split(2 * p, 2, [core_last[p], hT_read], pool if p % 2 else dve)
            if len(core_last) > NH // 2 - 2:
                yield

    sq_free = []

    def evac_res(g, half, acc, done):
        c = 4 * g + 2 * half
        d = xT[:, c:c + 2, :]
        t = dve.tt(d, d, acc.rearrange("p (n t) -> p n t", n=2), ALU.add, after=[done])
        if not sq_free:
            sq_free.extend(fence())
        sums.add(c, [t] + sq_free)
        sums.flush(keep=1)
        return [t]

    sums = SumSquares(xT, at(145, NCH, T))
    step, finish = runner(output_halves())
    out_products(oT, False, evac_res, step=step, every=EO)
    t_x = (dve.sem, dve.n)

    hT = Halves(64, 80, NCH)
    rms_halves(xT, [t_x], sums, "norm2b", hT, fence())
    stage_free = fence()
    oT = Halves(64, 112, NCH)
    o32 = oT.f32
    hankel = at(128, NH, T)
    zg = [at(144 + 2 * i, 2, T) for i in range(3)]
    v_tok = [at(150 + 2 * i, 2, 2 * P) for i in range(3)]
    qk = [at(156 + 4 * i, 4, T) for i in range(3)]
    core_mem = [168, 180]
    gain = at(194, 2)
    act.wait(*stage_free)
    rsrc = bass.AP(tensor=rel_rev.tensor, offset=1, ap=[[1, P], [513, NH], [1, T]])
    t_rel = small.start(nc.scalar, hankel, rsrc)
    t_gain = dve.ts(gain[:, 0:1], Pm("qnorm"), float(P) ** -0.5, ALU.mult, after=stage_free)
    t_gain = dve.copy(gain[:, 1:2], Pm("knorm"))

    def value_products(src, evacuate, step, every):
        banks = [next_bank(), next_bank()]
        for half in range(2):
            w = take_block()
            for t in range(2):
                for kl in range(8):
                    if kl % 2 == 0:
                        split_ahead(split_goal(8 * t + kl))
                    k = 8 * half + kl
                    last = passes(w, (src.hi, src.lo), ps[:, banks[t], 0:256], lambda a: a[:, kl, :],
                                  lambda x_: x_[:, k, t * P:(t + 1) * P], k == 0, k == NCH - 1,
                                  weights_move=True)
                    if kl == 7:
                        done = pe.mark(last)
                    if k % every == every - 1 and step is not None:
                        step()
                if half == 1:
                    bank_free[banks[t]] = evacuate(t, ps[:, banks[t], 0:256], done)
            release_block(done)

    z_ready.clear()
    core_last.clear()
    v_ready = {}

    def evac_v(p):
        def evac(t, acc, done):
            v_ready[p] = act.act(v_tok[p % 3][:, t, :], acc, ACT.Copy,
                                 after=[done] + (core_last[p - 3:p - 2] or stage_free))
            return [v_ready[p]]
        return evac

    qk_ready = {}

    def evac_qk(p, part):
        def evac(i, acc, done):
            t = act.act(qk[p % 3][:, 2 * part:2 * part + 2, :], acc, ACT.Copy,
                        after=[done] + (core_last[p - 3:p - 2] or stage_free))
            qk_ready[p] = [t]
            return [t]
        return evac

    def attention_core(p):
        src = qk[p % 3]
        prev = core_last[p - 2:p - 1] if p >= 2 else stage_free
        b0, b1 = (3, 4) if p % 2 == 0 else (5, 6)
        at0 = core_mem[p % 2]
        sqb, prob, probT = at(at0, 4, T), at(at0 + 4, 2, 384), at(at0 + 7, 2, 3, P)
        stat = at(at0 + 10, 2, 4)
        t_r = rms_pair(src, 4, sqb, 1.0 / P, Pm("eps_rms"), qk_ready[p] + prev, (b0, b1))
        yield
        for a in range(2):
            t_n = dve.stt(src[:, 2 * a:2 * a + 2], src[:, 2 * a:2 * a + 2], gain[:, a:a + 1],
                          sqb[:, 2 * a:2 * a + 2], ALU.mult, ALU.mult, after=[t_r, t_gain])
        yield
        pe.wait(t_n, t_rel)
        for hh in range(2):
            h = 2 * p + hh
            use_bank((b0, b1)[hh])
            s = ps[:, (b0, b1)[hh], 0:384]
            qh, kh = src[:, hh, :], src[:, 2 + hh, :]
            pe.mm(s[:, 0:P], qh[:, 0:P], kh[:, 0:P], start=True, stop=False)
            pe.mm(s[:, 0:P], C("flip"), hankel[:, h, P:2 * P], start=False, stop=True)
            pe.mm(s[:, P:384], qh[:, P:T], kh, start=True, stop=False)
            tp = pe.mark(pe.mm(s[:, P:384], C("flip"), hankel[:, h, :], start=False, stop=True))
            t = dve.tt(prob[:, hh, :], s, C("band", 0, 384), ALU.add, after=[tp] + prev)
            bank_free[(b0, b1)[hh]] = [t]
            dve.wait(t)
            for i, cols in enumerate((slice(0, P), slice(P, 384))):
                t = dve.mark(nc.vector.tensor_reduce(stat[:, 0, 2 * hh + i:2 * hh + i + 1], prob[:, hh, cols],
                                                     AX_X, ALU.max, negate=True))
            for i, cols in enumerate((slice(0, P), slice(P, 384))):
                te = act.act(prob[:, hh, cols], prob[:, hh, cols], ACT.Exp, after=[t],
                             bias=stat[:, 0, 2 * hh + i:2 * hh + i + 1],
                             accum_out=stat[:, 1, 2 * hh + i:2 * hh + i + 1])
            yield
        t = dve.recip(stat[:, 1], stat[:, 1], after=[te])
        for hh in range(2):
            for i, cols in enumerate((slice(0, P), slice(P, 384))):
                t1 = dve.ts(prob[:, hh, cols], prob[:, hh, cols], stat[:, 1, 2 * hh + i:2 * hh + i + 1],
                            ALU.mult, after=[t])
        yield
        pe.wait(t1)
        for hh in range(2):
            use_bank((b0, b1)[hh])
            for j in range(3):
                last = pe.transpose(ps[:, (b0, b1)[hh], j * P:(j + 1) * P], prob[:, hh, j * P:(j + 1) * P],
                                    ident)
            tp = pe.mark(last)
            t2 = act.act(probT[:, hh], ps[:, (b0, b1)[hh], 0:384].rearrange("p (j n) -> p j n", j=3), ACT.Copy,
                         after=[tp] + prev)
            bank_free[(b0, b1)[hh]] = [t2]
            yield
        use_bank(7)
        pe.wait(t2, v_ready[p])
        for hh in range(2):
            vh = slice(hh * P, (hh + 1) * P)
            o = ps[:, 7, 256 * hh:256 * hh + 256]
            pe.mm(o[:, 0:P], v_tok[p % 3][:, 0, vh], probT[:, hh, 0, :])
            pe.mm(o[:, P:T], v_tok[p % 3][:, 0, vh], probT[:, hh, 1, :], start=True, stop=False)
            last = pe.mm(o[:, P:T], v_tok[p % 3][:, 1, vh], probT[:, hh, 2, :], start=False, stop=True)
        tp = pe.mark(last)
        while p not in z_ready:
            yield
        t = dve.tt(o32[:, 2 * p:2 * p + 2, :], zg[p % 3],
                              ps[:, 7, :].rearrange("p (h t) -> p h t", h=2), ALU.mult,
                              after=[tp, z_ready[p]] + stage_free)
        core_last.append(t)
        bank_free[7] = [t]
        yield

    cores = InFlight()
    step = None
    for p in range(NH // 2 + Z_LATE_B):
        if p >= Z_LATE_B:
            linear(2, hT, evac_z(p - Z_LATE_B), step, every=EB)
        if p < NH // 2:
            for part in range(2):
                linear(2, hT, evac_qk(p, part), step, every=EB)
            value_products(hT, evac_v(p), step, every=EB)
            cores.start(attention_core(p))
            step = cores.step
    hT_read = (pe.sem, pe.n)
    step, finish = runner(output_halves())

    y = [at(144 + 2 * i, 512) for i in range(4)]
    y_sem = [Loads(sem(f"y_stored{i}")) for i in range(4)]
    y_free = [[] for _ in range(4)]
    dst = out.rearrange("b (t p) d -> p (b t) d", p=P)

    def start_residual(g, t, acc):
        for i in range(4):
            pe.mm(acc[:, i * P:(i + 1) * P], xT[:, 4 * g + i, t * P:(t + 1) * P], ident, start=(i == 0), stop=False)

    def evac_y(g, t, acc, done):
        i = (2 * g + t) % 4
        ty = act.act(y[i], acc, ACT.Copy, after=[done] + (y_free[i] or fence()))
        sp.wait(ty)
        y_free[i] = [y_sem[i].start(nc.sync, dst[:, t, 512 * g:512 * (g + 1)], y[i])]
        return [ty]

    pe.wait(t_x)
    out_products(oT, True, evac_y, before=start_residual, step=step, every=EO)
    for loads in y_sem:
        nc.sync.wait_ge(loads.sem, loads.n)
    ctx.close()


def _columns(v):
    return np.ascontiguousarray(v.reshape(-1, P).T)


def _states(a):
    return a.reshape(32, P).T


def _constants():
    c = np.zeros((P, NCONST), np.float32)
    i = np.arange(P)
    row, col = i[:, None], i[None, :]
    c[:, 0:P] = row == col
    c[:, P:2 * P] = 1.0
    c[:, 2 * P:3 * P] = row <= col
    c[:, 3 * P:4 * P] = row + col == P - 1
    for l in range(7):
        b = 1 << l
        c[:, (4 + l) * P:(5 + l) * P] = (row // (2 * b) == col // (2 * b)) & (row % (2 * b) < b) & (col % (2 * b) >= b)
    q = i[:, None] // CHUNK
    c[:, 11 * P:12 * P] = np.where(col // CHUNK <= q, 0.0, NEG)
    k = np.arange(2 * P)[None, :] // CHUNK
    c[:, 12 * P:14 * P] = np.where(k <= q + 2, 0.0, NEG)
    c[:, 14 * P:14 * P + 16] = np.arange(16)
    return c


def _layout(inp):
    f = {k: np.asarray(v) for k, v in inp.items()}
    L = lambda name: f[name][0]
    par = np.zeros((P, NPARAM), np.float32)

    def put(name, v):
        a, n = PCOL[name]
        par[:, a:a + n] = v

    for name, src in (("norm_mix", "norm_mix"), ("b_gate", "b_gate"), ("dw_b", "conv_b_dw"), ("ln_g", "conv_ln_g"),
                      ("ln_b", "conv_ln_b"), ("ssm_d", "ssm_d"), ("norm_ffn", "norm_ffn"),
                      ("norm2a", "norm_w_2"), ("onorm", "a_out_norm_w_2"), ("qnorm", "b_q_norm_w_2"),
                      ("knorm", "b_k_norm_w_2")):
        put(name, _columns(L(src)))
    put("norm_final", _columns(f["norm_final"]))
    put("norm2b", _columns(f["norm_w_2"][1]))
    put("dw_w", _columns(L("conv_w_dw").reshape(-1)))
    put("qkv_w", _columns(L("a_conv_w_2").reshape(-1)))
    put("a_re", _states(L("ssm_a_re")))
    put("a_im", _states(L("ssm_a_im")))
    put("log_dt", _states(np.repeat(L("ssm_log_dt")[:, None], 64, 1)))
    put("a_log", np.broadcast_to(L("a_a_log_2"), (P, 16)))
    put("dt_bias", np.broadcast_to(L("a_dt_bias_2"), (P, 16)))
    put("eps_rms", RMS_EPS)
    put("eps_ln", LN_EPS)
    bT = np.zeros((8, 4, 2, 16, 2, 2, 64), np.float32)
    cT = np.zeros((2, 64, 2, 32, 2, 16), np.float32)
    for plane, (b, c) in enumerate(((L("ssm_b_re"), L("ssm_c_re")), (L("ssm_b_im"), L("ssm_c_im")))):
        b5 = b.reshape(8, 4, 2, 64, 16)
        c4 = c.reshape(32, 2, 16, 64)
        for g in range(2):
            bT[:, :, g, :, plane, g, :] = b5[:, :, g].transpose(0, 1, 3, 2)
            cT[g, :, plane, :, g, :] = c4[:, g].transpose(2, 0, 1)
    keysT = L("peer_sub_keys").reshape(16, 128, 128).transpose(2, 0, 1)
    bc = np.stack([bT.reshape(8, P, 2, P), cT.reshape(P, 2, 8, 4, 32).transpose(2, 0, 1, 3, 4).reshape(8, P, 2, P)],
                  axis=2)
    matrices = {"w_in": L("w_in"), "conv_out": L("conv_w_out"), "w_val": L("ssm_w_val"), "w_gate": L("ssm_w_gate"),
                "w_out": L("w_out"), "w_q": L("peer_w_q"), "a_in": L("a_w_in_2"), "a_out": L("a_w_out_2"),
                "b_in": L("b_w_in_2"), "b_out": L("b_w_out_2")}
    weights = np.stack([matrices[m][r:r + 2048 * P // n, c:c + n].reshape(-1, P, n).transpose(1, 0, 2)
                        .reshape(P, 2048) for m, r, c, n in PLAN])
    a_small = L("a_w_in_2")[:, 8192:].reshape(16, P, 32).transpose(1, 0, 2)
    return {
        "x": f["x"], "consts": _constants(), "params": par, "weights": weights, "bcT": bc, "keysT": keysT,
        "u_tab": L("peer_u"), "v_tab": L("peer_v"), "a_small": a_small, "rel_rev": L("b_rel_bias_2")[:, ::-1],
    }


def kernel(**inputs):
    import concourse.bacc as bacc
    from concourse.bass_utils import run_bass_kernel_spmd

    nc = bacc.Bacc("TRN2", target_bir_lowering=False, num_devices=1)
    arrays = {k: np.ascontiguousarray(v) for k, v in _layout(inputs).items()}
    args = {k: nc.dram_tensor(k, v.shape, mybir.dt.from_np(v.dtype), kind="ExternalInput").ap()
            for k, v in arrays.items()}
    out = nc.dram_tensor("out", (1, 256, 2048), F32, kind="ExternalOutput").ap()
    build(nc, out=out, **args)
    got = run_bass_kernel_spmd(nc, [arrays], core_ids=[0])
    return got.results[0]["out"]
```
